# Optimizing a Trainium2 kernel written in Bass

```python
import jax, jax.numpy as jnp
from jax import lax
import numpy as np
import math

D_MODEL = 1024
BATCH = 1
SEQ = 256
DEPTH = 2

MEM_LEN = 256
HEAD_DIM = 64
N_SB_HEADS = 8
N_FOX_HEADS = 8
N_MEM_HEADS = 4
MEM_HEAD_DIM = 128
SB_W = N_SB_HEADS * HEAD_DIM
FOX_W = N_FOX_HEADS * HEAD_DIM
MEM_W = N_MEM_HEADS * MEM_HEAD_DIM
N_BRANCH = 3
IN_W = 3 * SB_W + 3 * FOX_W + N_FOX_HEADS + MEM_W
D_FF = ((8 * D_MODEL // 3 + 127) // 128) * 128
Q_BLOCK = 128
RMS_EPS = 1e-6


def _rmsnorm(t, g):
    t32 = t.astype(jnp.float32)
    t32 = t32 * lax.rsqrt(jnp.mean(t32 * t32, axis=-1, keepdims=True) + RMS_EPS)
    return t32.astype(t.dtype) * g

def _swiglu(t, w_gate, w_up, w_down):
    return (jax.nn.silu(t @ w_gate) * (t @ w_up)) @ w_down

def _split_heads(t, n_heads):
    b, s, _ = t.shape
    return t.reshape(b, s, n_heads, -1).transpose(0, 2, 1, 3)

def _merge_heads(t):
    b, h, s, d = t.shape
    return t.transpose(0, 2, 1, 3).reshape(b, s, h * d)

def _query_blocks(t):
    b, h, s = t.shape[:3]
    t = t.reshape((b, h, s // Q_BLOCK, Q_BLOCK) + t.shape[3:])
    return jnp.moveaxis(t, 2, 0)

def _unblock(o):
    nb, b, h, blk, d = o.shape
    return jnp.moveaxis(o, 0, 2).reshape(b, h, nb * blk, d)

def _stick_breaking_attention(q, k, v):
    b, h, s_len, d = q.shape
    scale = d ** -0.5
    key_pos = jnp.arange(s_len)

    def block(args):
        qb, i = args
        z = jnp.einsum('bhqd,bhkd->bhqk', qb, k).astype(jnp.float32) * scale
        q_pos = i * Q_BLOCK + jnp.arange(Q_BLOCK)
        mask = key_pos[None, :] < q_pos[:, None]
        log_beta = jax.nn.log_sigmoid(z)
        log_not = jnp.where(mask, log_beta - z, 0.0)
        log_between = lax.cumsum(log_not, axis=3, reverse=True) - log_not
        w = jnp.where(mask, jnp.exp(log_beta + log_between), 0.0)
        return jnp.einsum('bhqk,bhkd->bhqd', w.astype(v.dtype), v)

    out = lax.map(block, (_query_blocks(q), jnp.arange(s_len // Q_BLOCK)))
    return _unblock(out)

def _forgetting_attention(q, k, v, log_f):
    b, h, s_len, d = q.shape
    scale = d ** -0.5
    key_pos = jnp.arange(s_len)
    c = lax.cumsum(log_f.astype(jnp.float32), axis=2)
    neg = jnp.finfo(jnp.float32).min

    def block(args):
        qb, cb, i = args
        z = jnp.einsum('bhqd,bhkd->bhqk', qb, k).astype(jnp.float32) * scale
        z = z + cb[..., :, None] - c[..., None, :]
        q_pos = i * Q_BLOCK + jnp.arange(Q_BLOCK)
        mask = key_pos[None, :] <= q_pos[:, None]
        p = jax.nn.softmax(jnp.where(mask, z, neg), axis=-1)
        return jnp.einsum('bhqk,bhkd->bhqd', p.astype(v.dtype), v)

    out = lax.map(block, (_query_blocks(q), _query_blocks(c), jnp.arange(s_len // Q_BLOCK)))
    return _unblock(out)

def _memory_attention(q, k, v):
    z = jnp.einsum('bhqd,bhkd->bhqk', q, k).astype(jnp.float32) * (q.shape[-1] ** -0.5)
    p = jax.nn.softmax(z, axis=-1)
    return jnp.einsum('bhqk,bhkd->bhqd', p.astype(v.dtype), v)

def first_inputs(seed: int = 0) -> dict:
    key = jax.random.key(seed)
    ks = jax.random.split(key, 32)
    L = DEPTH

    def w(k, shape, fan_in):
        return jax.random.normal(k, shape, jnp.float32) * (fan_in ** -0.5)

    def gain(k, shape):
        return 1.0 + 0.05 * jax.random.normal(k, shape, jnp.float32)

    return {
        'x': jax.random.normal(ks[0], (BATCH, SEQ, D_MODEL), jnp.float32),
        'mem': jax.random.normal(ks[1], (BATCH, MEM_LEN, D_MODEL), jnp.float32),
        'ffn1_pre_g': gain(ks[2], (L, D_MODEL)),
        'ffn1_post_g': gain(ks[3], (L, D_MODEL)),
        'ffn1_w_gate': w(ks[4], (L, D_MODEL, D_FF), D_MODEL),
        'ffn1_w_up': w(ks[5], (L, D_MODEL, D_FF), D_MODEL),
        'ffn1_w_down': w(ks[6], (L, D_FF, D_MODEL), D_FF),
        'mix_pre_g': gain(ks[7], (L, D_MODEL)),
        'mix_post_g': gain(ks[8], (L, D_MODEL)),
        'w_in': w(ks[9], (L, D_MODEL, IN_W), D_MODEL),
        'b_forget': 2.0 + 0.5 * jax.random.normal(ks[10], (L, N_FOX_HEADS), jnp.float32),
        'mem_norm_g': gain(ks[11], (D_MODEL,)),
        'w_mem_kv': w(ks[12], (L, D_MODEL, 2 * MEM_W), D_MODEL),
        'w_gate': w(ks[13], (L, D_MODEL, N_BRANCH * D_MODEL), D_MODEL),
        'b_gate': 0.02 * jax.random.normal(ks[14], (L, N_BRANCH * D_MODEL), jnp.float32),
        'w_br_sb': w(ks[15], (L, SB_W, D_MODEL), SB_W),
        'w_br_fox': w(ks[16], (L, FOX_W, D_MODEL), FOX_W),
        'w_br_mem': w(ks[17], (L, MEM_W, D_MODEL), MEM_W),
        'w_out': w(ks[18], (L, D_MODEL, D_MODEL), D_MODEL),
        'ffn2_pre_g': gain(ks[19], (L, D_MODEL)),
        'ffn2_post_g': gain(ks[20], (L, D_MODEL)),
        'ffn2_w_gate': w(ks[21], (L, D_MODEL, D_FF), D_MODEL),
        'ffn2_w_up': w(ks[22], (L, D_MODEL, D_FF), D_MODEL),
        'ffn2_w_down': w(ks[23], (L, D_FF, D_MODEL), D_FF),
    }

def first_block(x, mem, ffn1_pre_g, ffn1_post_g, ffn1_w_gate, ffn1_w_up, ffn1_w_down,
              mix_pre_g, mix_post_g, w_in, b_forget, mem_norm_g, w_mem_kv, w_gate, b_gate,
              w_br_sb, w_br_fox, w_br_mem, w_out,
              ffn2_pre_g, ffn2_post_g, ffn2_w_gate, ffn2_w_up, ffn2_w_down):
    mem_n = _rmsnorm(mem, mem_norm_g)
    split_at = np.cumsum([SB_W, SB_W, SB_W, FOX_W, FOX_W, FOX_W, N_FOX_HEADS])
    h = x
    for l in range(DEPTH):
        f = _swiglu(_rmsnorm(h, ffn1_pre_g[l]), ffn1_w_gate[l], ffn1_w_up[l], ffn1_w_down[l])
        h = h + 0.5 * _rmsnorm(f, ffn1_post_g[l])

        u = _rmsnorm(h, mix_pre_g[l])
        proj = u @ w_in[l]
        q_sb, k_sb, v_sb, q_fx, k_fx, v_fx, f_logit, q_mem = jnp.split(proj, split_at, axis=-1)

        o_sb = _stick_breaking_attention(_split_heads(q_sb, N_SB_HEADS), _split_heads(k_sb, N_SB_HEADS),
                                         _split_heads(v_sb, N_SB_HEADS))
        log_f = jax.nn.log_sigmoid((f_logit + b_forget[l]).astype(jnp.float32)).transpose(0, 2, 1)
        o_fx = _forgetting_attention(_split_heads(q_fx, N_FOX_HEADS), _split_heads(k_fx, N_FOX_HEADS),
                                     _split_heads(v_fx, N_FOX_HEADS), log_f)
        k_mem, v_mem = jnp.split(mem_n @ w_mem_kv[l], 2, axis=-1)
        o_mem = _memory_attention(_split_heads(q_mem, N_MEM_HEADS), _split_heads(k_mem, N_MEM_HEADS),
                                  _split_heads(v_mem, N_MEM_HEADS))

        g_sb, g_fx, g_mem = jnp.split(jax.nn.sigmoid(u @ w_gate[l] + b_gate[l]), N_BRANCH, axis=-1)
        merged = (g_sb * (_merge_heads(o_sb) @ w_br_sb[l])
                  + g_fx * (_merge_heads(o_fx) @ w_br_fox[l])
                  + g_mem * (_merge_heads(o_mem) @ w_br_mem[l]))
        h = h + _rmsnorm(merged @ w_out[l], mix_post_g[l])

        f = _swiglu(_rmsnorm(h, ffn2_pre_g[l]), ffn2_w_gate[l], ffn2_w_up[l], ffn2_w_down[l])
        h = h + 0.5 * _rmsnorm(f, ffn2_post_g[l])
    return h


N_MIXERS = 2
N_A_LAYERS = (DEPTH + 1) // 2
N_B_LAYERS = DEPTH // 2
N_VRES = max(N_B_LAYERS - 1, 0)

D_FF_2 = 2816
CHUNK = 128
D_SGU = 2 * D_MODEL
SGU_GROUPS = 16
SGU_GROUP_DIM = D_SGU // SGU_GROUPS
RWKV_HEAD = 64
RWKV_HEADS = D_MODEL // RWKV_HEAD
DECAY_LORA = 64
AAA_LORA = 64
MV_LORA = 32
GATE_LORA = 160
GN_EPS = 64e-5
LN_EPS = 1e-5
DN_ALPHA = (2 * DEPTH) ** 0.25
DN_BETA = (8 * DEPTH) ** -0.25


def layer_norm(x, g, b, eps=LN_EPS):
    xf = x.astype(jnp.float32)
    mu = jnp.mean(xf, axis=-1, keepdims=True)
    var = jnp.mean(jnp.square(xf - mu), axis=-1, keepdims=True)
    return ((xf - mu) * lax.rsqrt(var + eps) * g + b).astype(x.dtype)

def swiglu(x, w_in, w_out):
    gate, up = jnp.split(x @ w_in, 2, axis=-1)
    return (jax.nn.silu(gate) * up) @ w_out

def sgu_mixer(x, w_in, b_in, ln_g, ln_b, w_sp, b_sp, w_out):
    bsz, seq, _ = x.shape
    z = jax.nn.gelu(x @ w_in + b_in, approximate=False)
    u, v = jnp.split(z, 2, axis=-1)
    v = layer_norm(v, ln_g, ln_b)
    n_chunks = seq // CHUNK
    v = v.reshape(bsz, n_chunks, CHUNK, SGU_GROUPS, SGU_GROUP_DIM)
    causal = jnp.tril(jnp.ones((CHUNK, CHUNK), dtype=bool))
    w = jnp.where(causal[None], w_sp, 0)
    mixed = jnp.einsum('gts,bcsgd->bctgd', w, v) + b_sp.T[None, None, :, :, None]
    mixed = mixed.reshape(bsz, seq, D_SGU)
    return (u * mixed) @ w_out

def rwkv7_scan(r, decay, k, v, a, b):
    def step(state, inp):
        r_t, w_t, k_t, v_t, a_t, b_t = inp
        sa = jnp.einsum('bhij,bhj->bhi', state, a_t)
        state = (state * w_t[:, :, None, :] + sa[..., None] * b_t[:, :, None, :]
                 + v_t[..., None] * k_t[:, :, None, :])
        y = jnp.einsum('bhij,bhj->bhi', state, r_t)
        return state, y
    s0 = jnp.zeros(r.shape[1:3] + (RWKV_HEAD, RWKV_HEAD), jnp.float32)
    _, y = lax.scan(step, s0, (r, decay, k, v, a, b))
    return y

def rwkv7_mixer(x, v_first, vres, mu, w_rkv, w0, w1, w2, a0, a1, a2,
                g1, g2, k_k, k_a, r_k, gn_g, gn_b, w_o):
    bsz, seq, d = x.shape
    H, N = RWKV_HEADS, RWKV_HEAD
    xx = jnp.pad(x, ((0, 0), (1, 0), (0, 0)))[:, :-1] - x
    x_rkv = x[None] + xx[None] * mu[:3, None, None, :]
    r, k, v = jnp.einsum('nbsd,nde->nbse', x_rkv, w_rkv)
    xw = x + xx * mu[3]
    xa = x + xx * mu[4]
    xg = x + xx * mu[5]
    w = -jax.nn.softplus(-(w0 + jnp.tanh(xw @ w1) @ w2)) - 0.5
    if vres is None:
        v_first = v
    else:
        v0, v1, v2 = vres
        xv = x + xx * mu[2]
        v = v + (v_first - v) * jax.nn.sigmoid(v0 + (xv @ v1) @ v2)
    a = jax.nn.sigmoid(a0 + (xa @ a1) @ a2)
    g = jax.nn.sigmoid(xg @ g1) @ g2
    kk = (k * k_k).reshape(bsz, seq, H, N).astype(jnp.float32)
    kk = kk / jnp.maximum(jnp.linalg.norm(kk, axis=-1, keepdims=True), 1e-12)
    k = k * (1 + (a - 1) * k_a)

    def heads(z):
        return z.reshape(bsz, seq, H, N).astype(jnp.float32)

    def tmaj(z):
        return jnp.moveaxis(z, 1, 0)

    r_h, k_h, v_h, a_h = heads(r), heads(k), heads(v), heads(a)
    decay = jnp.exp(-jnp.exp(heads(w)))
    y = rwkv7_scan(tmaj(r_h), tmaj(decay), tmaj(k_h), tmaj(v_h), tmaj(-kk), tmaj(kk * a_h))
    y = jnp.moveaxis(y, 0, 1)
    mean = jnp.mean(y, axis=-1, keepdims=True)
    var = jnp.mean(jnp.square(y - mean), axis=-1, keepdims=True)
    y = (y - mean) * lax.rsqrt(var + GN_EPS) * gn_g.reshape(H, N) + gn_b.reshape(H, N)
    bonus = jnp.sum(r_h * k_h * r_k, axis=-1, keepdims=True) * v_h
    out = ((y + bonus).reshape(bsz, seq, d).astype(x.dtype) * g) @ w_o
    return out, v_first

def second_inputs(seed: int = 0) -> dict:
    key = jax.random.key(seed)
    ks = iter(jax.random.split(key, 40))
    f32 = jnp.float32

    def nrm(shape, scale):
        return jax.random.normal(next(ks), shape, f32) * scale

    def unif(shape, lo, hi):
        return jax.random.uniform(next(ks), shape, f32, lo, hi)

    D = D_MODEL
    NA, NB, NV = N_A_LAYERS, N_B_LAYERS, N_VRES
    return {
        "x": nrm((BATCH, SEQ, D), 1.0),
        "ln_g": 1.0 + nrm((DEPTH, 3, D), 0.02),
        "ln_b": nrm((DEPTH, 3, D), 0.02),
        "ffn_w_in": nrm((DEPTH, 2, D, 2 * D_FF_2), D ** -0.5),
        "ffn_w_out": nrm((DEPTH, 2, D_FF_2, D), D_FF_2 ** -0.5 * DN_BETA),
        "sgu_w_in": nrm((NA, D, 2 * D_SGU), D ** -0.5),
        "sgu_b_in": nrm((NA, 2 * D_SGU), 0.02),
        "sgu_ln_g": 1.0 + nrm((NA, D_SGU), 0.02),
        "sgu_ln_b": nrm((NA, D_SGU), 0.02),
        "sgu_w_sp": nrm((NA, SGU_GROUPS, CHUNK, CHUNK), CHUNK ** -0.5),
        "sgu_b_sp": 1.0 + nrm((NA, SGU_GROUPS, CHUNK), 0.02),
        "sgu_w_out": nrm((NA, D_SGU, D), D_SGU ** -0.5 * DN_BETA),
        "rwkv_mu": unif((NB, 6, D), 0.0, 1.0),
        "rwkv_w_rkv": nrm((NB, 3, D, D), D ** -0.5),
        "rwkv_w0": unif((NB, D), -6.0, -1.0),
        "rwkv_w1": nrm((NB, D, DECAY_LORA), D ** -0.5),
        "rwkv_w2": nrm((NB, DECAY_LORA, D), 0.1 * DECAY_LORA ** -0.5),
        "rwkv_a0": nrm((NB, D), 0.1),
        "rwkv_a1": nrm((NB, D, AAA_LORA), D ** -0.5),
        "rwkv_a2": nrm((NB, AAA_LORA, D), 0.5 * AAA_LORA ** -0.5),
        "rwkv_v0": nrm((NV, D), 0.1),
        "rwkv_v1": nrm((NV, D, MV_LORA), D ** -0.5),
        "rwkv_v2": nrm((NV, MV_LORA, D), 0.5 * MV_LORA ** -0.5),
        "rwkv_g1": nrm((NB, D, GATE_LORA), D ** -0.5),
        "rwkv_g2": nrm((NB, GATE_LORA, D), GATE_LORA ** -0.5),
        "rwkv_k_k": 0.85 + nrm((NB, D), 0.02),
        "rwkv_k_a": 1.0 + nrm((NB, D), 0.02),
        "rwkv_r_k": nrm((NB, RWKV_HEADS, RWKV_HEAD), 0.1),
        "rwkv_gn_g": 1.0 + nrm((NB, D), 0.02),
        "rwkv_gn_b": nrm((NB, D), 0.02),
        "rwkv_w_o": nrm((NB, D, D), D ** -0.5 * DN_BETA),
    }

def second_block(x, ln_g, ln_b, ffn_w_in, ffn_w_out, sgu_w_in, sgu_b_in, sgu_ln_g, sgu_ln_b,
              sgu_w_sp, sgu_b_sp, sgu_w_out, rwkv_mu, rwkv_w_rkv, rwkv_w0, rwkv_w1, rwkv_w2,
              rwkv_a0, rwkv_a1, rwkv_a2, rwkv_v0, rwkv_v1, rwkv_v2, rwkv_g1, rwkv_g2,
              rwkv_k_k, rwkv_k_a, rwkv_r_k, rwkv_gn_g, rwkv_gn_b, rwkv_w_o):
    v_first = None
    for i in range(DEPTH):
        x = layer_norm(DN_ALPHA * x + 0.5 * swiglu(x, ffn_w_in[i, 0], ffn_w_out[i, 0]),
                       ln_g[i, 0], ln_b[i, 0])
        j = i // N_MIXERS
        if i % N_MIXERS == 0:
            mix = sgu_mixer(x, sgu_w_in[j], sgu_b_in[j], sgu_ln_g[j], sgu_ln_b[j],
                            sgu_w_sp[j], sgu_b_sp[j], sgu_w_out[j])
        else:
            vres = None if v_first is None else (rwkv_v0[j - 1], rwkv_v1[j - 1], rwkv_v2[j - 1])
            mix, v_first = rwkv7_mixer(x, v_first, vres, rwkv_mu[j], rwkv_w_rkv[j], rwkv_w0[j],
                                       rwkv_w1[j], rwkv_w2[j], rwkv_a0[j], rwkv_a1[j], rwkv_a2[j],
                                       rwkv_g1[j], rwkv_g2[j], rwkv_k_k[j], rwkv_k_a[j],
                                       rwkv_r_k[j], rwkv_gn_g[j], rwkv_gn_b[j], rwkv_w_o[j])
        x = layer_norm(DN_ALPHA * x + mix, ln_g[i, 1], ln_b[i, 1])
        x = layer_norm(DN_ALPHA * x + 0.5 * swiglu(x, ffn_w_in[i, 1], ffn_w_out[i, 1]),
                       ln_g[i, 2], ln_b[i, 2])
    return x


_first_inputs = second_inputs


def second_inputs(seed=0):
    import zlib

    import numpy as np

    out = dict(_first_inputs(seed))
    spreads = {}
    factors = {'sgu_b_in': 7.761,
     'sgu_ln_g': 29.046,
     'sgu_ln_b': 29.849,
     'sgu_b_sp': 8.0,
     'rwkv_w1': 8.0,
     'rwkv_w2': 8.0,
     'rwkv_a0': 7.104,
     'rwkv_k_k': 24.541,
     'rwkv_k_a': 8.0,
     'rwkv_gn_g': 27.253,
     'rwkv_gn_b': 29.537}
    for name, (base, spread) in spreads.items():
        noise = np.random.default_rng([zlib.crc32(name.encode()), seed]).standard_normal(out[name].shape)
        drawn = base * np.exp(spread * noise) if base else spread * noise
        out[name] = __import__('jax').numpy.asarray(drawn.astype(out[name].dtype))
    for name, factor in factors.items():
        out[name] = (out[name] * factor).astype(out[name].dtype)
    return out


_narrow_inputs = second_inputs


def second_inputs(seed=0):

    out = dict(_narrow_inputs(seed))
    wider = {'sgu_b_sp': 3.8, 'rwkv_k_k': 4.03, 'rwkv_gn_g': 3.25, 'rwkv_gn_b': 3.17}
    for name, times in wider.items():
        mean = out[name].mean()
        out[name] = (mean + times * (out[name] - mean)).astype(out[name].dtype)
    return out


DEPTH_3 = 1

NSA_HEADS = 4
NSA_W = NSA_HEADS * HEAD_DIM
NSA_CMP_LEN = 32
NSA_CMP_STRIDE = 16
NSA_CMP_HIDDEN = 256
NSA_SEL_BLOCK = 64
NSA_TOPN = 16
NSA_WINDOW = 512
MOBA_HEADS = 4
MOBA_W = MOBA_HEADS * HEAD_DIM
MOBA_BLOCK = 256
MOBA_TOPK = 3
CONV_CH = 256
CONV_WIDTH = 31
HGRN_HEADS = 4
HGRN_KDIM = 64
HGRN_VDIM = 64
HGRN_W = HGRN_HEADS * HGRN_VDIM
HGRN_CHUNK = 64
MIX_WIDTH = NSA_W + MOBA_W + CONV_CH + HGRN_W
IN_WIDTHS = (NSA_W, HEAD_DIM, HEAD_DIM, HEAD_DIM, HEAD_DIM, HEAD_DIM, HEAD_DIM, 3 * NSA_HEADS,
             MOBA_W, MOBA_W, MOBA_W, 2 * CONV_CH, HGRN_W, HGRN_W, HGRN_W, HGRN_W)
IN_COLS = NSA_W + 6 * HEAD_DIM + 3 * NSA_HEADS + 3 * MOBA_W + 2 * CONV_CH + 4 * HGRN_W
D_FF_3 = 4 * D_MODEL
REL_BUCKETS = 32
REL_MAX_EXACT = 16
REL_MAX_DIST = 128
N_ATTN_HEADS = NSA_HEADS + MOBA_HEADS
BIG = 1e9
DEEPNORM_ALPHA = (2 * DEPTH_3) ** 0.25
DEEPNORM_BETA = (8 * DEPTH_3) ** -0.25


def layer_norm_3(x, g, b):
    xf = x.astype(jnp.float32)
    mu = jnp.mean(xf, -1, keepdims=True)
    var = jnp.mean(jnp.square(xf - mu), -1, keepdims=True)
    return ((xf - mu) * lax.rsqrt(var + LN_EPS)).astype(x.dtype) * g + b

def masked_softmax(s, mask):
    s = jnp.where(mask, s.astype(jnp.float32), -jnp.inf)
    m = jnp.max(s, -1, keepdims=True)
    m = jnp.where(jnp.isfinite(m), m, 0.0)
    p = jnp.where(mask, jnp.exp(s - m), 0.0)
    return p / jnp.maximum(jnp.sum(p, -1, keepdims=True), 1e-30)

def rel_bucket(dist):
    n = jnp.maximum(dist, 0)
    nf = jnp.maximum(n, 1).astype(jnp.float32)
    large = REL_MAX_EXACT + (jnp.log(nf / REL_MAX_EXACT) / math.log(REL_MAX_DIST / REL_MAX_EXACT)
                             * (REL_BUCKETS - REL_MAX_EXACT)).astype(jnp.int32)
    return jnp.where(n < REL_MAX_EXACT, n, jnp.minimum(large, REL_BUCKETS - 1))

def nsa_compress(k, pe, w1, b1, w2):
    B, S, dh = k.shape
    n_cmp = (S - NSA_CMP_LEN) // NSA_CMP_STRIDE + 1
    idx = jnp.arange(n_cmp)[:, None] * NSA_CMP_STRIDE + jnp.arange(NSA_CMP_LEN)[None, :]
    blocks = (k[:, idx] + pe).reshape(B, n_cmp, NSA_CMP_LEN * dh)
    return jax.nn.gelu(blocks @ w1 + b1) @ w2

def nsa_attention(q, kc, vc, ks, vs, kw, vw, gates, tab):
    B, S, H, dh = q.shape
    n_cmp = kc.shape[1]
    n_sel = S // NSA_SEL_BLOCK
    topn = min(NSA_TOPN, n_sel)
    scale = dh ** -0.5
    cmp_start = jnp.arange(n_cmp) * NSA_CMP_STRIDE
    cmp_end = cmp_start + NSA_CMP_LEN - 1
    sel_start = jnp.arange(n_sel) * NSA_SEL_BLOCK
    overlap = jnp.clip(jnp.minimum(cmp_end[:, None] + 1, sel_start[None, :] + NSA_SEL_BLOCK)
                       - jnp.maximum(cmp_start[:, None], sel_start[None, :]), 0, None).astype(jnp.float32) / NSA_CMP_LEN
    kw_pad = jnp.pad(kw, ((0, 0), (NSA_WINDOW, 0), (0, 0)))
    vw_pad = jnp.pad(vw, ((0, 0), (NSA_WINDOW, 0), (0, 0)))
    bi = jnp.arange(B)[:, None, None]
    jsel = jnp.arange(n_sel)

    def block(c):
        s0 = c * Q_BLOCK
        qb = lax.dynamic_slice_in_dim(q, s0, Q_BLOCK, axis=1) * scale
        gb = lax.dynamic_slice_in_dim(gates, s0, Q_BLOCK, axis=1)
        t = s0 + jnp.arange(Q_BLOCK)
        dist_c = t[:, None] - cmp_end[None, :]
        s_c = jnp.einsum('bthd,bnd->bhtn', qb, kc) + tab[:, rel_bucket(dist_c)][None]
        p_c = masked_softmax(s_c, dist_c >= 0)
        o_c = jnp.einsum('bhtn,bnd->bthd', p_c.astype(vc.dtype), vc)
        imp = jnp.einsum('bhtn,nj->btj', p_c, overlap)
        blk_t = t // NSA_SEL_BLOCK
        forced = (jsel[None, :] == 0) | (jsel[None, :] == blk_t[:, None]) | (jsel[None, :] == blk_t[:, None] - 1)
        valid = jsel[None, :] <= blk_t[:, None]
        imp = jnp.where(forced, BIG, jnp.where(valid, imp, -BIG))
        _, sel = lax.top_k(imp, topn)
        pos = (sel[..., None] * NSA_SEL_BLOCK + jnp.arange(NSA_SEL_BLOCK)).reshape(B, Q_BLOCK, topn * NSA_SEL_BLOCK)
        k_sel = ks[bi, pos]
        v_sel = vs[bi, pos]
        dist_s = t[None, :, None] - pos
        s_s = jnp.einsum('bthd,btkd->bhtk', qb, k_sel) + jnp.moveaxis(tab[:, rel_bucket(dist_s)], 0, 1)
        p_s = masked_softmax(s_s, (dist_s >= 0)[:, None])
        o_s = jnp.einsum('bhtk,btkd->bthd', p_s.astype(v_sel.dtype), v_sel)
        kwb = lax.dynamic_slice_in_dim(kw_pad, s0, Q_BLOCK + NSA_WINDOW, axis=1)
        vwb = lax.dynamic_slice_in_dim(vw_pad, s0, Q_BLOCK + NSA_WINDOW, axis=1)
        kpos = s0 - NSA_WINDOW + jnp.arange(Q_BLOCK + NSA_WINDOW)
        dist_w = t[:, None] - kpos[None, :]
        mask_w = (dist_w >= 0) & (dist_w < NSA_WINDOW) & (kpos[None, :] >= 0)
        s_w = jnp.einsum('bthd,bkd->bhtk', qb, kwb) + tab[:, rel_bucket(dist_w)][None]
        p_w = masked_softmax(s_w, mask_w)
        o_w = jnp.einsum('bhtk,bkd->bthd', p_w.astype(vwb.dtype), vwb)
        return gb[..., 0:1] * o_c + gb[..., 1:2] * o_s + gb[..., 2:3] * o_w

    out = lax.map(block, jnp.arange(S // Q_BLOCK))
    return jnp.moveaxis(out, 0, 1).reshape(B, S, H * dh)

def moba_attention(q, k, v, tab):
    B, S, H, dh = q.shape
    s_pad = -(-S // MOBA_BLOCK) * MOBA_BLOCK
    nb = s_pad // MOBA_BLOCK
    ktop = min(MOBA_TOPK, nb)
    scale = dh ** -0.5
    padw = ((0, 0), (0, s_pad - S), (0, 0), (0, 0))
    kbh = jnp.pad(k, padw).reshape(B, nb, MOBA_BLOCK, H, dh).transpose(0, 3, 1, 2, 4)
    vbh = jnp.pad(v, padw).reshape(B, nb, MOBA_BLOCK, H, dh).transpose(0, 3, 1, 2, 4)
    k_mean = jnp.mean(kbh, axis=3)
    bi = jnp.arange(B)[:, None, None, None]
    hi = jnp.arange(H)[None, :, None, None]
    jblk = jnp.arange(nb)

    def block(c):
        s0 = c * Q_BLOCK
        qb = lax.dynamic_slice_in_dim(q, s0, Q_BLOCK, axis=1) * scale
        t = s0 + jnp.arange(Q_BLOCK)
        own = s0 // MOBA_BLOCK
        gate = jnp.einsum('bthd,bhnd->bhtn', qb, k_mean).astype(jnp.float32)
        gate = jnp.where((jblk < own)[None, None, None, :], gate, -BIG)
        gv, sel = lax.top_k(gate, ktop)
        sel_ok = gv > -0.5 * BIG
        k_sel = kbh[bi, hi, sel].reshape(B, H, Q_BLOCK, ktop * MOBA_BLOCK, dh)
        v_sel = vbh[bi, hi, sel].reshape(B, H, Q_BLOCK, ktop * MOBA_BLOCK, dh)
        pos_sel = (sel[..., None] * MOBA_BLOCK + jnp.arange(MOBA_BLOCK)).reshape(B, H, Q_BLOCK, ktop * MOBA_BLOCK)
        bias_sel = tab[hi, rel_bucket(t[None, None, :, None] - pos_sel)]
        s_sel = jnp.einsum('bthd,bhtkd->bhtk', qb, k_sel) + bias_sel
        mask_sel = jnp.repeat(sel_ok, MOBA_BLOCK, axis=-1)
        k_own = lax.dynamic_slice_in_dim(kbh, own, 1, axis=2)[:, :, 0]
        v_own = lax.dynamic_slice_in_dim(vbh, own, 1, axis=2)[:, :, 0]
        pos_own = own * MOBA_BLOCK + jnp.arange(MOBA_BLOCK)
        dist_own = t[:, None] - pos_own[None, :]
        s_own = jnp.einsum('bthd,bhkd->bhtk', qb, k_own) + tab[:, rel_bucket(dist_own)][None]
        mask_own = jnp.broadcast_to(dist_own >= 0, (B, H, Q_BLOCK, MOBA_BLOCK))
        p = masked_softmax(jnp.concatenate([s_sel, s_own], -1), jnp.concatenate([mask_sel, mask_own], -1))
        p_sel = p[..., :ktop * MOBA_BLOCK].astype(v.dtype)
        p_own = p[..., ktop * MOBA_BLOCK:].astype(v.dtype)
        return jnp.einsum('bhtk,bhtkd->bthd', p_sel, v_sel) + jnp.einsum('bhtk,bhkd->bthd', p_own, v_own)

    out = lax.map(block, jnp.arange(S // Q_BLOCK))
    return jnp.moveaxis(out, 0, 1).reshape(B, S, H * dh)

def conformer_conv(u, w_dw, b_dw, ln_g, ln_b, w_pw):
    a, g = jnp.split(u, 2, axis=-1)
    h = a * jax.nn.sigmoid(g)
    h = lax.conv_general_dilated(h, w_dw[:, None, :], window_strides=(1,),
                                 padding=[(CONV_WIDTH - 1, 0)],
                                 dimension_numbers=('NWC', 'WIO', 'NWC'),
                                 feature_group_count=CONV_CH) + b_dw
    h = jax.nn.silu(layer_norm_3(h, ln_g, ln_b))
    return h @ w_pw

def hgrn2_mixer(q, f_logit, i, g, lb, norm_g):
    B, S, _ = q.shape
    H, dk, dv, C = HGRN_HEADS, HGRN_KDIM, HGRN_VDIM, HGRN_CHUNK
    nc = S // C
    f = lb + (1.0 - lb) * jax.nn.sigmoid(f_logit.astype(jnp.float32))
    log_f = jnp.log(f)
    k = 1.0 - f

    def chunks(a, d):
        return a.astype(jnp.float32).reshape(B, nc, C, H, d).transpose(1, 0, 3, 2, 4)

    causal = jnp.tril(jnp.ones((C, C), dtype=bool))[:, :, None]

    def step(state, inp):
        qc, kc, vc, gc = inp
        cum = jnp.cumsum(gc, axis=2)
        diff = cum[:, :, :, None, :] - cum[:, :, None, :, :]
        decay = jnp.where(causal, jnp.exp(jnp.where(causal, diff, 0.0)), 0.0)
        attn = jnp.einsum('bhtk,bhsk,bhtsk->bhts', qc, kc, decay)
        o = jnp.einsum('bhtk,bhkv->bhtv', qc * jnp.exp(cum), state) + jnp.einsum('bhts,bhsv->bhtv', attn, vc)
        last = cum[:, :, -1:, :]
        state = jnp.exp(last[:, :, 0, :])[..., None] * state + jnp.einsum('bhsk,bhsv->bhkv', kc * jnp.exp(last - cum), vc)
        return state, o

    s_init = jnp.zeros((B, H, dk, dv), jnp.float32)
    _, o = lax.scan(step, s_init, (chunks(q, dk), chunks(k, dk), chunks(i, dv), chunks(log_f, dk)))
    o = o.transpose(1, 0, 3, 2, 4).reshape(B, S, H, dv)
    o = o * lax.rsqrt(jnp.mean(o * o, -1, keepdims=True) + RMS_EPS)
    return o.reshape(B, S, H * dv).astype(q.dtype) * norm_g * jax.nn.sigmoid(g)

def hybrid_layer(x, w_in, cmp_pe, cmp_w1, cmp_b1, cmp_w2, dw_w, dw_b, cln_g, cln_b, pw_w,
                 lb, hn_g, w_out, ln1_g, ln1_b, w_ff1, w_ff2, ln2_g, ln2_b, rel_tab):
    B, S, _ = x.shape
    split_points = [int(v) for v in np.cumsum(IN_WIDTHS)[:-1]]
    h = x @ w_in
    (q_n, kc, vc, ks, vs, kw, vw, g_n, q_m, k_m, v_m, conv_in,
     q_h, f_h, i_h, g_h) = jnp.split(h, split_points, axis=-1)
    kc = nsa_compress(kc, cmp_pe[0], cmp_w1[0], cmp_b1[0], cmp_w2[0])
    vc = nsa_compress(vc, cmp_pe[1], cmp_w1[1], cmp_b1[1], cmp_w2[1])
    gates = jax.nn.sigmoid(g_n.reshape(B, S, NSA_HEADS, 3))
    o_nsa = nsa_attention(q_n.reshape(B, S, NSA_HEADS, HEAD_DIM), kc, vc, ks, vs, kw, vw, gates,
                          rel_tab[:NSA_HEADS])
    o_moba = moba_attention(q_m.reshape(B, S, MOBA_HEADS, HEAD_DIM), k_m.reshape(B, S, MOBA_HEADS, HEAD_DIM),
                            v_m.reshape(B, S, MOBA_HEADS, HEAD_DIM), rel_tab[NSA_HEADS:])
    o_conv = conformer_conv(conv_in, dw_w, dw_b, cln_g, cln_b, pw_w)
    o_hgrn = hgrn2_mixer(q_h, f_h, i_h, g_h, lb, hn_g)
    mixed = jnp.concatenate([o_nsa, o_moba, o_conv, o_hgrn], axis=-1) @ w_out
    x = layer_norm_3(DEEPNORM_ALPHA * x + mixed, ln1_g, ln1_b)
    ff = jnp.square(jax.nn.relu(x @ w_ff1)) @ w_ff2
    return layer_norm_3(DEEPNORM_ALPHA * x + ff, ln2_g, ln2_b)

def third_inputs(seed: int = 0) -> dict:
    key = jax.random.key(seed)
    ks = jax.random.split(key, 24)

    def nrm(k, shape, scale):
        return jax.random.normal(k, shape, jnp.float32) * scale

    return {
        'x': nrm(ks[0], (BATCH, SEQ, D_MODEL), 1.0),
        'w_in': nrm(ks[1], (DEPTH_3, D_MODEL, IN_COLS), D_MODEL ** -0.5),
        'nsa_cmp_pe': nrm(ks[2], (DEPTH_3, 2, NSA_CMP_LEN, HEAD_DIM), 0.1),
        'nsa_cmp_w1': nrm(ks[3], (DEPTH_3, 2, NSA_CMP_LEN * HEAD_DIM, NSA_CMP_HIDDEN), (NSA_CMP_LEN * HEAD_DIM) ** -0.5),
        'nsa_cmp_b1': nrm(ks[4], (DEPTH_3, 2, NSA_CMP_HIDDEN), 0.02),
        'nsa_cmp_w2': nrm(ks[5], (DEPTH_3, 2, NSA_CMP_HIDDEN, HEAD_DIM), NSA_CMP_HIDDEN ** -0.5),
        'conv_dw_w': nrm(ks[6], (DEPTH_3, CONV_WIDTH, CONV_CH), CONV_WIDTH ** -0.5),
        'conv_dw_b': nrm(ks[7], (DEPTH_3, CONV_CH), 0.02),
        'conv_ln_g': 1.0 + nrm(ks[8], (DEPTH_3, CONV_CH), 0.02),
        'conv_ln_b': nrm(ks[9], (DEPTH_3, CONV_CH), 0.02),
        'conv_pw_w': nrm(ks[10], (DEPTH_3, CONV_CH, CONV_CH), CONV_CH ** -0.5),
        'hgrn_lb_logits': nrm(ks[11], (DEPTH_3, HGRN_HEADS * HGRN_KDIM), 0.5),
        'hgrn_norm_g': 1.0 + nrm(ks[12], (DEPTH_3, HGRN_W), 0.02),
        'w_out': nrm(ks[13], (DEPTH_3, MIX_WIDTH, D_MODEL), MIX_WIDTH ** -0.5 * DEEPNORM_BETA),
        'ln1_g': 1.0 + nrm(ks[14], (DEPTH_3, D_MODEL), 0.02),
        'ln1_b': nrm(ks[15], (DEPTH_3, D_MODEL), 0.02),
        'w_ff1': nrm(ks[16], (DEPTH_3, D_MODEL, D_FF_3), D_MODEL ** -0.5),
        'w_ff2': nrm(ks[17], (DEPTH_3, D_FF_3, D_MODEL), D_FF_3 ** -0.5 * DEEPNORM_BETA),
        'ln2_g': 1.0 + nrm(ks[18], (DEPTH_3, D_MODEL), 0.02),
        'ln2_b': nrm(ks[19], (DEPTH_3, D_MODEL), 0.02),
        'rel_bias': nrm(ks[20], (N_ATTN_HEADS, REL_BUCKETS), 0.5),
    }

def third_block(x, w_in, nsa_cmp_pe, nsa_cmp_w1, nsa_cmp_b1, nsa_cmp_w2, conv_dw_w, conv_dw_b,
              conv_ln_g, conv_ln_b, conv_pw_w, hgrn_lb_logits, hgrn_norm_g, w_out, ln1_g, ln1_b,
              w_ff1, w_ff2, ln2_g, ln2_b, rel_bias):
    lb_sm = jax.nn.softmax(hgrn_lb_logits.astype(jnp.float32), axis=0)
    lbs = (jnp.cumsum(lb_sm, axis=0) - lb_sm[0]).astype(x.dtype)
    for l in range(DEPTH_3):
        x = hybrid_layer(x, w_in[l], nsa_cmp_pe[l], nsa_cmp_w1[l], nsa_cmp_b1[l], nsa_cmp_w2[l],
                         conv_dw_w[l], conv_dw_b[l], conv_ln_g[l], conv_ln_b[l], conv_pw_w[l],
                         lbs[l], hgrn_norm_g[l], w_out[l], ln1_g[l], ln1_b[l], w_ff1[l], w_ff2[l],
                         ln2_g[l], ln2_b[l], rel_bias)
    return x


_first_inputs_3 = third_inputs


def third_inputs(seed=0):
    import zlib

    import numpy as np

    out = dict(_first_inputs_3(seed))
    spreads = {}
    factors = {'nsa_cmp_pe': 44.131,
     'nsa_cmp_b1': 200.0,
     'conv_dw_b': 8.0,
     'conv_ln_g': 120.871,
     'conv_ln_b': 108.114,
     'hgrn_norm_g': 155.275,
     'ln1_g': 2.756,
     'ln1_b': 2.761,
     'ln2_g': 24.959,
     'ln2_b': 24.232,
     'rel_bias': 15.267,
     'nsa_cmp_w1': 4.902,
     'nsa_cmp_w2': 2.754}
    for name, (base, spread) in spreads.items():
        noise = np.random.default_rng([zlib.crc32(name.encode()), seed]).standard_normal(out[name].shape)
        drawn = base * np.exp(spread * noise) if base else spread * noise
        out[name] = __import__('jax').numpy.asarray(drawn.astype(out[name].dtype))
    for name, factor in factors.items():
        out[name] = (out[name] * factor).astype(out[name].dtype)
    return out


_narrow_inputs_3 = third_inputs


def third_inputs(seed=0):

    out = dict(_narrow_inputs_3(seed))
    wider = {'conv_ln_g': 4.4, 'conv_ln_b': 4.41, 'hgrn_norm_g': 4.39, 'ln2_g': 3.3, 'ln2_b': 3.29}
    for name, times in wider.items():
        mean = out[name].mean()
        out[name] = (mean + times * (out[name] - mean)).astype(out[name].dtype)
    return out


def setup_inputs(seed=0):
    out = dict(first_inputs(seed))
    for name, value in second_inputs(seed + 1).items():
        if name != "x":
            out[name + "_2"] = value
    for name, value in third_inputs(seed + 2).items():
        if name != "x":
            out[name + "_3"] = value
    return out


def reference(
    x, mem, ffn1_pre_g, ffn1_post_g, ffn1_w_gate, ffn1_w_up, ffn1_w_down, mix_pre_g, mix_post_g,
    w_in, b_forget, mem_norm_g, w_mem_kv, w_gate, b_gate, w_br_sb, w_br_fox, w_br_mem, w_out,
    ffn2_pre_g, ffn2_post_g, ffn2_w_gate, ffn2_w_up, ffn2_w_down, ln_g_2, ln_b_2, ffn_w_in_2,
    ffn_w_out_2, sgu_w_in_2, sgu_b_in_2, sgu_ln_g_2, sgu_ln_b_2, sgu_w_sp_2, sgu_b_sp_2,
    sgu_w_out_2, rwkv_mu_2, rwkv_w_rkv_2, rwkv_w0_2, rwkv_w1_2, rwkv_w2_2, rwkv_a0_2, rwkv_a1_2,
    rwkv_a2_2, rwkv_v0_2, rwkv_v1_2, rwkv_v2_2, rwkv_g1_2, rwkv_g2_2, rwkv_k_k_2, rwkv_k_a_2,
    rwkv_r_k_2, rwkv_gn_g_2, rwkv_gn_b_2, rwkv_w_o_2, w_in_3, nsa_cmp_pe_3, nsa_cmp_w1_3,
    nsa_cmp_b1_3, nsa_cmp_w2_3, conv_dw_w_3, conv_dw_b_3, conv_ln_g_3, conv_ln_b_3, conv_pw_w_3,
    hgrn_lb_logits_3, hgrn_norm_g_3, w_out_3, ln1_g_3, ln1_b_3, w_ff1_3, w_ff2_3, ln2_g_3,
    ln2_b_3, rel_bias_3,
):
    x = first_block(
        x, mem, ffn1_pre_g, ffn1_post_g, ffn1_w_gate, ffn1_w_up, ffn1_w_down, mix_pre_g,
        mix_post_g, w_in, b_forget, mem_norm_g, w_mem_kv, w_gate, b_gate, w_br_sb, w_br_fox,
        w_br_mem, w_out, ffn2_pre_g, ffn2_post_g, ffn2_w_gate, ffn2_w_up, ffn2_w_down,
    )
    x = second_block(
        x, ln_g_2, ln_b_2, ffn_w_in_2, ffn_w_out_2, sgu_w_in_2, sgu_b_in_2, sgu_ln_g_2,
        sgu_ln_b_2, sgu_w_sp_2, sgu_b_sp_2, sgu_w_out_2, rwkv_mu_2, rwkv_w_rkv_2, rwkv_w0_2,
        rwkv_w1_2, rwkv_w2_2, rwkv_a0_2, rwkv_a1_2, rwkv_a2_2, rwkv_v0_2, rwkv_v1_2, rwkv_v2_2,
        rwkv_g1_2, rwkv_g2_2, rwkv_k_k_2, rwkv_k_a_2, rwkv_r_k_2, rwkv_gn_g_2, rwkv_gn_b_2,
        rwkv_w_o_2,
    )
    return third_block(
        x, w_in_3, nsa_cmp_pe_3, nsa_cmp_w1_3, nsa_cmp_b1_3, nsa_cmp_w2_3, conv_dw_w_3,
        conv_dw_b_3, conv_ln_g_3, conv_ln_b_3, conv_pw_w_3, hgrn_lb_logits_3, hgrn_norm_g_3,
        w_out_3, ln1_g_3, ln1_b_3, w_ff1_3, w_ff2_3, ln2_g_3, ln2_b_3, rel_bias_3,
    )


_drawn_inputs = setup_inputs


def setup_inputs(seed=0):
    import zlib

    import numpy as np

    out = dict(_drawn_inputs(seed))
    spreads = {}
    factors = {'ln1_g_3': 2.695, 'ln1_b_3': 6.522}
    for name, (base, spread) in spreads.items():
        noise = np.random.default_rng([zlib.crc32(name.encode()), seed]).standard_normal(out[name].shape)
        drawn = base * np.exp(spread * noise) if base else spread * noise
        out[name] = __import__('jax').numpy.asarray(drawn.astype(out[name].dtype))
    for name, factor in factors.items():
        out[name] = (out[name] * factor).astype(out[name].dtype)
    return out
```

```python
from contextlib import ExitStack, contextmanager

import numpy as np
import concourse.bass as bass
from concourse import mybir

F32 = mybir.dt.float32
BF16 = mybir.dt.bfloat16
ALU = mybir.AluOpType
ACT = mybir.ActivationFunctionType
AX = mybir.AxisListType.X

P = 128
D = 1024
KT = D // P
S = 256
NB = S // P
DFF = 2816
RING = 6
UNIT = 2048
CREDIT = 512


class Loop:

    def __init__(self, n, parent):
        self.n, self.parent, self.entry, self.stride, self.cur = n, parent, {}, {}, None


class Count:

    def __init__(self, sem, start=0):
        self.sem, self.off = sem, start


class Tok:

    def __init__(self, count, off, loop, back=0):
        self.count, self.off, self.loop, self.back = count, off, loop, back

    def value(self, inside):
        v, s, back = self.off, self.loop, self.back
        while s is not None:
            if s in inside:
                v = v + s.entry[self.count] + (s.cur - back) * s.stride[self.count]
            else:
                v = v + s.entry[self.count] + (s.n - 1) * s.stride[self.count]
            back, s = 0, s.parent
        return v


class Prog:

    ENGINES = ("tensor", "scalar", "vector", "gpsimd", "sync")

    def __init__(self, nc, ctx):
        self.nc, self.ctx = nc, ctx
        self.queues = {e: [] for e in self.ENGINES}
        self.at = {e: self.queues[e] for e in self.ENGINES}
        self.counts, self.hands, self.loop, self.pending = [], [], None, 0
        self.s_free = ctx.enter_context(nc.semaphore("s_weight_units_read"))
        self.main = {e: self.count(f"s_{e}", CREDIT) for e in self.ENGINES[:4]}

    def count(self, name, start=0):
        c = Count(self.ctx.enter_context(self.nc.semaphore(name)), start)
        self.counts.append(c)
        return c

    def op(self, engine, fn, *waits, count=None, inc=1):
        c = count or self.main[engine]
        c.off += inc
        self.at[engine].append(("op", fn, flat(waits), c, inc))
        return Tok(c, c.off, self.loop)

    def pe(self, fn, *w):
        return self.op("tensor", fn, *w)

    def mms(self, calls, *w, release=False):
        if len(calls) == 1:
            freed, self.pending = 0, self.pending + int(release)
        else:
            freed, self.pending = self.pending, int(release)

        def fn(e):
            n = freed
            for call in calls:
                last = e.matmul(*call[:3], start=call[3], stop=call[4], skip_group_check=True)
                if n:
                    last.then_inc(self.s_free, n)
                    n = 0
            return last

        return self.op("tensor", fn, *w)

    def act(self, fn, *w):
        return self.op("scalar", fn, *w)

    def dve(self, fn, *w):
        return self.op("vector", fn, *w)

    def pool(self, fn, *w):
        return self.op("gpsimd", fn, *w)

    def load(self, out, in_, *w, engine="sync", name="ld"):
        c = self.count(f"d_{name}_{len(self.counts)}")
        return self.op(engine, lambda e: e.dma_start(out, in_), *w, count=c, inc=16)

    def now(self):
        return [Tok(c, c.off, self.loop) for c in self.main.values()]

    def barrier(self):
        w = self.now()
        for e in self.ENGINES[:4]:
            self.at[e].append(("wait", w))

    @contextmanager
    def repeat(self, n):
        loop = Loop(n, self.loop)
        saved = dict(self.at)
        for e in self.ENGINES:
            body = []
            self.at[e].append(("loop", loop, body))
            self.at[e] = body
        for c in self.counts:
            loop.entry[c], c.off = c.off, 0
        self.loop, pending = loop, self.pending
        yield loop
        assert pending == self.pending
        for h in self.hands:
            h.close(loop)
        for c in self.counts:
            if c not in loop.entry:
                loop.entry[c] = 0
            loop.stride[c] = c.off
            c.off = loop.entry[c] + n * c.off
        self.loop = loop.parent
        self.at = saved

    def emit(self):
        block = self.ctx.enter_context(self.nc.Block())
        for name in self.ENGINES:
            enter = {"tensor": block.tensor, "scalar": block.scalar, "vector": block.vector,
                        "gpsimd": block.gpsimd, "sync": block.sync}[name]

            def body(eng, name=name):
                if name in self.main:
                    eng.sem_inc(self.main[name].sem, CREDIT)
                self.walk(eng, self.queues[name], [])

            enter(body)

    def walk(self, eng, nodes, inside):
        seen = {}

        def wait(t):
            if t.count.off == 0 and t.off == 0:
                return
            key = (t.count, t.loop, t.back)
            if seen.get(key, -1) >= t.off:
                return
            seen[key] = t.off
            eng.wait_ge(t.count.sem, t.value(inside))

        for node in nodes:
            if node[0] == "wait":
                for t in latest(node[1]):
                    wait(t)
            elif node[0] == "raw":
                node[1](eng)
            elif node[0] == "op":
                _, fn, waits, c, inc = node
                for t in latest(waits):
                    wait(t)
                fn(eng).then_inc(c.sem, inc)
            else:
                _, loop, body = node
                if has_ops(body):
                    with eng.Fori(0, loop.n) as i:
                        loop.cur = i
                        self.walk(eng, body, inside + [loop])
                    loop.cur = None


def has_ops(nodes):
    return any(n[0] in ("op", "wait") or has_ops(n[2]) for n in nodes)


def flat(ws):
    out = []
    for w in ws:
        if isinstance(w, (list, tuple)):
            out += flat(w)
        elif isinstance(w, Hand):
            out += w.take()
        elif w is not None:
            out.append(w)
    return out


def latest(waits):
    best = {}
    for t in waits:
        if isinstance(t, Later):
            for u in t.toks:
                k = (u.count, u.loop, u.back)
                if k not in best or best[k].off < u.off:
                    best[k] = u
            continue
        k = (t.count, t.loop, t.back)
        if k not in best or best[k].off < t.off:
            best[k] = t
    return list(best.values())


class Later:

    def __init__(self):
        self.toks = []


class Hand:

    def __init__(self, prog):
        self.prog, self.toks, self.open = prog, [], []
        prog.hands.append(self)

    def take(self):
        loop, out = self.prog.loop, list(self.toks)
        if loop is not None and not any(t.loop is loop for t in self.toks):
            later = Later()
            self.open.append((loop, later))
            out.append(later)
        return out

    def give(self, *toks):
        self.toks = flat(toks)
        return self.toks

    def close(self, loop):
        for l, later in self.open:
            if l is loop:
                later.toks = [Tok(t.count, t.off, t.loop, 1) for t in self.toks if t.loop is loop]
        self.open = [(l, x) for l, x in self.open if l is not loop]


def shape_constants():
    r = np.arange(P)
    row, colm = r[:, None], r[None, :]
    one = np.ones((P, P))
    chunk = row // 16 == colm // 16
    mats = {
        "identity": row == colm,
        "mean": one / D,
        "mean_half": one / (2 * D),
        "after": row > colm,
        "ones": one,
        "mean_256": one / 256,
        "upto": row <= colm,
        "before": row < colm,
        "not_before": np.where(row < colm, -1e30, 0),
        "head_sum": row // 64 == colm // 64,
        "head_mean": (row // 64 == colm // 64) / 64,
        "chunk_of": row // 16 == colm,
        "chunk_upto": chunk & (row <= colm),
        "chunk_before": chunk & (row < colm),
        "chunk_after": chunk & (row > colm),
        "chunk_all": chunk,
        "identity_pair": row % 64 == colm,
        "flip": row + colm == P - 1,
    }
    return mats


MATS = shape_constants()
CONS = list(MATS)

EPS = [1e-6, 1e-5, 64e-5, 1.0]

def vectors():
    out = []
    for l in range(2):
        out += [("ffn1_pre_g", l), ("ffn1_post_g", l), ("mix_pre_g", l), ("mix_post_g", l), ("b_gate", l),
                ("ffn2_pre_g", l), ("ffn2_post_g", l)]
    out += [("mem_norm_g", ())]
    out += [(f"ln_{x}_2", (i, j)) for i in range(2) for j in range(3) for x in "gb"]
    out += [(n, 0) for n in ("sgu_b_in_2", "sgu_ln_g_2", "sgu_ln_b_2")]
    out += [("rwkv_mu_2", (0, j)) for j in range(6)]
    out += [(f"rwkv_{n}_2", 0) for n in ("w0", "a0", "k_k", "k_a", "r_k", "gn_g", "gn_b")]
    out += [("conv_dw_w_3", (0, j)) for j in range(31)]
    out += [(n, 0) for n in ("conv_dw_b_3", "conv_ln_g_3", "conv_ln_b_3", "hgrn_norm_g_3", "ln1_g_3", "ln1_b_3",
                             "ln2_g_3", "ln2_b_3")]
    out += [("nsa_cmp_b1_3", (0, j)) for j in range(2)]
    out += [("nsa_cmp_pe_3", (0, j)) for j in range(2)]
    return out


SIZES = {"b_gate": 3072, "sgu_b_in_2": 4096, "sgu_ln_g_2": 2048, "sgu_ln_b_2": 2048, "conv_dw_w_3": 256,
         "conv_dw_b_3": 256, "conv_ln_g_3": 256, "conv_ln_b_3": 256, "hgrn_norm_g_3": 256, "nsa_cmp_b1_3": 256,
         "nsa_cmp_pe_3": 2048}
VECTORS = vectors()
COLS, N_COLS = {}, 0
for _name, _index in VECTORS:
    COLS[_name, _index] = N_COLS
    N_COLS += SIZES.get(_name, D) // P
COLS["mem_norm_g"] = COLS["mem_norm_g", ()]


class Core(Prog):

    def __init__(self, nc, ctx, aps):
        super().__init__(nc, ctx)
        self.aps = aps
        self.plan, self.n_units = [], 0
        self.slot = [self.count(f"s_weight_slot{k}") for k in range(RING)]
        self.ring = self.sb("weight_ring", [P, RING, UNIT])
        self.bank = [self.ps(f"bank{i}", [P, 512]) for i in range(4)]
        self.acc = self.ps("acc", [P, KT, S])
        self.hb = [Hand(self) for _ in range(4)]
        self.h = self.sb("h", [P, KT, S])
        self.xn = self.sb("xn", [P, KT, S])
        self.tmp = self.sb("tmp", [P, KT, S])
        self.rstd = self.sb("rstd", [P, S])
        self.act_gate = self.sb("act_gate", [P, 2, S])
        self.hidden = self.sb("hidden", [P, 2, S])
        self.h_gate, self.h_hidden = [Hand(self) for _ in range(2)], [Hand(self) for _ in range(2)]
        self.cons = self.sb("cons", [P, len(CONS) * P])
        self.pv = self.sb("pv", [P, N_COLS])
        self.epsc = self.sb("epsc", [P, len(EPS)])
        start = [self.load(self.cons[:, :], aps["shape_constants"], name="cons"),
                 self.load(self.pv[:, :], aps["columns"], engine="scalar", name="pv")]
        start += [self.pool(lambda e, i=i, v=v: e.memset(self.epsc[:, i:i + 1], v)) for i, v in enumerate(EPS)]
        self.everyone_waits(start)

    def everyone_waits(self, toks):
        for e in self.ENGINES[:4]:
            self.at[e].append(("wait", toks))

    def sb(self, name, shape, dt=F32):
        return self.ctx.enter_context(self.nc.sbuf_tensor(name, shape, dt))

    def ps(self, name, shape):
        return self.ctx.enter_context(self.nc.psum_tensor(name, shape, F32))

    def con(self, name):
        i = CONS.index(name)
        return self.cons[:, i * P:(i + 1) * P]

    def col(self, name, k=0, n=1):
        c = COLS[name] + k
        return self.pv[:, c:c + n]

    def eps(self, v):
        i = EPS.index(v)
        return self.epsc[:, i:i + 1]

    def unit(self, what, a=KT):
        k = self.n_units % RING
        self.n_units += 1
        self.slot[k].off += 16
        self.plan.append(what)
        return (self.ring[:, k, :].rearrange("p (a b) -> p a b", a=a),
                Tok(self.slot[k], self.slot[k].off, self.loop))

    @contextmanager
    def repeat(self, n):
        plan, self.plan = self.plan, []
        first = self.n_units
        with super().repeat(n) as loop:
            yield loop
        body = self.plan
        assert len(body) % RING == 0, len(body)
        self.n_units = first + n * len(body)
        self.plan = plan + [(lambda *o, i=i, w=w: w(*o, i)) for i in range(n) for w in body]

    def pad_units(self, start=0):
        while (self.n_units - start) % RING:
            ap, tok = self.unit(lambda *_: None)
            t = self.mms([(self.bank[0][:, 0:8], ap[:, 0, 0:P], ap[:, 0, 0:8], True, True)] * 2,
                         tok, self.hb[0], release=True)
            self.hb[0].give(t)

    def flush(self):
        if self.pending:
            t = self.mms([(self.bank[0][0:8, 0:8], self.con("identity")[:, 0:8], self.con("identity")[:, 0:8],
                           True, True)] * 2, self.hb[0])
            self.hb[0].give(t)

    def stream(self):
        w, slots = self.aps["weights"], [(self.ring[:, k, :], self.slot[k].sem) for k in range(RING)]

        def run(e):
            for k in range(RING):
                e.dma_start(slots[k][0], w[k]).then_inc(slots[k][1], 16)
            with e.Fori(1, self.n_units // RING) as turn:
                for k in range(RING):
                    e.wait_ge(self.s_free, (turn - 1) * RING + k + 1)
                    e.dma_start(slots[k][0], w[turn * RING + k]).then_inc(slots[k][1], 16)
        return run

    def tile_T(self, ap, c, tok, src, ready, out, w, kt=KT, release=False):
        return self.mms([(out, ap[:, k, c * P:(c + 1) * P], src[:, k, :], k == 0, k == kt - 1)
                         for k in range(kt)], tok, ready, w, release=release)

    def tile_tok(self, ap, b, tok, src, ready, out, w, width=256, release=False):
        return self.mms([(out, src[:, k, b * P:(b + 1) * P], ap[:, k, 0:width], k == 0, k == KT - 1)
                         for k in range(KT)], tok, ready, w, release=release)

    def ffn(self, gate, up, down, src, ready):
        depth, p = 0, self.loop
        while p is not None:
            depth, p = depth + 1, p.parent
        last = []

        def chunk(j, first=False):
            g, tg = self.unit(lambda *i: gate(i[:depth], j(*i[depth:])))
            u, tu = self.unit(lambda *i: up(i[:depth], j(*i[depth:])))
            d, td = self.unit(lambda *i: down(i[:depth], j(*i[depth:])), a=2)
            made = []
            for c in range(2):
                gm = self.tile_T(g, c, tg, src, ready, self.bank[c][:, 0:S], self.hb[c], release=c == 1)
                um = self.tile_T(u, c, tu, src, ready, self.bank[2 + c][:, 0:S], self.hb[2 + c], release=c == 1)
                s = self.act(lambda e, c=c: e.activation(self.act_gate[:, c, :], self.bank[c][:, 0:S], ACT.Silu),
                             gm, self.h_gate[c])
                m = self.dve(lambda e, c=c: e.tensor_tensor(self.hidden[:, c, :], self.bank[2 + c][:, 0:S],
                                                            self.act_gate[:, c, :], ALU.mult), um, s, self.h_hidden[c])
                self.hb[c].give(s), self.hb[2 + c].give(m), self.h_gate[c].give(m)
                made.append(m)
            for c in range(2):
                t = self.mms([(self.acc[:, m, :], d[:, c, m * P:(m + 1) * P], self.hidden[:, c, :],
                               first and c == 0 and m % 2 == 0, False) for m in range(KT)],
                             td, made[c], release=c == 1)
                self.h_hidden[c].give(t)
            return t

        chunk(lambda: 0, first=True)
        with self.repeat(5):
            chunk(lambda i: 1 + 2 * i)
            t = chunk(lambda i: 2 + 2 * i)
        return t

    def inv_sqrt(self, ps, eps, ready, scale=1.0):
        s = self.act(lambda e: e.activation(self.rstd[:, :], ps, ACT.Sqrt, bias=self.eps(eps)), ready)
        self.hb[0].give(s)
        r = self.dve(lambda e: e.reciprocal(self.rstd[:, :], self.rstd[:, :]), s)
        if scale != 1.0:
            r = self.dve(lambda e: e.tensor_scalar(self.rstd[:, :], self.rstd[:, :], scale, None, ALU.mult), r)
        return r

    def mean_sq(self, src, kt, ready, sq, mat="mean", acc_src=False):
        t = None
        for k in range(0, kt, 2):
            s = self.act(lambda e, k=k: e.activation(sq[:, k:k + 2, :], src[:, k:k + 2, :], ACT.Square), ready)
            t = self.mms([(self.bank[0][:, 0:S], self.con(mat), sq[:, j, :], j == 0, j == kt - 1)
                          for j in (k, k + 1)], s, self.hb[0] if k == 0 else None)
        return t

    def rms_scale(self, src, gain, ready, scale=1.0):
        t = self.mean_sq(src, KT, ready, self.tmp)
        return self.inv_sqrt(self.bank[0][:, 0:S], 1e-6, t, scale)

    def rms_norm(self, src, gain, dst, ready):
        r = self.rms_scale(src, gain, ready)
        for k in range(KT):
            t = self.dve(lambda e, k=k: e.scalar_tensor_tensor(
                out=dst[:, k, :], in0=src[:, k, :], scalar=gain(k), in1=self.rstd[:, :],
                op0=ALU.mult, op1=ALU.mult), r)
        return t

    def add_rms(self, gain, ready, scale):
        r = self.rms_scale(self.acc, gain, ready, scale)
        for k in range(KT):
            t = self.dve(lambda e, k=k: e.scalar_tensor_tensor(
                out=self.tmp[:, k, :], in0=self.acc[:, k, :], scalar=gain(k), in1=self.rstd[:, :],
                op0=ALU.mult, op1=ALU.mult), r)
        return self.dve(lambda e: e.tensor_tensor(self.h[:, :, :], self.h[:, :, :], self.tmp[:, :, :], ALU.add), t)

    def layer_norm(self, src, kt, gain, bias, dst, ready, sq, mat="mean", eps=1e-5):
        t = self.mms([(self.bank[1][:, 0:S], self.con(mat), src[:, j, :], j == 0, j == kt - 1)
                      for j in range(kt)], ready, self.hb[1])
        for k in range(kt):
            c = self.dve(lambda e, k=k: e.tensor_tensor(src[:, k, :], src[:, k, :], self.bank[1][:, 0:S],
                                                        ALU.subtract), t)
        self.hb[1].give(c)
        t = self.mean_sq(src, kt, c, sq, mat)
        r = self.inv_sqrt(self.bank[0][:, 0:S], eps, t)
        for k in range(kt):
            t = self.dve(lambda e, k=k: e.scalar_tensor_tensor(
                out=src[:, k, :], in0=src[:, k, :], scalar=gain(k), in1=self.rstd[:, :],
                op0=ALU.mult, op1=ALU.mult), r)
            t = self.act(lambda e, k=k: e.activation(dst[:, k, :], src[:, k, :], ACT.Identity, bias=bias(k)), t)
        return t

    def evac_heads(self, ps, q, t, scale, ready, free):
        a = self.act(lambda e: e.activation(q[:, 2 * t, :], ps[0:64, 0:S], ACT.Copy, scale=scale), ready)
        b = self.dve(lambda e: e.tensor_scalar(q[:, 2 * t + 1, :], ps[64:128, 0:S], scale, None, ALU.mult), ready)
        free.give(a, b)
        return [a, b]

    def project(self, what, n_units, src, ready, take):
        out = []
        for n in range(n_units):
            ap, tok = self.unit(lambda *i, n=n: what(i, n))
            for c in range(2):
                b = (2 * n + c) % 4
                t = self.tile_T(ap, c, tok, src, ready, self.bank[b][:, 0:S], self.hb[b], release=c == 1)
                out.append(take(2 * n + c, self.bank[b], t, self.hb[b]))
        return out

    def project_tok(self, what, n_units, src, ready, dst):
        out = []
        for n in range(n_units):
            ap, tok = self.unit(lambda *i, n=n: what(i, n))
            for c in range(NB):
                b = (2 * n + c) % 4
                t = self.tile_tok(ap, c, tok, src, ready, self.bank[b][:, 0:S], self.hb[b], release=c == 1)
                cp = self.act if c else self.dve
                d = dst[:, c, n * 256:(n + 1) * 256]
                t = (self.act(lambda e, b=b, d=d: e.activation(d, self.bank[b][:, 0:S], ACT.Copy), t) if c else
                     self.dve(lambda e, b=b, d=d: e.tensor_copy(d, self.bank[b][:, 0:S]), t))
                self.hb[b].give(t)
                out.append(t)
        return out

    def attention_buffers(self, of):
        self.wq = self.sb(f"{of}_att_w_by_query", [P, 2, 2, 512])
        self.wk = self.sb(f"{of}_att_w_by_key", [P, 2, 2, 512])
        self.stat = self.sb(f"{of}_att_stats", [P, 2, 3, 2, NB])
        self.h_wq = [Hand(self) for _ in range(2)]
        self.h_wk = [Hand(self) for _ in range(2)]
        self.h_pt2 = [Hand(self) for _ in range(2)]
        self.h_o = [Hand(self) for _ in range(2)]
        self.turn = 0
        self.h_z = [Hand(self) for _ in range(2)]
        self.h_acc = [Hand(self) for _ in range(2)]
        self.h_sg = [Hand(self) for _ in range(4)]
        self.h_tmp = [Hand(self) for _ in range(KT)]

    def softmax_pair(self, scores, causal, norm=None, ready=()):
        side = self.turn % 2
        self.turn += 1
        z, wq, wk, st = self.bank[2 * side:2 * side + 2], self.wq[:, side], self.wk[:, side], self.stat[:, side]
        span = [(0, 128), (128, 256)] if causal else [(0, 256), (256, 256)]
        hands = self.hb[2 * side:2 * side + 2]
        done = []
        for hd in range(2):
            for qb, (at, n) in enumerate(span):
                last = self.mms(scores(hd, qb, z[hd][:, at:at + n]), hands[hd] if qb == 0 else None, ready)
            mx = [self.dve(lambda e, hd=hd, qb=qb, at=at, n=n: e.tensor_reduce(
                st[:, 0, hd, qb:qb + 1], z[hd][:, at:at + n], AX, ALU.max, negate=True), last,
                self.h_wq[side] if hd + qb == 0 else None) for qb, (at, n) in enumerate(span)]
            ex = [self.act(lambda e, hd=hd, qb=qb, at=at, n=n: e.activation(
                wq[:, hd, at:at + n], z[hd][:, at:at + n], ACT.Exp, bias=st[:, 0, hd, qb:qb + 1],
                accum_out=st[:, 1, hd, qb:qb + 1]), mx) for qb, (at, n) in enumerate(span)]
            hands[hd].give(ex)
            r = self.dve(lambda e, hd=hd: e.reciprocal(st[:, 2, hd, :], st[:, 1, hd, :]), ex)
            if norm is not None:
                for qb in range(NB):
                    r = self.dve(lambda e, hd=hd, qb=qb: e.tensor_tensor(
                        st[:, 2, hd, qb:qb + 1], st[:, 2, hd, qb:qb + 1], norm(hd, qb), ALU.mult), r)
            nrm = [self.dve(lambda e, hd=hd, qb=qb, at=at, n=n: e.tensor_scalar(
                wq[:, hd, at:at + n], wq[:, hd, at:at + n], st[:, 2, hd, qb:qb + 1], None, ALU.mult), r)
                for qb, (at, n) in enumerate(span)]
            blocks = [(0, 0), (1, 0), (1, 1)] if causal else [(0, 0), (1, 0), (0, 1), (1, 1)]
            pt = self.acc[:, 2 * hd:2 * hd + 2, :].rearrange("p a b -> p (a b)")

            def turn(e, hd=hd, pt=pt):
                for qb, kb in blocks:
                    i = e.transpose(pt[:, self.kcol(qb, kb, causal):][:, 0:P],
                                    wq[:, hd, span[qb][0] + kb * P:][:, 0:P], self.con("identity"))
                return i
            tr = self.pe(turn, nrm, self.h_pt2[hd])
            w = 128 * len(blocks)
            if hd:
                cp = self.act(lambda e, hd=hd, pt=pt: e.activation(wk[:, hd, 0:w], pt[:, 0:w], ACT.Copy), tr,
                              self.h_wk[side])
            else:
                cp = self.dve(lambda e, hd=hd, pt=pt: e.tensor_copy(wk[:, hd, 0:w], pt[:, 0:w]), tr, self.h_wk[side])
            self.h_pt2[hd].give(cp)
            done.append(cp)
            trl = tr
        self.h_wq[side].give(trl)
        return side, done

    @staticmethod
    def kcol(qb, kb, causal):
        return (kb * 256 + qb * 128) if not (causal and kb == 1) else 256

    def values_pair(self, side, ready, parts, causal, width, take, first=True, last=True):
        ob = self.acc[:, 4 + 2 * side:6 + 2 * side, :]
        for hd in range(2):
            calls = []
            for kb in range(NB):
                q0 = 128 if causal and kb == 1 else 0
                w = self.wk[:, side, hd, kb * 256:kb * 256 + 256 - q0]
                calls.append((ob[0:width, hd, q0:256], parts(hd, kb), w, first and kb == 0, last and kb == 1))
            t = self.mms(calls, ready, self.h_o[side] if first and hd == 0 else None)
        self.h_wk[side].give(t)
        if last:
            self.h_o[side].give(take(ob, t))
        return t


L1 = 2
HEADS, HD = 8, 64
Q_SB, K_SB, V_SB, Q_FX, K_FX, V_FX, F_FX, Q_MEM = 0, 512, 1024, 1536, 2048, 2560, 3072, 3080
LAYER_COLS = {"ffn1_pre_g": 0, "ffn1_post_g": 8, "mix_pre_g": 16, "mix_post_g": 24, "b_gate": 32,
              "ffn2_pre_g": 56, "ffn2_post_g": 64}
N_LAYER_COLS = 72


def block1(c):
    with ExitStack() as own:
        outer, c.ctx = c.ctx, own
        lp = c.sb("layer_params", [P, N_LAYER_COLS])
        wf, bf = c.sb("w_forget", [P, L1 * KT * HEADS]), c.sb("b_forget", [P, L1 * HEADS])
        wfl, bfl = c.sb("w_forget_layer", [P, KT * HEADS]), c.sb("b_forget_layer", [P, HEADS])
        memn = c.sb("mem_norm", [P, KT, S])
        qh, kh = c.sb("q_heads", [64, HEADS, S]), c.sb("k_heads", [64, HEADS, S])
        vh = c.sb("v_tokens", [P, NB, 512])
        oT = c.sb("branch_out", [P, 3, 4, S])
        merged = c.sb("merged", [P, KT, S])
        qmem, kmem = c.sb("q_mem", [P, 4, S]), c.sb("k_mem", [P, 4, S])
        lf, lf2 = c.sb("log_forget", [P, NB, HEADS]), c.sb("log_forget_t", [P, NB, HEADS])
        cT, ncT = c.sb("cum_forget", [HEADS, S]), c.sb("neg_cum_forget", [HEADS, S])
        zt = [c.sb(f"sb_{n}", [P, 2, 2, 384]) for n in ("abs", "softplus", "log_not")]
        sgm = c.sb("branch_gate", [P, 4, S])
        c.attention_buffers("b1")
        t = [c.load(wf[:, :], c.aps["w_forget"], engine="scalar", name="wf"),
             c.load(bf[:, :], c.aps["b_forget_rows"], engine="scalar", name="bf"),
             c.load(memn[:, :, :], c.aps["memory"], engine="scalar", name="mem")]
        ident = c.con("identity")

        c.rms_norm(memn, lambda k: c.col("mem_norm_g", k), memn, t)
        c.barrier()

        with c.repeat(L1) as layer:
            body_start = c.n_units
            g = lambda name: (lambda k: lp[:, LAYER_COLS[name] + k:LAYER_COLS[name] + k + 1])
            tl = [c.dve(lambda e, to=to, of=of, n=n: e.tensor_copy(to[:, :], of[:, bass.ts(layer.cur, n)]))
                  for to, of, n in ((lp, c.pv, N_LAYER_COLS), (wfl, wf, KT * HEADS), (bfl, bf, HEADS))]

            def ffn(n):
                c.barrier()
                t = c.rms_norm(c.h, g(f"ffn{n}_pre_g"), c.xn, tl)
                t = c.ffn(lambda i, j: ("cols", f"ffn{n}_w_gate", i, j * 256),
                          lambda i, j: ("cols", f"ffn{n}_w_up", i, j * 256),
                          lambda i, j: ("rows", f"ffn{n}_w_down", i, j * 256), c.xn, t)
                c.barrier()
                c.add_rms(g(f"ffn{n}_post_g"), t, 0.5)
                c.barrier()

            ffn(1)
            u = c.rms_norm(c.h, g("mix_pre_g"), c.xn, tl)
            w = lambda name, start: (lambda i, n: ("cols", name, i, start + n * 256))

            def heads(q_at, k_at, v_at):
                sc = HD ** -0.5
                tq = c.project(w("w_in", q_at), 2, c.xn, u, lambda t, ps, r, f: c.evac_heads(ps, qh, t, sc, r, f))
                tk = c.project(w("w_in", k_at), 2, c.xn, u, lambda t, ps, r, f: c.evac_heads(ps, kh, t, 1.0, r, f))
                tv = c.project_tok(w("w_in", v_at), 2, c.xn, u, vh)
                return [tq, tk, tv]

            def take_heads(br, pair):
                def take(ob, t):
                    a = c.act(lambda e: e.activation(oT[0:64, br, pair, :], ob[0:64, 0, :], ACT.Copy), t)
                    return c.act(lambda e: e.activation(oT[64:128, br, pair, :], ob[0:64, 1, :], ACT.Copy), a)
                return take

            vpart = lambda pair: (lambda hd, kb: vh[:, kb, (2 * pair + hd) * 64:(2 * pair + hd + 1) * 64])

            r = heads(Q_SB, K_SB, V_SB)
            def weights(pair, hd):
                side, wk = pair % 2, c.wk
                ab, sp, ln = (z[:, side] for z in zt)
                hh, zb, bt = 2 * pair + hd, c.bank[2 * side + hd], c.acc[:, 2 * hd:2 * hd + 2, :]
                bt = bt.rearrange("p a b -> p (a b)")
                tz = c.mms([(zb[:, 0:256], kh[:, hh, 0:128], qh[:, hh, :], True, True),
                            (zb[:, 256:384], kh[:, hh, 128:256], qh[:, hh, 128:256], True, True)],
                           r, c.hb[2 * side + hd])
                z = zb[:, 0:384]
                a = c.act(lambda e: e.activation(ab[:, hd, :], z, ACT.Abs), tz, c.h_z[side] if hd == 0 else None)
                a = c.act(lambda e: e.activation(ab[:, hd, :], ab[:, hd, :], ACT.Exp, scale=-1.0), a)
                a = c.act(lambda e: e.activation(ab[:, hd, :], ab[:, hd, :], ACT.Ln, bias=c.eps(1.0)), a)
                s = c.dve(lambda e: e.scalar_tensor_tensor(out=sp[:, hd, :], in0=z, scalar=0.0, in1=ab[:, hd, :],
                                                           op0=ALU.max, op1=ALU.add), a)
                n = None
                for at, m in ((0, "before"), (128, "ones"), (256, "before")):
                    n = c.dve(lambda e, at=at, m=m: e.scalar_tensor_tensor(
                        out=ln[:, hd, at:at + P], in0=sp[:, hd, at:at + P], scalar=-1.0, in1=c.con(m),
                        op0=ALU.mult, op1=ALU.mult), s)
                lb = c.dve(lambda e: e.tensor_tensor(sp[:, hd, :], z, sp[:, hd, :], ALU.subtract), n)
                c.hb[2 * side + hd].give(lb)
                later, ones = c.con("after"), c.con("ones")
                tb = c.mms([(bt[:, 0:256], later, ln[:, hd, 0:256], True, False),
                            (bt[:, 128:256], ones, ln[:, hd, 256:384], False, True),
                            (bt[:, 256:384], later, ln[:, hd, 256:384], False, True)],
                           n, c.h_pt2[hd])
                x = c.dve(lambda e: e.tensor_tensor(ab[:, hd, :], bt[:, 0:384], sp[:, hd, :], ALU.add), tb, lb)
                c.h_pt2[hd].give(x)
                x = c.act(lambda e: e.activation(ab[:, hd, :], ab[:, hd, :], ACT.Exp), x)
                for at, m in ((0, "before"), (128, "ones"), (256, "before")):
                    x2 = c.pool(lambda e, at=at, m=m: e.tensor_tensor(
                        wk[:, side, hd, at:at + P], ab[:, hd, at:at + P], c.con(m), ALU.mult),
                        x, c.h_wk[side])
                c.h_z[side].give(x2, tb)
                return x2

            for pair in range(4):
                x2 = [weights(pair, 0), weights(pair, 1)]
                c.values_pair(pair % 2, [r, x2], vpart(pair), True, 64, take_heads(0, pair))
            c.barrier()

            r = heads(Q_FX, K_FX, V_FX)
            for b in range(NB):
                t = c.mms([(c.bank[b][:, 0:HEADS], c.xn[:, k, b * P:(b + 1) * P], wfl[:, k * HEADS:(k + 1) * HEADS],
                            k == 0, k == KT - 1) for k in range(KT)], u, tl, c.hb[b])
                x, y = lf[:, b, :], lf2[:, b, :]
                t = c.dve(lambda e, b=b, x=x: e.tensor_tensor(x, c.bank[b][:, 0:HEADS], bfl[:, :], ALU.add), t)
                c.hb[b].give(t)
                a = c.act(lambda e, x=x, y=y: e.activation(y, x, ACT.Abs), t)
                a = c.act(lambda e, y=y: e.activation(y, y, ACT.Exp, scale=-1.0), a)
                a = c.act(lambda e, y=y: e.activation(y, y, ACT.Ln, bias=c.eps(1.0)), a)
                tlf = c.dve(lambda e, x=x, y=y: e.scalar_tensor_tensor(out=x, in0=x, scalar=0.0, in1=y, op0=ALU.min,
                                                                       op1=ALU.subtract), a)
            t = c.mms([(c.bank[0][0:HEADS, 0:128], lf[:, 0, :], c.con("upto"), True, True),
                       (c.bank[0][0:HEADS, 128:256], lf[:, 0, :], c.con("ones"), False, False),
                       (c.bank[0][0:HEADS, 128:256], lf[:, 1, :], c.con("upto"), False, True)], tlf, c.hb[0])
            a = c.dve(lambda e: e.tensor_copy(cT[:, :], c.bank[0][0:HEADS, 0:S]), t)
            a = c.dve(lambda e: e.tensor_scalar(ncT[:, :], c.bank[0][0:HEADS, 0:S], -1.0, None, ALU.mult), a)
            c.hb[0].give(a)
            r = [r, a]
            for pair in range(4):
                def scores(hd, qb, z):
                    hh, n = 2 * pair + hd, 128 * (qb + 1)
                    sel = ident[0:HEADS, hh:hh + 1]
                    out = [(z, qh[:, hh, qb * P:(qb + 1) * P], kh[:, hh, 0:n], True, False),
                           (z, cT[:, qb * P:(qb + 1) * P], sel.to_broadcast([HEADS, n]), False, False),
                           (z, sel.to_broadcast([HEADS, P]), ncT[:, 0:n], False, False),
                           (z[:, n - P:n], ident, c.con("not_before"), False, True)]
                    return out
                side, tw = c.softmax_pair(scores, True, ready=r)
                c.values_pair(side, tw, vpart(pair), True, 64, take_heads(1, pair))

            c.barrier()
            def take128(dst, sc):
                def take(t, ps, ready, free):
                    x = c.act(lambda e: e.activation(dst[:, t, :], ps[:, 0:S], ACT.Copy, scale=sc), ready)
                    free.give(x)
                    return x
                return take
            r = [c.project(w("w_in", Q_MEM), 2, c.xn, u, take128(qmem, 128 ** -0.5)),
                 c.project(w("w_mem_kv", 0), 2, memn, u, take128(kmem, 1.0)),
                 c.project_tok(w("w_mem_kv", 512), 2, memn, u, vh)]
            for pair in range(2):
                scores = lambda hd, qb, z: [(z, qmem[:, 2 * pair + hd, qb * P:(qb + 1) * P], kmem[:, 2 * pair + hd, :],
                                             True, True)]
                side, tw = c.softmax_pair(scores, False, ready=r)
                take = lambda ob, t, pair=pair: c.act(lambda e: e.activation(oT[:, 2, 2 * pair:2 * pair + 2, :], ob, ACT.Copy), t)
                c.values_pair(side, [tw, r], lambda hd, kb: vh[:, kb, (2 * pair + hd) * P:(2 * pair + hd + 1) * P],
                              False, P, take)
            c.barrier()

            for br, name in enumerate(("w_br_sb", "w_br_fox", "w_br_mem")):
                for half in range(2):
                    wb, tb = c.unit(lambda *i, name=name, half=half: ("cols", name, i, half * 512), a=4)
                    for n in range(4):
                        t = c.mms([(c.acc[:, 4 * half + n, :], wb[:, k, n * P:(n + 1) * P], oT[:, br, k, :], k == 0, k == 3)
                                   for k in range(4)], tb, c.h_acc[half] if n == 0 else None, release=n == 3)
                    for n in range(2):
                        wg, tg = c.unit(lambda *i, br=br, half=half, n=n: ("cols", "w_gate", i, br * D + half * 512 + n * 256))
                        for q in range(2):
                            b, m = 2 * n + q, 4 * half + 2 * n + q
                            tq = c.tile_T(wg, q, tg, c.xn, u, c.bank[b][:, 0:S], c.hb[b], release=q == 1)
                            s = c.act(lambda e, b=b, m=m, br=br: e.activation(sgm[:, b, :], c.bank[b][:, 0:S], ACT.Sigmoid,
                                      bias=lp[:, LAYER_COLS["b_gate"] + br * 8 + m:][:, 0:1]), tq, c.h_sg[b])
                            c.hb[b].give(s)
                            dst = merged if br == 0 else c.tmp
                            v = c.dve(lambda e, b=b, m=m, dst=dst: e.tensor_tensor(
                                dst[:, m, :], c.acc[:, m, :], sgm[:, b, :], ALU.mult), s, t, c.h_tmp[m] if br else None)
                            c.h_sg[b].give(v)
                            if br:
                                a = c.pool(lambda e, m=m: e.tensor_tensor(merged[:, m, :], merged[:, m, :], c.tmp[:, m, :],
                                                                         ALU.add), v)
                                c.h_tmp[m].give(a)
                                v2 = [v, a]
                    c.h_acc[half].give(v)
            r = v2
            c.barrier()
            for n in range(4):
                ap, tok = c.unit(lambda *i, n=n: ("cols", "w_out", i, n * 256))
                for q in range(2):
                    t = c.tile_T(ap, q, tok, merged, r, c.acc[:, 2 * n + q, :], None, release=q == 1)
            c.add_rms(g("mix_post_g"), t, 1.0)
            ffn(2)
            c.pad_units(body_start)
            c.flush()
        c.barrier()
        c.ctx = outer


ALPHA2 = 4 ** 0.25
SGU = 2048
CHUNK = 16
NCH = S // CHUNK


def residual_norm(c, alpha, scale, gain, bias, ready):
    for k in range(0, KT, 2):
        t = c.act(lambda e, k=k: e.activation(c.tmp[:, k:k + 2, :], c.acc[:, k:k + 2, :], ACT.Copy, scale=scale), ready)
        t = c.dve(lambda e, k=k: e.scalar_tensor_tensor(out=c.h[:, k:k + 2, :], in0=c.h[:, k:k + 2, :], scalar=alpha,
                                                        in1=c.tmp[:, k:k + 2, :], op0=ALU.mult, op1=ALU.add), t)
    return c.layer_norm(c.h, KT, gain, bias, c.h, t, c.tmp)


def block2(c):
    def ln(i, j):
        return [lambda k, x=x: c.col((f"ln_{x}_2", (i, j)), k) for x in "gb"]

    def ffn(i, j):
        c.barrier()
        t = c.ffn(lambda _, n: ("cols", "ffn_w_in_2", (i, 0 if j == 0 else 1), n * 256),
                  lambda _, n: ("cols", "ffn_w_in_2", (i, 0 if j == 0 else 1), DFF + n * 256),
                  lambda _, n: ("rows", "ffn_w_out_2", (i, 0 if j == 0 else 1), n * 256), c.h, None)
        c.barrier()
        t = residual_norm(c, ALPHA2, 0.5, *ln(i, j), t)
        c.barrier()

    ffn(0, 0)
    spatial_gating(c)
    residual_norm(c, ALPHA2, 1.0, *ln(0, 1), None)
    ffn(0, 2)
    ffn(1, 0)
    rwkv(c)
    residual_norm(c, ALPHA2, 1.0, *ln(1, 1), None)
    ffn(1, 2)


def spatial_gating(c):
    with ExitStack() as own:
        outer, c.ctx = c.ctx, own
        n_t = SGU // P
        uv = c.sb("sgu_uv", [P, 2 * n_t, S])
        sq = c.sb("sgu_squares", [P, n_t, S])
        vt = sq[:, :, :].rearrange("p a b -> p (a b)").rearrange("p (b f) -> p b f", b=NB)
        wsp, bsp = c.sb("sgu_w_spatial", [P, n_t, P]), c.sb("sgu_b_spatial", [n_t, P])
        tw = [c.load(wsp[:, :, :], c.aps["sgu_w_spatial"], engine="scalar", name="wsp"),
              c.load(bsp[:, :], c.aps["sgu_b_spatial"], engine="scalar", name="bsp")]
        for g in range(n_t):
            tm = c.pool(lambda e, g=g: e.tensor_tensor(wsp[:, g, :], wsp[:, g, :], c.con("upto"), ALU.mult), tw)

        def take(t, ps, ready, free):
            x = c.act(lambda e: e.activation(uv[:, t, :], ps[:, 0:S], ACT.Gelu, bias=c.col(("sgu_b_in_2", 0), t)), ready)
            free.give(x)
            return x
        z = c.project(lambda _, n: ("cols", "sgu_w_in_2", 0, n * 256), 16, c.h, None, take)
        v = uv[:, n_t:2 * n_t, :]
        t = c.layer_norm(v, n_t, lambda k: c.col(("sgu_ln_g_2", 0), k), lambda k: c.col(("sgu_ln_b_2", 0), k),
                         v, z, sq, mat="mean_half")
        c.barrier()
        turned = []
        for b in range(NB):
            for g4 in range(n_t // 4):
                n = (g4 + b * 4) % 4

                def turn(e, b=b, g4=g4, n=n):
                    for q in range(4):
                        i = e.transpose(c.bank[n][:, q * P:(q + 1) * P], v[:, 4 * g4 + q, b * P:(b + 1) * P],
                                        c.con("identity"))
                    return i
                t = c.pe(turn, c.hb[n])
                f = vt[:, b, g4 * 512:(g4 + 1) * 512]
                t = (c.act(lambda e, f=f, n=n: e.activation(f, c.bank[n][:, :], ACT.Copy), t) if n % 2 else
                     c.dve(lambda e, f=f, n=n: e.tensor_copy(f, c.bank[n][:, :]), t))
                c.hb[n].give(t)
                turned.append(t)
        for g in range(n_t):
            n = g % 4
            calls = []
            for b in range(NB):
                o = c.bank[n][:, b * P:(b + 1) * P]
                calls += [(o, vt[:, b, g * P:(g + 1) * P], wsp[:, g, :], b == 0, False),
                          (o, c.con("identity")[0:n_t, g:g + 1].to_broadcast([n_t, P]), bsp[:, :], False, True)]
            t = c.mms(calls, turned, tm, tw, c.hb[n])
            t = c.dve(lambda e, g=g, n=n: e.tensor_tensor(uv[:, g, :], uv[:, g, :], c.bank[n][:, 0:S], ALU.mult), t)
            c.hb[n].give(t)
        for n in range(8):
            ap, tok = c.unit(lambda *_, n=n: ("rows", "sgu_w_out_2", 0, n * 256), a=2)
            for q in range(2):
                t2 = c.mms([(c.acc[:, m, :], ap[:, q, m * P:(m + 1) * P], uv[:, 2 * n + q, :],
                             n == 0 and q == 0 and m % 2 == 0, False) for m in range(KT)], tok, t, release=q == 1)
        c.barrier()
        c.ctx = outer


def rwkv(c):
    with ExitStack() as own:
        outer, c.ctx = c.ctx, own
        flat8 = lambda x: x[:, :, :].rearrange("p a b -> p (a b)")
        r, k, kk, bb, v = (c.sb(f"rwkv_{n}", [P, KT, S]) for n in ("r", "k", "kk", "b", "v"))
        ld = c.sb("rwkv_log_decay", [P, NB, D])
        w0row = c.sb("rwkv_w0_row", [1, D])
        lora = c.sb("rwkv_lora", [P, 2, S])
        G, H = c.sb("rwkv_G", [P, 4, NCH, 64]), c.sb("rwkv_H", [P, 4, NCH, 64])
        Rs = c.sb("rwkv_R", [P, 4, S])
        tw0 = c.load(w0row[:, :], c.aps["rwkv_w0_row"], engine="scalar", name="w0")
        ones_row = c.con("ones")[0:1, :]

        def shifted(dst):
            a = c.dve(lambda e: e.tensor_tensor(dst[:, :, 1:S], c.h[:, :, 0:S - 1], c.h[:, :, 1:S], ALU.subtract))
            b = c.dve(lambda e: e.tensor_scalar(dst[:, :, 0:1], c.h[:, :, 0:1], -1.0, None, ALU.mult))
            return [a, b]

        def mix(j, xx, dst, ready):
            for q in range(KT):
                t = c.dve(lambda e, q=q: e.scalar_tensor_tensor(
                    out=dst[:, q, :], in0=xx[:, q, :], scalar=c.col(("rwkv_mu_2", (0, j)), q), in1=c.h[:, q, :],
                    op0=ALU.mult, op1=ALU.add), ready)
            return t

        def copy_out(dst):
            def take(t, ps, ready, free):
                x = (c.act(lambda e: e.activation(dst[:, t, :], ps[:, 0:S], ACT.Copy), ready) if t % 2 else
                     c.dve(lambda e: e.tensor_copy(dst[:, t, :], ps[:, 0:S]), ready))
                free.give(x)
                return x
            return take

        sx = shifted(c.tmp)
        used = None
        ta = None
        for j, dst in enumerate((r, k, v)):
            mixed = c.xn if j % 2 == 0 else kk
            t = mix(j, c.tmp, mixed, [sx, used if j == 2 else None])
            out = c.project(lambda _, n, j=j: ("cols", "rwkv_w_rkv_2", (0, j), n * 256), 4, mixed, t, copy_out(dst))
            if j == 0:
                used = out
        xw = mix(3, c.tmp, kk, out)
        xa = mix(4, c.tmp, bb, None)
        ap, tok = c.unit(lambda *_: ("side", ["rwkv_w1_2", "rwkv_a1_2"], 0, 0))
        t1 = c.mms([(c.bank[0][0:64, 0:S], ap[:, q, 0:64], kk[:, q, :], q == 0, q == KT - 1) for q in range(KT)],
                   tok, xw, c.hb[0])
        t2 = c.mms([(c.bank[1][0:64, 0:S], ap[:, q, 64:128], bb[:, q, :], q == 0, q == KT - 1) for q in range(KT)],
                   tok, xa, c.hb[1], release=True)
        t1 = c.act(lambda e: e.activation(lora[0:64, 0, :], c.bank[0][0:64, 0:S], ACT.Tanh), t1)
        t2 = c.dve(lambda e: e.tensor_copy(lora[0:64, 1, :], c.bank[1][0:64, 0:S]), t2)
        c.hb[0].give(t1), c.hb[1].give(t2)
        c.barrier()
        ap, tok = c.unit(lambda *_: ("stack", ["rwkv_w2_2", "rwkv_a2_2"], 0, 0), a=2)
        for b in range(NB):
            for q in range(2):
                n = 2 * b + q
                t = c.mms([(c.bank[n][:, :], lora[0:64, 0, b * P:(b + 1) * P], ap[0:64, 0, q * 512:(q + 1) * 512], True, False),
                           (c.bank[n][:, :], ones_row, w0row[:, q * 512:(q + 1) * 512], False, True)], tok, tw0, c.hb[n])
                dst = ld[:, b, q * 512:(q + 1) * 512]
                t = c.act(lambda e, n=n, dst=dst: e.activation(dst, c.bank[n][:, :], ACT.Sigmoid), t)
                c.hb[n].give(t)
                tld = c.dve(lambda e, dst=dst: e.tensor_scalar(dst, dst, -float(np.exp(-0.5)), None, ALU.mult), t)
        for q in range(KT):
            n = q % 4
            t = c.mms([(c.bank[n][:, 0:S], ap[0:64, 1, q * P:(q + 1) * P], lora[0:64, 1, :], True, True)] , tok, c.hb[n],
                      release=q == KT - 1)
            ta = c.act(lambda e, n=n, q=q: e.activation(bb[:, q, :], c.bank[n][:, 0:S], ACT.Sigmoid,
                                                        bias=c.col(("rwkv_a0_2", 0), q)), t)
            c.hb[n].give(ta)
        for q in range(KT):
            t = c.dve(lambda e, q=q: e.tensor_scalar(kk[:, q, :], k[:, q, :], c.col(("rwkv_k_k_2", 0), q), None, ALU.mult))
            t = c.act(lambda e, q=q: e.activation(c.xn[:, q, :], kk[:, q, :], ACT.Square), t)
            n = q % 4
            t = c.mms([(c.bank[n][:, 0:S], c.con("head_sum"), c.xn[:, q, :], True, True)], t, c.hb[n])
            t = c.act(lambda e, q=q, n=n: e.activation(c.tmp[:, q, :], c.bank[n][:, 0:S], ACT.Sqrt), t)
            c.hb[n].give(t)
        t = c.dve(lambda e: e.tensor_scalar(c.tmp[:, :, :], c.tmp[:, :, :], 1e-12, None, ALU.max), t)
        t = c.dve(lambda e: e.reciprocal(c.tmp[:, :, :], c.tmp[:, :, :]), t)
        tkk = c.dve(lambda e: e.tensor_tensor(kk[:, :, :], kk[:, :, :], c.tmp[:, :, :], ALU.mult), t)
        for q in range(KT):
            t = c.dve(lambda e, q=q: e.tensor_scalar(c.xn[:, q, :], bb[:, q, :], 1.0, c.col(("rwkv_k_a_2", 0), q),
                                                     ALU.subtract, ALU.mult), ta, tkk)
        t = c.dve(lambda e: e.scalar_tensor_tensor(out=flat8(k), in0=flat8(c.xn), scalar=1.0, in1=flat8(k),
                                                   op0=ALU.add, op1=ALU.mult), t)
        t = c.dve(lambda e: e.tensor_tensor(bb[:, :, :], bb[:, :, :], kk[:, :, :], ALU.mult), tkk)
        c.barrier()
        c.flush()
        rwkv_scan(c, r, k, kk, bb, v, ld, G, H, Rs)
        c.barrier()

        y = kk
        for q in range(KT):
            n = q % 4
            t = c.mms([(c.bank[n][:, 0:S], c.con("head_mean"), y[:, q, :], True, True)], c.hb[n])
            t = c.dve(lambda e, q=q, n=n: e.tensor_tensor(y[:, q, :], y[:, q, :], c.bank[n][:, 0:S], ALU.subtract), t)
            c.hb[n].give(t)
            t = c.act(lambda e, q=q: e.activation(c.tmp[:, q, :], y[:, q, :], ACT.Square), t)
            t = c.mms([(c.bank[n][:, 0:S], c.con("head_mean"), c.tmp[:, q, :], True, True)], t, c.hb[n])
            t = c.act(lambda e, q=q, n=n: e.activation(c.tmp[:, q, :], c.bank[n][:, 0:S], ACT.Sqrt, bias=c.eps(64e-5)), t)
            c.hb[n].give(t)
        t = c.dve(lambda e: e.reciprocal(c.tmp[:, :, :], c.tmp[:, :, :]), t)
        for q in range(KT):
            t2 = c.dve(lambda e, q=q: e.scalar_tensor_tensor(
                out=y[:, q, :], in0=y[:, q, :], scalar=c.col(("rwkv_gn_g_2", 0), q), in1=c.tmp[:, q, :],
                op0=ALU.mult, op1=ALU.mult), t)
            tr = c.dve(lambda e, q=q: e.scalar_tensor_tensor(
                out=c.xn[:, q, :], in0=r[:, q, :], scalar=c.col(("rwkv_r_k_2", 0), q), in1=k[:, q, :],
                op0=ALU.mult, op1=ALU.mult))
            n = q % 4
            tb = c.mms([(c.bank[n][:, 0:S], c.con("head_sum"), c.xn[:, q, :], True, True)], tr, c.hb[n])
            tb = c.dve(lambda e, q=q, n=n: e.tensor_tensor(v[:, q, :], v[:, q, :], c.bank[n][:, 0:S], ALU.mult), tb)
            c.hb[n].give(tb)
            t3 = c.dve(lambda e, q=q: e.scalar_tensor_tensor(
                out=y[:, q, :], in0=y[:, q, :], scalar=c.col(("rwkv_gn_b_2", 0), q), in1=v[:, q, :],
                op0=ALU.add, op1=ALU.add), t2, tb)
        c.barrier()
        sx = shifted(c.tmp)
        t = mix(5, c.tmp, c.xn, sx)
        ap, tok = c.unit(lambda *_: ("side", ["rwkv_g1_2"], 0, 0))
        for q, n in enumerate((P, 32)):
            tq = c.mms([(c.bank[q][0:n, 0:S], ap[:, m, q * P:q * P + n], c.xn[:, m, :], m == 0, m == KT - 1)
                        for m in range(KT)], tok, t, c.hb[q], release=q == 1)
            tg = c.act(lambda e, q=q, n=n: e.activation(lora[0:n, q, :], c.bank[q][0:n, 0:S], ACT.Sigmoid), tq)
            c.hb[q].give(tg)
        ap, tok = c.unit(lambda *_: ("rows", "rwkv_g2_2", 0, 0), a=2)
        for q in range(KT):
            n = q % 4
            t = c.mms([(c.bank[n][:, 0:S], ap[:, 0, q * P:(q + 1) * P], lora[:, 0, :], True, False),
                       (c.bank[n][:, 0:S], ap[0:32, 1, q * P:(q + 1) * P], lora[0:32, 1, :], False, True)],
                      tok, tg, c.hb[n], release=q == KT - 1)
            t = c.dve(lambda e, q=q, n=n: e.tensor_tensor(y[:, q, :], y[:, q, :], c.bank[n][:, 0:S], ALU.mult), t)
            c.hb[n].give(t)
        for n in range(4):
            ap, tok = c.unit(lambda *_, n=n: ("cols", "rwkv_w_o_2", 0, n * 256))
            for q in range(2):
                c.tile_T(ap, q, tok, y, t, c.acc[:, 2 * n + q, :], None, release=q == 1)
        c.barrier()
        c.ctx = outer


def rwkv_scan(c, r, k, kk, bb, v, ld, G, H, Rs):
    flat8 = lambda x: x[:, :, :].rearrange("p a b -> p (a b)")
    pair8 = {n: flat8(x) for n, x in (("r", r), ("k", k), ("kk", kk), ("b", bb), ("v", v))}
    part = lambda n, i: pair8[n][:, bass.ts(i, S)]
    two = lambda x: x.rearrange("p (b t) -> p b t", b=NB)
    with ExitStack() as own:
        outer, c.ctx = c.ctx, own
        sb2 = lambda n: c.sb(f"rwkv_{n}", [P, S])
        ldp = c.sb("rwkv_ld_pair", [P, NB, P])
        eL, emL, eX, eA = (sb2(n) for n in ("e_cum", "e_neg_cum", "e_cum_before", "e_to_end"))
        at, bt, kt, rt, bh, kh, vs = (sb2(n) for n in ("at", "bt", "kt", "rt", "bh", "kh", "vs"))
        sq2 = c.sb("rwkv_squares", [P, 2, 4, P])
        wt, zt, ut = (c.sb(f"rwkv_{n}", [P, NB, P]) for n in ("W", "Z", "U"))
        bx, ux, vx = (c.sb(f"rwkv_{n}", [P, 8, 64]) for n in ("b_by_chunk", "u_by_chunk", "v_by_chunk"))
        st = c.sb("rwkv_state", [P, 2, 4, 64])
        tf, xf = flat8(c.tmp), flat8(c.xn)
        tok = tf[:, 0:1024].rearrange("p (a b f) -> p a b f", a=4, b=NB)
        diag = tf[:, 1024:2048].rearrange("p (n j) -> p n j", n=NCH)
        pm = xf[:, 0:1024].rearrange("p (h a t) -> p h a t", h=2, a=4)
        arb = xf[:, 1024:2048].rearrange("p (h a t) -> p h a t", h=2, a=4)
        rk = c.act_gate[:, :, :].rearrange("p h (b t) -> p h b t", b=NB)
        X = c.hidden[:, :, :].rearrange("p h (b t) -> p h b t", b=NB)
        B = [b[:, :] for b in c.bank] + [c.acc[:, 2 * i:2 * i + 2, :].rearrange("p a b -> p (a b)") for i in range(4)]
        hB = c.hb + [Hand(c) for _ in range(4)]
        ident = c.con("identity")
        mask2 = lambda name: c.con(name).unsqueeze(1).to_broadcast([P, 2, P])
        ld_v = ld[:, :, :]

        def copy(dst, src, ready, who):
            if who == "act":
                return c.act(lambda e: e.activation(dst, src, ACT.Copy), ready)
            return c.dve(lambda e: e.tensor_copy(dst, src), ready)

        def tt(dst, a, b, op, *ready, who=c.dve):
            return who(lambda e: e.tensor_tensor(dst, a, b, op), *ready)

        for half in range(2):
            with c.repeat(4) as q:
                px = lambda half=half, q=q: half * 4 + q.cur
                c.barrier()
                t0 = c.dve(lambda e, px=px: e.tensor_copy(ldp[:, :, :], ld_v[:, :, bass.ts(px(), P)]))
                tv = c.pool(lambda e, px=px: e.tensor_copy(vs[:, :], part("v", px())))
                tl = []
                for i, m in enumerate(("chunk_upto", "chunk_before", "chunk_after")):
                    for b in range(NB):
                        o = B[i // 2][:, (i % 2) * S + b * P:][:, 0:P]
                        tl.append(c.mms([(o, ldp[:, b, :], c.con(m), b == 0, True)], t0,
                                        hB[i // 2] if b == 0 and i % 2 == 0 else None))
                ex = []
                for dst, src, sc in ((eL, B[0][:, 0:S], 1.0), (emL, B[0][:, 0:S], -1.0), (eX, B[0][:, S:2 * S], 1.0),
                                     (eA, B[1][:, 0:S], 1.0)):
                    ex.append(c.act(lambda e, dst=dst, src=src, sc=sc: e.activation(dst[:, :], src, ACT.Exp, scale=sc), tl))
                hB[0].give(ex[:3]), hB[1].give(ex[3])
                ta = c.dve(lambda e, px=px: e.scalar_tensor_tensor(out=at[:, :], in0=part("kk", px()), scalar=-1.0,
                                                            in1=eX[:, :], op0=ALU.mult, op1=ALU.mult), ex)
                tb = c.dve(lambda e, px=px: e.tensor_tensor(bt[:, :], part("b", px()), emL[:, :], ALU.mult), ex)
                tr = c.dve(lambda e, px=px: e.tensor_tensor(rt[:, :], part("r", px()), eL[:, :], ALU.mult), ex)
                tk = c.pool(lambda e, px=px: e.tensor_tensor(kt[:, :], part("k", px()), emL[:, :], ALU.mult), ex)
                tbh = c.dve(lambda e, px=px: e.tensor_tensor(bh[:, :], part("b", px()), eA[:, :], ALU.mult), ex)
                tkh = c.pool(lambda e, px=px: e.tensor_tensor(kh[:, :], part("k", px()), eA[:, :], ALU.mult), ex)
                tt_done = []
                for n, (x, y, w) in enumerate(((at, bh, [ta, tbh]), (kh, vs, [tkh, tv]))):
                    def turn(e, n=n, x=x, y=y):
                        for i, z in enumerate((x, y)):
                            for b in range(NB):
                                ins = e.transpose(B[2 + n][:, (2 * i + b) * P:][:, 0:P], z[:, b * P:(b + 1) * P], ident)
                        return ins
                    t = c.pe(turn, w, hB[2 + n])
                    t = copy(tok[:, 2 * n:2 * n + 2, :, :], B[2 + n].rearrange("p (a b f) -> p a b f", a=2, b=NB), t, "act")
                    hB[2 + n].give(t)
                    tt_done.append(t)
                dc = two(eL[:, :]).rearrange("p b (n t) -> p (b n) t", t=CHUNK)[:, :, CHUNK - 1:CHUNK]
                tdg = tt(diag, c.con("identity_pair")[:, 0:64].unsqueeze(1).to_broadcast([P, NCH, 64]),
                         dc.to_broadcast([P, NCH, 64]), ALU.mult, ex, who=c.pool)
                tri = []
                for hd in range(2):
                    R = slice(64 * hd, 64 * hd + 64)
                    bA, bB, bC = 4 + 2 * hd, 5 + 2 * hd, hd
                    T = [slice(b * P, (b + 1) * P) for b in range(NB)]
                    prod = lambda bank, at_, x, y: [(B[bank][:, at_ + b * P:][:, 0:P], x[R, T[b]], y[R, T[b]],
                                                     at_ == 0 and b == 0, True) for b in range(NB)]
                    t = c.mms(prod(bA, 0, bt, at) + prod(bA, S, at, bt), ta, tb, hB[bA])
                    m1 = tt(pm[:, hd, 0:2, :], two(B[bA][:, 0:S]), mask2("chunk_before"), ALU.mult, t)
                    m2 = tt(pm[:, hd, 2:4, :], two(B[bA][:, S:2 * S]), mask2("chunk_after"), ALU.mult, t)
                    hB[bA].give(m2)
                    t = c.mms(prod(bB, 0, kt, at) + prod(bB, S, bt, rt), ta, tb, tr, tk, hB[bB])
                    m3 = tt(arb[:, hd, 0:2, :], two(B[bB][:, 0:S]), mask2("chunk_before"), ALU.mult, t)
                    m4 = tt(arb[:, hd, 2:4, :], two(B[bB][:, S:2 * S]), mask2("chunk_upto"), ALU.mult, t)
                    hB[bB].give(m4)
                    t = c.mms(prod(bC, 0, kt, rt), tr, tk, hB[bC])
                    m5 = tt(rk[:, hd], two(B[bC][:, 0:S]), mask2("chunk_upto"), ALU.mult, t)
                    hB[bC].give(m5)
                    x0 = tt(X[:, hd], pm[:, hd, 0:2, :], mask2("identity"), ALU.add, m1)
                    tri.append((m1, m2, m3, m4, m5, x0))
                mats = [dict(P=pm[:, hd, 0:2, :], M=pm[:, hd, 2:4, :], t=list(tri[hd])) for hd in range(2)]
                for step in range(3):
                    for hd in range(2):
                        m = mats[hd]
                        bA, bB = 4 + 2 * hd, 5 + 2 * hd
                        dst = sq2[:, hd] if step % 2 == 0 else pm[:, hd]
                        calls = [(B[bA][:, S + b * P:][:, 0:P], m["P"][:, b, :], m["M"][:, b, :], b == 0, True) for b in range(NB)]
                        if step < 2:
                            calls += [(B[bA][:, b * P:][:, 0:P], m["M"][:, b, :], m["P"][:, b, :], False, True) for b in range(NB)]
                        t = c.mms(calls, m["t"], hB[bA])
                        if step < 2:
                            cp = copy(dst, B[bA].rearrange("p (a t) -> p a t", a=4), t, "act")
                        else:
                            cp = copy(dst[:, 2:4, :], two(B[bA][:, S:2 * S]), t, "act")
                        hB[bA].give(cp)
                        m["P"], m["M"] = dst[:, 0:2, :], dst[:, 2:4, :]
                        t = c.mms([(B[bB][:, b * P:][:, 0:P], m["M"][:, b, :], X[:, hd, b, :], b == 0, True)
                                   for b in range(NB)], cp, m["t"], hB[bB])
                        ad = tt(X[:, hd], X[:, hd], two(B[bB][:, 0:S]), ALU.add, t)
                        hB[bB].give(ad)
                        m["t"] = [cp, ad]
                done = [m["t"] for m in mats]
                F = [slice(64 * hd, 64 * hd + 64) for hd in range(2)]
                hdb = [(hd, b) for hd in range(2) for b in range(NB)]
                t = c.mms([(B[2][:, b * P + 64 * hd:][:, 0:64], X[:, hd, b, :], tok[:, 0, b, F[hd]], i == 0, True)
                           for i, (hd, b) in enumerate(hdb)], done, tt_done, hB[2])
                tw_ = copy(wt[:, :, :], two(B[2][:, 0:S]), t, "act")
                hB[2].give(tw_)
                t = c.mms([(B[3][:, b * P + 64 * hd:][:, 0:64], arb[:, hd, b, :], tok[:, 3, b, F[hd]], i == 0, True)
                           for i, (hd, b) in enumerate(hdb)], done, tt_done, hB[3])
                tz = copy(zt[:, :, :], two(B[3][:, 0:S]), t, "dve")
                hB[3].give(tz)
                t = c.mms([(B[3][:, b * P + 64 * hd:][:, 0:64], X[:, hd, b, :], zt[:, b, F[hd]], i == 0, True)
                           for i, (hd, b) in enumerate(hdb)], tz, hB[3])
                tu = copy(ut[:, :, :], two(B[3][:, 0:S]), t, "dve")
                hB[3].give(tu)
                for hd in range(2):
                    R, bk, bk2 = slice(64 * hd, 64 * hd + 64), 4 + hd, 6 + hd
                    t = c.mms([(B[bk][:, b * P:][:, 0:P], wt[:, b, :], arb[:, hd, 2 + b, :], b == 0, True)
                               for b in range(NB)], tw_, tri[hd], hB[bk])
                    t = c.dve(lambda e, R=R, bk=bk, q=q: e.tensor_tensor(
                        Rs[R].rearrange("p a b -> p (a b)")[:, bass.ts(q.cur, S)], B[bk][R, 0:S], rt[R, :], ALU.add), t)
                    hB[bk].give(t)
                    calls = []
                    for b in range(NB):
                        calls += [(B[bk2][:, b * P:][:, 0:P], ut[:, b, :], arb[:, hd, 2 + b, :], b == 0, False),
                                  (B[bk2][:, b * P:][:, 0:P], tok[:, 3, b, :], rk[:, hd, b, :], False, True)]
                    t = c.mms(calls, tu, tri[hd], tt_done, hB[bk2])
                    t = c.act(lambda e, R=R, bk2=bk2, px=px: e.activation(pair8["kk"][R, bass.ts(px(), S)], B[bk2][R, 0:S],
                                                                   ACT.Copy), t, ta)
                    hB[bk2].give(t)
                h_x = None
                for i, (hd, b) in enumerate(hdb):
                    R = slice(64 * hd, 64 * hd + 64)
                    spread = lambda src: src.unsqueeze(1).to_broadcast([P, 8, 64])
                    chunks = c.con("chunk_of")[:, 0:8].unsqueeze(2).to_broadcast([P, 8, 64])
                    s1 = tt(bx[:, :, :], spread(tok[:, 1, b, F[hd]]), chunks, ALU.mult, tt_done, h_x)
                    s2 = tt(ux[:, :, :], spread(ut[:, b, F[hd]]), chunks, ALU.mult, tu, h_x)
                    s3 = tt(vx[:, :, :], spread(tok[:, 3, b, F[hd]]), chunks, ALU.mult, tt_done, h_x, who=c.pool)
                    bg, bq = i % 2, 2 + i % 2
                    fl = lambda x: x[:, :, :].rearrange("p n j -> p (n j)")
                    tg = c.mms([(B[bg], wt[:, b, :], fl(bx), True, True)], tw_, s1, hB[bg])
                    th = c.mms([(B[bq], tok[:, 1, b, :], fl(ux), True, False), (B[bq], tok[:, 2, b, :], fl(vx), False, True)],
                               s2, s3, hB[bq])
                    h_x = [tg, th]
                    n8 = slice(8 * b, 8 * b + 8)
                    gdst = lambda x, R=R, n8=n8, q=q: x[R].rearrange("p q n j -> p q (n j)")[:, bass.ds(q.cur, 1), 512 * (n8.start // 8):][:, :, 0:512]
                    tg = c.dve(lambda e, R=R, n8=n8, bg=bg, gdst=gdst: e.tensor_tensor(
                        gdst(G), B[bg][R, :].unsqueeze(1), diag[R, n8, :].rearrange("p n j -> p (n j)").unsqueeze(1), ALU.add), tg, tdg)
                    hB[bg].give(tg)
                    th = c.act(lambda e, R=R, n8=n8, bq=bq, gdst=gdst: e.activation(
                        gdst(H), B[bq][R, :].unsqueeze(1), ACT.Copy), th)
                    hB[bq].give(th)
            c.barrier()
            t = c.dve(lambda e: e.memset(st[:, 0, :, :], 0.0))
            yb = c.acc[:, 0:4, :]
            for n in range(NCH):
                cur, nxt = n % 2, (n + 1) % 2
                sb_, hs_ = B[nxt], hB[nxt]
                if n < NCH - 1:
                    tg = c.mms([(sb_[64 * hd:64 * hd + 64, p_ * 64:(p_ + 1) * 64], G[64 * hd:64 * hd + 64, p_, n, :],
                                 st[64 * hd:64 * hd + 64, cur, p_, :], p_ == 0, True)
                                for p_ in range(4) for hd in range(2)], t, hs_)
                ty = c.mms([(yb[64 * hd:64 * hd + 64, p_, n * CHUNK:(n + 1) * CHUNK], st[64 * hd:64 * hd + 64, cur, p_, :],
                             Rs[64 * hd:64 * hd + 64, p_, n * CHUNK:(n + 1) * CHUNK], True, True)
                            for p_ in range(4) for hd in range(2)], t)
                if n < NCH - 1:
                    t2 = tt(st[:, nxt], sb_[:, 0:S].rearrange("p (a j) -> p a j", a=4), H[:, :, n, :], ALU.add,
                            tg, last_y if n else None)
                    hs_.give(t2)
                    t = t2
                last_y = ty
            y4 = kk[:, 4 * half:4 * half + 4, :]
            tt(y4, y4, yb, ALU.add, ty)
            c.barrier()
        c.ctx = outer


ALPHA3 = 2 ** 0.25
Q_N, KV_C, KV_S, KV_W, Q_M, K_M, V_M, CONV_A, CONV_G = 0, 256, 384, 512, 652, 908, 1164, 1420, 1676
Q_H, F_H, I_H, G_H = 1932, 2188, 2444, 2700
N_CMP, CMP_STEP = 15, 16
BIAS_W = 512
HANKEL_W = 384
TAPS = 31


def bucket_constants():
    d = 255 - np.arange(BIAS_W)
    n = np.maximum(d, 0)
    large = 16 + (np.log(np.maximum(n, 1).astype(np.float32) / 16) / np.log(128 / 16) * 16).astype(np.int32)
    bucket = np.where(n < 16, n, np.minimum(large, 31))
    hot = (np.arange(32)[:, None] == bucket[None, :]) & (d[None, :] >= 0)
    return hot.astype(np.float32), np.where(d < 0, -1e30, 0.0)[None, :].astype(np.float32)


def block3(c):
    c.barrier()
    w3 = lambda start: (lambda *_: ("cols", "w_in_3", 0, start))
    with ExitStack() as own:
        outer, c.ctx = c.ctx, own
        mix = c.sb("mix_out", [P, KT, S])
        attention3(c, w3, mix)
        conv3(c, w3, mix)
        hgrn3(c, w3, mix)
        for n in range(4):
            ap, tok = c.unit(lambda *_, n=n: ("cols", "w_out_3", 0, n * 256))
            for q in range(2):
                c.tile_T(ap, q, tok, mix, None, c.acc[:, 2 * n + q, :], None, release=q == 1)
        c.barrier()
        residual_norm(c, ALPHA3, 1.0, lambda k: c.col(("ln1_g_3", 0), k), lambda k: c.col(("ln1_b_3", 0), k), None)
        c.barrier()

        def chunk(j, parity, first=False):
            a, ta = c.unit(lambda *i: ("cols", "w_ff1_3", 0, j(*i) * 256))
            d, td = c.unit(lambda *i: ("rows", "w_ff2_3", 0, j(*i) * 256), a=2)
            made = []
            for q in range(2):
                b = 2 * parity + q
                t = c.tile_T(a, q, ta, c.h, None, c.bank[b][:, 0:S], c.hb[b], release=q == 1)
                r = c.act(lambda e, q=q, b=b: e.activation(c.act_gate[:, q, :], c.bank[b][:, 0:S], ACT.Relu), t, c.h_gate[q])
                c.hb[b].give(r)
                m = c.dve(lambda e, q=q: e.tensor_tensor(c.hidden[:, q, :], c.act_gate[:, q, :], c.act_gate[:, q, :],
                                                         ALU.mult), r, c.h_hidden[q])
                c.h_gate[q].give(m)
                made.append(m)
            for q in range(2):
                t = c.mms([(c.acc[:, m, :], d[:, q, m * P:(m + 1) * P], c.hidden[:, q, :],
                            first and q == 0 and m % 2 == 0, False) for m in range(KT)], td, made[q], release=q == 1)
                c.h_hidden[q].give(t)

        chunk(lambda: 0, 0, first=True)
        with c.repeat(5):
            for n in range(3):
                chunk(lambda i, n=n: 1 + 3 * i + n, (n + 1) % 2)
        c.barrier()
        residual_norm(c, ALPHA3, 1.0, lambda k: c.col(("ln2_g_3", 0), k), lambda k: c.col(("ln2_b_3", 0), k), None)
        c.barrier()
        c.ctx = outer


def attention3(c, w3, mix):
    with ExitStack() as own:
        outer, c.ctx = c.ctx, own
        c.attention_buffers("b3")
        hot, mrow = c.sb("bias_one_hot", [32, BIAS_W]), c.sb("bias_mask", [1, BIAS_W])
        tabT, brow = c.sb("bias_table", [32, 8]), c.sb("bias_rows", [8, BIAS_W])
        hk = c.sb("bias_hankel", [P, 8, HANKEL_W])
        w2 = c.sb("cmp_w2", [P, 2, 2, 64])
        qn, qm, kmo = (c.sb(n, [64, 4, S]) for n in ("q_nsa", "q_moba", "k_moba"))
        kw_ = c.sb("k_sel_win", [64, 2, S])
        vw_ = c.sb("v_sel_win", [P, NB, 2, 64])
        vmo = c.sb("v_moba", [P, NB, 256])
        gates = c.sb("nsa_gates", [P, NB, 12])
        dup = c.sb("cmp_tokens", [P, 2, S])
        win = c.sb("cmp_windows", [P, 2, 16, N_CMP])
        hc = c.sb("cmp_hidden", [P, 2, 2, N_CMP])
        kc, vc = c.sb("cmp_k", [64, N_CMP]), c.sb("cmp_v", [N_CMP, 64])
        pc, pct = c.sb("cmp_w", [P, 2, NB, 16]), c.sb("cmp_w_by_key", [N_CMP, 2, S])
        cst = c.sb("cmp_stats", [P, 3, 2, NB])
        ident, flip = c.con("identity"), c.con("flip")

        tl = [c.load(x[:, :], c.aps[n], engine="scalar", name=n) for x, n in
              ((hot, "bias_one_hot"), (mrow, "bias_mask"), (tabT, "bias_table"))]
        tw2 = c.load(w2[:, :, :, :], c.aps["cmp_w2"], engine="scalar", name="cmp_w2")
        t = c.mms([(c.bank[0][0:8, :], tabT[:, :], hot[:, :], True, False),
                   (c.bank[0][0:8, :], c.con("ones")[0:1, 0:8], mrow[:, :], False, True)], tl, c.hb[0])
        t = c.dve(lambda e: e.tensor_copy(brow[:, :], c.bank[0][0:8, :]), t)
        c.hb[0].give(t)
        scratch = c.nc.dram_tensor("bias_scratch", (8, BIAS_W), F32, kind="Internal").ap()
        t = c.load(scratch, brow[:, :], t, engine="scalar", name="bias_store")
        hankel = bass.AP(tensor=scratch.tensor, offset=0, ap=[[1, P], [BIAS_W, 8], [1, HANKEL_W]])
        thk = c.load(hk[:, :, :], hankel, t, engine="scalar", name="hankel")

        sc = HD ** -0.5
        take_heads = lambda dst, s: (lambda t, ps, r, f: c.evac_heads(ps, dst, t, s, r, f))
        r_q = c.project(lambda _, n: w3(Q_N)(), 1, c.h, None, take_heads(qn, sc))
        ap, tok = c.unit(w3(KV_C))
        t = c.tile_T(ap, 0, tok, c.h, None, c.bank[2][:, 0:S], c.hb[2])
        td = []
        for e_ in range(2):
            for half in range(2):
                td.append(c.act(lambda e, e_=e_, half=half: e.activation(
                    dup[64 * half:64 * half + 64, e_, :], c.bank[2][64 * e_:64 * e_ + 64, 0:S], ACT.Copy), t))
        c.hb[2].give(td)
        t = c.mms([(c.bank[3][0:64, 0:S], ap[:, k, 128:192], c.h[:, k, :], k == 0, k == KT - 1) for k in range(KT)],
                  tok, c.hb[3])
        rk = [c.dve(lambda e: e.tensor_copy(kw_[:, 0, :], c.bank[3][0:64, 0:S]), t)]
        c.hb[3].give(rk)
        rv = []

        def tokens(ap, tok, at, width, b, bank, dst, func=ACT.Copy, release=False):
            t = c.mms([(c.bank[bank][:, 0:width], c.h[:, k, b * P:(b + 1) * P], ap[:, k, at:at + width], k == 0,
                        k == KT - 1) for k in range(KT)], tok, c.hb[bank], release=release)
            t = c.act(lambda e: e.activation(dst, c.bank[bank][:, 0:width], func), t)
            c.hb[bank].give(t)
            return t
        for b in range(NB):
            rv.append(tokens(ap, tok, 192, 64, b, b, vw_[:, b, 0, :], release=b == 1))
        ap, tok = c.unit(w3(KV_W))
        t = c.mms([(c.bank[2][0:64, 0:S], ap[:, k, 0:64], c.h[:, k, :], k == 0, k == KT - 1) for k in range(KT)],
                  tok, c.hb[2])
        rk.append(c.dve(lambda e: e.tensor_copy(kw_[:, 1, :], c.bank[2][0:64, 0:S]), t))
        c.hb[2].give(rk[-1])
        for b in range(NB):
            rv.append(tokens(ap, tok, 64, 64, b, b, vw_[:, b, 1, :]))
        for b in range(NB):
            rv.append(tokens(ap, tok, 128, 12, b, 2 + b, gates[:, b, :], func=ACT.Sigmoid, release=b == 1))
        r_m = [c.project(lambda _, n: w3(Q_M)(), 1, c.h, None, take_heads(qm, sc)),
               c.project(lambda _, n: w3(K_M)(), 1, c.h, None, take_heads(kmo, 1.0)),
               c.project_tok(lambda _, n: w3(V_M)(), 1, c.h, None, vmo)]

        for e_ in range(2):
            tw = []
            for half in range(2):
                R = slice(64 * half, 64 * half + 64)
                v = dup[R, e_, :].rearrange("p (n l m) -> p l m n", n=16, l=8, m=2)
                for hi in range(2):
                    pe_ = c.col(("nsa_cmp_pe_3", (0, e_)), 8 * hi, 8)[R].unsqueeze(2).to_broadcast([64, 8, N_CMP])
                    tw.append(c.dve(lambda e, v=v, hi=hi, half=half, R=R, e_=e_, pe_=pe_: e.tensor_tensor(
                        win[R, e_, 8 * hi:8 * hi + 8, :], v[:, :, half, hi:hi + N_CMP], pe_, ALU.add), td))
            t = []
            for n in range(2):
                ap, tok = c.unit(lambda *_, n=n, e_=e_: ("cols", "nsa_cmp_w1_3", (0, e_, slice(n * D, n * D + D)), 0))
                for m in range(2):
                    t.append(c.mms([(c.bank[2 * e_ + m][:, 0:N_CMP], ap[:, k, m * P:(m + 1) * P], win[:, e_, 8 * n + k, :],
                                     n == 0 and k == 0, n == 1 and k == KT - 1) for k in range(KT)],
                                   tok, tw, c.hb[2 * e_ + m] if n == 0 else None, release=m == 1))
            tg = []
            for m in range(2):
                tg.append(c.act(lambda e, m=m, e_=e_: e.activation(hc[:, e_, m, :], c.bank[2 * e_ + m][:, 0:N_CMP],
                          ACT.Gelu_apprx_tanh, bias=c.col(("nsa_cmp_b1_3", (0, e_)), m)), t))
                c.hb[2 * e_ + m].give(tg[-1])
            if e_ == 0:
                t = c.mms([(c.bank[0][0:64, 0:N_CMP], w2[:, 0, m, :], hc[:, 0, m, :], m == 0, m == 1) for m in range(2)],
                          tg, tw2, c.hb[0])
                tkc = c.dve(lambda e: e.tensor_copy(kc[:, :], c.bank[0][0:64, 0:N_CMP]), t)
                c.hb[0].give(tkc)
            else:
                t = c.mms([(c.bank[1][0:N_CMP, 0:64], hc[:, 1, m, :], w2[:, 1, m, :], m == 0, m == 1) for m in range(2)],
                          tg, tw2, c.hb[1])
                tvc = c.dve(lambda e: e.tensor_copy(vc[:, :], c.bank[1][0:N_CMP, 0:64]), t)
                c.hb[1].give(tvc)

        def bias(z, head, qb):
            w = hk[:, head, P:2 * P] if qb == 0 else hk[:, head, 0:2 * P]
            return (z, flip, w, False, True)

        def take(pair):
            def f(ob, t):
                a = c.act(lambda e: e.activation(mix[0:64, pair, :], ob[0:64, 0, :], ACT.Copy), t)
                return c.act(lambda e: e.activation(mix[64:128, pair, :], ob[0:64, 1, :], ACT.Copy), a)
            return f

        def compressed(pair, ready):
            z = c.bank[0][:, 0:64].rearrange("p (h b n) -> p h b n", h=2, b=NB)
            calls = []
            for hd in range(2):
                for qb in range(NB):
                    h = 2 * pair + hd
                    off = 159 if qb == 0 else 31
                    calls += [(z[:, hd, qb, 0:N_CMP], qn[:, h, qb * P:(qb + 1) * P], kc[:, :], hd + qb == 0, False),
                              (z[:, hd, qb, 0:N_CMP], flip, hk[:, h, off:off + CMP_STEP * (N_CMP - 1) + 1:CMP_STEP], False, True)]
            t = c.mms(calls, ready, c.hb[0])
            t = c.dve(lambda e: e.tensor_reduce(cst[:, 0, :, :], z[:, :, :, 0:N_CMP], AX, ALU.max, negate=True), t)
            t = c.dve(lambda e: e.tensor_scalar(cst[:, 0, :, :], cst[:, 0, :, :], 1e20, None, ALU.min), t)
            ex = [c.act(lambda e, hd=hd, qb=qb: e.activation(
                pc[:, hd, qb, 0:N_CMP], z[:, hd, qb, 0:N_CMP], ACT.Exp, bias=cst[:, 0, hd, qb:qb + 1],
                accum_out=cst[:, 1, hd, qb:qb + 1]), t) for hd in range(2) for qb in range(NB)]
            c.hb[0].give(ex)
            t = c.dve(lambda e: e.tensor_scalar(cst[:, 1, :, :], cst[:, 1, :, :], 1e-30, None, ALU.max), ex)
            t = c.dve(lambda e: e.reciprocal(cst[:, 2, :, :], cst[:, 1, :, :]), t)
            tn = []
            for hd in range(2):
                for qb in range(NB):
                    g = gates[:, qb, 3 * (2 * pair + hd):][:, 0:1]
                    tn.append(c.dve(lambda e, hd=hd, qb=qb, g=g: e.tensor_scalar(
                        pc[:, hd, qb, 0:N_CMP], pc[:, hd, qb, 0:N_CMP], cst[:, 2, hd, qb:qb + 1], g, ALU.mult, ALU.mult), t, rv))
            pt = c.acc[:, 0:2, :].rearrange("p a b -> p (a b)")

            def turn(e):
                for hd in range(2):
                    for qb in range(NB):
                        i = e.transpose(pt[0:N_CMP, (2 * hd + qb) * P:][:, 0:P], pc[:, hd, qb, 0:N_CMP], ident)
                return i
            t = c.pe(turn, tn, c.h_pt2[0])
            t = c.act(lambda e: e.activation(pct[:, :, :], pt[0:N_CMP, :].rearrange("p (h q) -> p h q", h=2), ACT.Copy),
                      t, h_pct)
            c.h_pt2[0].give(t)
            return t

        h_pct = Hand(c)
        for pair in range(2):
            ready = [r_q, rk, thk]
            ws = []
            for kind in range(2):
                def scores(hd, qb, z, kind=kind, pair=pair):
                    h = 2 * pair + hd
                    return [(z, qn[:, h, qb * P:(qb + 1) * P], kw_[:, kind, 0:(qb + 1) * P], True, False), bias(z, h, qb)]
                gate = lambda hd, qb, kind=kind, pair=pair: gates[:, qb, 3 * (2 * pair + hd) + 1 + kind:][:, 0:1]
                ws.append(c.softmax_pair(scores, True, norm=gate, ready=[ready, rv]))
            tc_ = compressed(pair, [ready, tkc])
            ob = c.acc[:, 4 + 2 * pair:6 + 2 * pair, :]
            for hd in range(2):
                calls = [(ob[0:64, hd, :], vc[:, :], pct[:, hd, :], True, False)]
                for kind in range(2):
                    for kb in range(NB):
                        q0 = 128 * kb
                        calls.append((ob[0:64, hd, q0:256], vw_[:, kb, kind, :],
                                      c.wk[:, kind, hd, kb * 256:kb * 256 + 256 - q0], False, kind + kb == 2))
                t = c.mms(calls, [w[1] for w in ws], tc_, tvc, rv, c.h_o[pair] if hd == 0 else None)
            c.h_wk[0].give(t), c.h_wk[1].give(t), h_pct.give(t)
            c.h_o[pair].give(take(pair)(ob, t))
        for pair in range(2):
            def scores(hd, qb, z, pair=pair):
                h = 2 * pair + hd
                return [(z, qm[:, h, qb * P:(qb + 1) * P], kmo[:, h, 0:(qb + 1) * P], True, False), bias(z, 4 + h, qb)]
            side, tw = c.softmax_pair(scores, True, ready=[r_m, thk])
            c.values_pair(side, [tw, r_m], lambda hd, kb, pair=pair: vmo[:, kb, (2 * pair + hd) * 64:][:, 0:64],
                          True, 64, take(2 + pair))
        c.barrier()
        c.ctx = outer


def conv3(c, w3, mix):
    with ExitStack() as own:
        outer, c.ctx = c.ctx, own
        hp = c.sb("conv_in", [P, 2, S + TAPS - 1])
        sg, cv, sq = (c.sb(f"conv_{n}", [P, 2, S]) for n in ("gate", "out", "sq"))
        pw = c.sb("conv_pw", [P, 2, 256])
        tp = c.load(pw[:, :, :], c.aps["conv_pw"], engine="scalar", name="conv_pw")
        tz = c.pool(lambda e: e.memset(hp[:, :, 0:TAPS - 1], 0.0))

        def copy_in(t, ps, r, f):
            x = c.dve(lambda e: e.tensor_copy(hp[:, t, TAPS - 1:], ps[:, 0:S]), r)
            f.give(x)
            return x

        def gate(t, ps, r, f):
            x = c.act(lambda e: e.activation(sg[:, t, :], ps[:, 0:S], ACT.Sigmoid), r)
            f.give(x)
            return x
        a = c.project(lambda _, n: w3(CONV_A)(), 1, c.h, None, copy_in)
        g = c.project(lambda _, n: w3(CONV_G)(), 1, c.h, None, gate)
        t = c.dve(lambda e: e.tensor_tensor(hp[:, :, TAPS - 1:], hp[:, :, TAPS - 1:], sg[:, :, :], ALU.mult), a, g)
        t = [c.dve(lambda e, q=q: e.tensor_scalar(cv[:, q, :], hp[:, q, 0:S], c.col(("conv_dw_w_3", (0, 0)), q),
                                                  c.col(("conv_dw_b_3", 0), q), ALU.mult, ALU.add), t, tz) for q in range(2)]
        for j in range(1, TAPS):
            t = [c.dve(lambda e, q=q, j=j: e.scalar_tensor_tensor(
                out=cv[:, q, :], in0=hp[:, q, j:j + S], scalar=c.col(("conv_dw_w_3", (0, j)), q), in1=cv[:, q, :],
                op0=ALU.mult, op1=ALU.add), t[q]) for q in range(2)]
        t = c.layer_norm(cv, 2, lambda k: c.col(("conv_ln_g_3", 0), k), lambda k: c.col(("conv_ln_b_3", 0), k), cv, t, sq,
                         mat="mean_256")
        t = c.act(lambda e: e.activation(cv[:, :, :], cv[:, :, :], ACT.Silu), t)
        for q in range(2):
            t2 = c.mms([(c.bank[q][:, 0:S], pw[:, k, q * P:(q + 1) * P], cv[:, k, :], k == 0, k == 1) for k in range(2)],
                       t, tp, c.hb[q])
            t2 = c.dve(lambda e, q=q: e.tensor_copy(mix[:, 4 + q, :], c.bank[q][:, 0:S]), t2)
            c.hb[q].give(t2)
        c.barrier()
        c.ctx = outer


def hgrn3(c, w3, mix):
    with ExitStack() as own:
        outer, c.ctx = c.ctx, own
        PAD = CHUNK
        t3 = lambda n: c.sb(f"hgrn_{n}", [P, 2, S])
        qT, kT_, eU, eA, F, pr, qp, gT, o, kh = (t3(n) for n in ("q", "k", "e_from_start", "e_to_end", "decay", "pairs",
                                                                "pairs_q", "gate", "o", "k_to_end"))
        kp, fp, vp = (c.sb(f"hgrn_{n}_padded", [P, 2, PAD + S]) for n in ("k", "f", "v"))
        lf, lf2 = c.sb("hgrn_log_f", [P, NB, 256]), c.sb("hgrn_log_f_t", [P, NB, 256])
        vt, kt = c.sb("hgrn_v_tok", [P, NB, 256]), c.sb("hgrn_k_tok", [P, NB, 256])
        vx = c.sb("hgrn_v_by_chunk", [P, 2, 8, 64])
        Hc, St = c.sb("hgrn_H", [P, 2, NCH, 64]), c.sb("hgrn_S", [P, 2, NCH, 64])
        pv_ = c.sb("hgrn_part", [P, 2, S])
        tz = [c.pool(lambda e, x=x: e.memset(x[:, :, 0:PAD], 0.0)) for x in (kp, fp, vp)]

        def to(dst, func=ACT.Copy):
            def take(t, ps, r, f):
                x = c.act(lambda e: e.activation(dst[:, t, :], ps[:, 0:S], func), r)
                f.give(x)
                return x
            return take
        rq = c.project(lambda _, n: w3(Q_H)(), 1, c.h, None, to(qT))

        def both(start, take, tok_dst):
            ap, tok = c.unit(w3(start))
            out = []
            for q in range(2):
                t = c.tile_T(ap, q, tok, c.h, None, c.bank[q][:, 0:S], c.hb[q])
                out.append(take(q, c.bank[q], t, c.hb[q]))
            for b in range(NB):
                t = c.tile_tok(ap, b, tok, c.h, None, c.bank[2 + b][:, 0:S], c.hb[2 + b], release=b == 1)
                t = c.dve(lambda e, b=b: e.tensor_copy(tok_dst[:, b, :], c.bank[2 + b][:, 0:S]), t)
                c.hb[2 + b].give(t)
                out.append(t)
            return out
        rf = both(F_H, to(fp[:, :, PAD:], ACT.Sigmoid), lf)
        ri = both(I_H, to(vp[:, :, PAD:]), vt)
        rg = c.project(lambda _, n: w3(G_H)(), 1, c.h, None, to(gT, ACT.Sigmoid))
        tk = c.dve(lambda e: e.tensor_scalar(kp[:, :, PAD:], fp[:, :, PAD:], -1.0, 1.0, ALU.mult, ALU.add), rf)
        tf = c.dve(lambda e: e.memset(fp[:, :, :].rearrange("p a (n t) -> p a n t", t=CHUNK)[:, :, :, 0:1], 0.0), tk, tz)
        a = c.act(lambda e: e.activation(lf2[:, :, :], lf[:, :, :], ACT.Abs), rf)
        a = c.act(lambda e: e.activation(lf2[:, :, :], lf2[:, :, :], ACT.Exp, scale=-1.0), a)
        a = c.act(lambda e: e.activation(lf2[:, :, :], lf2[:, :, :], ACT.Ln, bias=c.eps(1.0)), a)
        tl = c.dve(lambda e: e.scalar_tensor_tensor(out=lf[:, :, :].rearrange("p a b -> p (a b)"),
                                                    in0=lf[:, :, :].rearrange("p a b -> p (a b)"), scalar=0.0,
                                                    in1=lf2[:, :, :].rearrange("p a b -> p (a b)"),
                                                    op0=ALU.min, op1=ALU.subtract), a)
        ex = []
        for i, (m, dst) in enumerate((("chunk_upto", eU), ("chunk_after", eA))):
            t = c.mms([(c.bank[i][:, q * S + b * P:][:, 0:P], lf[:, b, q * P:(q + 1) * P], c.con(m), q + b == 0, True)
                       for q in range(2) for b in range(NB)], tl, c.hb[i])
            t = c.act(lambda e, i=i, dst=dst: e.activation(dst[:, :, :].rearrange("p a b -> p (a b)"), c.bank[i][:, :],
                                                           ACT.Exp), t)
            c.hb[i].give(t)
            ex.append(t)
        tkh = c.dve(lambda e: e.tensor_tensor(kh[:, :, :], kp[:, :, PAD:], eA[:, :, :], ALU.mult), ex, tk)
        tqs = c.dve(lambda e: e.tensor_tensor(eA[:, :, :], qT[:, :, :], eU[:, :, :], ALU.mult), tkh, rq, ex)

        def turn(e):
            for q in range(2):
                for b in range(NB):
                    i = e.transpose(c.bank[2][:, b * S + q * P:][:, 0:P], kh[:, q, b * P:(b + 1) * P], c.con("identity"))
            return i
        t = c.pe(turn, tkh, c.hb[2])
        tkt = c.act(lambda e: e.activation(kt[:, :, :].rearrange("p a b -> p (a b)"), c.bank[2][:, :], ACT.Copy), t)
        c.hb[2].give(tkt)
        th = []
        h_vx = [Hand(c) for _ in range(2)]
        for hd in range(4):
            for b in range(NB):
                i, R, q = b, slice(64 * (hd % 2), 64 * (hd % 2) + 64), hd // 2
                s = c.pool(lambda e, hd=hd, b=b, i=i: e.tensor_tensor(
                    vx[:, i, :, :], vt[:, b, hd * 64:(hd + 1) * 64].unsqueeze(1).to_broadcast([P, 8, 64]),
                    c.con("chunk_of")[:, 0:8].unsqueeze(2).to_broadcast([P, 8, 64]), ALU.mult), ri, h_vx[i])
                n = 2 + i
                t = c.mms([(c.bank[n][:, :], kt[:, b, q * P:(q + 1) * P], vx[:, i, :, :].rearrange("p n j -> p (n j)"),
                            True, True)], s, tkt, c.hb[n])
                h_vx[i].give(t)
                t = c.act(lambda e, R=R, q=q, b=b, n=n: e.activation(
                    Hc[R, q, 8 * b:8 * b + 8, :].rearrange("p n j -> p (n j)"), c.bank[n][R, :], ACT.Copy), t)
                c.hb[n].give(t)
                th.append(t)
        t = c.dve(lambda e: e.memset(St[:, :, 0, :], 0.0))
        ts = [t, t]
        for n in range(NCH - 1):
            ts = [c.dve(lambda e, q=q, n=n: e.scalar_tensor_tensor(
                out=St[:, q, n + 1, :], in0=St[:, q, n, :], scalar=eU[:, q, (n + 1) * CHUNK - 1:(n + 1) * CHUNK],
                in1=Hc[:, q, n, :], op0=ALU.mult, op1=ALU.add), ts[q], th, ex) for q in range(2)]
        ob = c.acc[:, 0:2, :]
        ty = c.mms([(ob[64 * hd:64 * hd + 64, q, n * CHUNK:(n + 1) * CHUNK], St[64 * hd:64 * hd + 64, q, n, :],
                     eA[64 * hd:64 * hd + 64, q, n * CHUNK:(n + 1) * CHUNK], True, True)
                    for q in range(2) for n in range(NCH) for hd in range(2)], ts, tqs)
        ab = c.acc[:, 2:4, :]
        h_ab, h_qp, h_pv = Hand(c), Hand(c), Hand(c)

        def distance(q_ready, vsh, first):
            t = c.mms([(ab[:, q, :], c.con("head_sum"), qp[:, q, :], q == 0, True) for q in range(2)], q_ready, h_ab)
            h_qp.give(t)
            if first:
                m = c.dve(lambda e: e.tensor_tensor(o[:, :, :], ab, vsh(), ALU.mult), t, ri)
                h_ab.give(m)
                return m
            m = c.dve(lambda e: e.tensor_tensor(pv_[:, :, :], ab, vsh(), ALU.mult), t, h_pv)
            h_ab.give(m)
            a = c.pool(lambda e: e.tensor_tensor(o[:, :, :], o[:, :, :], pv_[:, :, :], ALU.add), m, h_o)
            h_pv.give(a)
            return a
        h_o = Hand(c)
        t = c.pool(lambda e: e.tensor_tensor(qp[:, :, :], kp[:, :, PAD:], qT[:, :, :], ALU.mult), tk, rq)
        h_o.give(distance(t, lambda: vp[:, :, PAD:], True))
        tF = c.dve(lambda e: e.memset(F[:, :, :], 1.0), tf)
        h_F, h_pr = Hand(c), Hand(c)
        h_F.give(tF)
        c.flush()
        with c.repeat(CHUNK - 1) as dist:
            tF = c.dve(lambda e: e.tensor_tensor(F[:, :, :], F[:, :, :], fp[:, :, bass.ds(dist.cur * -1 + PAD, S)], ALU.mult), h_F)
            h_F.give(tF)
            t = c.dve(lambda e: e.tensor_tensor(pr[:, :, :], F[:, :, :], kp[:, :, bass.ds(dist.cur * -1 + (PAD - 1), S)], ALU.mult),
                      tF, h_pr)
            t = c.pool(lambda e: e.tensor_tensor(qp[:, :, :], pr[:, :, :], qT[:, :, :], ALU.mult), t, h_qp)
            h_pr.give(t)
            h_o.give(distance(t, lambda: vp[:, :, bass.ds(dist.cur * -1 + (PAD - 1), S)], False))
        c.barrier()
        t = c.dve(lambda e: e.tensor_tensor(o[:, :, :], o[:, :, :], ob, ALU.add), ty)
        t = c.act(lambda e: e.activation(pr[:, :, :], o[:, :, :], ACT.Square), t)
        t = c.mms([(ab[:, q, :], c.con("head_mean"), pr[:, q, :], q == 0, True) for q in range(2)], t)
        t = c.act(lambda e: e.activation(pr[:, :, :], ab, ACT.Sqrt, bias=c.eps(1e-6)), t)
        t = c.dve(lambda e: e.reciprocal(pr[:, :, :], pr[:, :, :]), t)
        t = c.dve(lambda e: e.tensor_tensor(pr[:, :, :], pr[:, :, :], gT[:, :, :], ALU.mult), t)
        for q in range(2):
            c.dve(lambda e, q=q: e.scalar_tensor_tensor(out=mix[:, 6 + q, :], in0=o[:, q, :],
                                                        scalar=c.col(("hgrn_norm_g_3", 0), q), in1=pr[:, q, :],
                                                        op0=ALU.mult, op1=ALU.mult), t)
        c.barrier()
        c.ctx = outer


def lay_unit(inputs, what):
    out = np.zeros((P, UNIT), np.float32)
    if what is None:
        return out
    kind, name, index, start = what
    if kind in ("side", "stack"):
        for n, x in enumerate(name):
            x = inputs[x][index]
            if kind == "stack":
                out.reshape(P, 2, D)[:x.shape[0], n] = x
            else:
                w = x.shape[1]
                out.reshape(P, KT, 256)[:, :, n * w:(n + 1) * w] = x.reshape(KT, P, w).transpose(1, 0, 2)
        return out
    w = inputs[name][index]
    if kind == "rows":
        part = w[start:start + 256]
        part = np.concatenate([part, np.zeros((256 - len(part), part.shape[1]), np.float32)])
    else:
        part = w[:, start:start + UNIT * P // w.shape[0]]
    k = part.shape[0] // P
    out.reshape(P, k, UNIT // k)[:, :, :part.shape[1]] = part.reshape(k, P, -1).transpose(1, 0, 2)
    return out


def feature_major(a):
    return np.ascontiguousarray(a.reshape(a.shape[0], -1, P).transpose(2, 1, 0))


def small_inputs(inputs):
    columns = np.concatenate([np.asarray(inputs[n][i]).reshape(-1, P) for n, i in VECTORS]).T
    wf = inputs["w_in"][:, :, F_FX:F_FX + HEADS].reshape(L1, KT, P, HEADS).transpose(2, 0, 1, 3)
    hot, mask = bucket_constants()
    w2 = inputs["nsa_cmp_w2_3"][0].reshape(2, 2, P, 64).transpose(2, 0, 1, 3)
    return {
        "bias_one_hot": hot,
        "bias_mask": mask,
        "bias_table": np.ascontiguousarray(inputs["rel_bias_3"].T),
        "cmp_w2": np.ascontiguousarray(w2),
        "conv_pw": np.ascontiguousarray(inputs["conv_pw_w_3"][0].reshape(2, P, 256).transpose(1, 0, 2)),
        "columns": np.ascontiguousarray(columns),
        "shape_constants": np.concatenate([np.asarray(MATS[n], np.float32) for n in CONS], axis=1),
        "w_forget": np.ascontiguousarray(wf.reshape(P, -1)),
        "b_forget_rows": np.ascontiguousarray(np.broadcast_to(inputs["b_forget"].reshape(1, -1), (P, L1 * HEADS))),
        "sgu_w_spatial": np.ascontiguousarray(inputs["sgu_w_sp_2"][0].transpose(2, 0, 1)),
        "sgu_b_spatial": inputs["sgu_b_sp_2"][0],
        "rwkv_w0_row": inputs["rwkv_w0_2"],
        "memory": feature_major(inputs["mem"][0]),
        "x": feature_major(inputs["x"][0]),
    }


def build(nc, small, blocks):
    aps = {n: nc.dram_tensor(f"in_{n}", a.shape, F32, kind="ExternalInput").ap() for n, a in small.items()}
    out = nc.dram_tensor("out", (P, KT, S), F32, kind="ExternalOutput").ap()
    with ExitStack() as ctx:
        c = Core(nc, ctx, aps)
        c.everyone_waits([c.load(c.h[:, :, :], aps["x"], name="x")])
        c.at["sync"].append(("raw", lambda e: c.stream()(e)))
        for b in blocks:
            b(c)
        c.pad_units()
        aps["weights"] = nc.dram_tensor("in_weights", (c.n_units, P, UNIT), F32, kind="ExternalInput").ap()
        t = c.load(out, c.h[:, :, :], c.now(), name="out")
        c.at["sync"].append(("wait", [t]))
        c.emit()
    return [w() for w in c.plan]


BLOCKS = [block1, block2, block3]


def kernel(**inputs):
    import concourse.bacc as bacc
    from concourse.bass_utils import run_bass_kernel_spmd

    nc = bacc.Bacc("TRN2", target_bir_lowering=False, num_devices=1)
    inputs = {k: np.asarray(v) for k, v in inputs.items()}
    small = small_inputs(inputs)
    plan = build(nc, small, BLOCKS)
    weights = np.stack([lay_unit(inputs, w) for w in plan])
    got = run_bass_kernel_spmd(nc, [{f"in_{n}": a for n, a in {**small, "weights": weights}.items()}], core_ids=[0]).results[0]["out"]
    return np.ascontiguousarray(got.transpose(2, 1, 0)).reshape(1, S, D)
```

```python
from contextlib import ExitStack, contextmanager

import numpy as np
import concourse.bass as bass
from concourse import mybir

F32 = mybir.dt.float32
F32R = mybir.dt.float32r
ALU = mybir.AluOpType
ACT = mybir.ActivationFunctionType
AX = mybir.AxisListType.X

P = 128
D = 1024
KT = D // P
S = 256
NB = S // P
DFF = 2816
RING = 3
TURN = 6
UNIT = 2048
CREDIT = 512


class Loop:

    def __init__(self, n, parent):
        self.n, self.parent, self.entry, self.stride, self.cur = n, parent, {}, {}, None


class Count:

    def __init__(self, sem, start=0):
        self.sem, self.off = sem, start


class Tok:

    def __init__(self, count, off, loop, back=0):
        self.count, self.off, self.loop, self.back = count, off, loop, back

    def value(self, inside):
        v, s, back = self.off, self.loop, self.back
        while s is not None:
            if s in inside:
                v = v + s.entry[self.count] + (s.cur - back) * s.stride[self.count]
            else:
                v = v + s.entry[self.count] + (s.n - 1) * s.stride[self.count]
            back, s = 0, s.parent
        return v


class Prog:

    ENGINES = ("tensor", "scalar", "vector", "gpsimd", "sync")

    def __init__(self, nc, ctx):
        self.nc, self.ctx = nc, ctx
        self.queues = {e: [] for e in self.ENGINES}
        self.at = {e: self.queues[e] for e in self.ENGINES}
        self.counts, self.hands, self.loop = [], [], None
        self.low = self.count("s_units_split", CREDIT)
        self.main = {e: self.count(f"s_{e}", CREDIT) for e in self.ENGINES[:4]}

    def count(self, name, start=0):
        c = Count(self.ctx.enter_context(self.nc.semaphore(name)), start)
        self.counts.append(c)
        return c

    def op(self, engine, fn, *waits, count=None, inc=1):
        c = count or self.main[engine]
        c.off += inc
        self.at[engine].append(("op", fn, flat(waits), c, inc))
        return Tok(c, c.off, self.loop)

    def pe(self, fn, *w):
        return self.op("tensor", fn, *w)

    def mms(self, calls, *w):
        def fn(e):
            for out, x, y, start, stop in calls:
                if isinstance(x, Pair):
                    e.matmul(out, x.hi, y.hi, start=start, stop=False, skip_group_check=True)
                    e.matmul(out, x.hi, y.lo, start=False, stop=False, skip_group_check=True)
                    last = e.matmul(out, x.lo, y.hi, start=False, stop=stop, skip_group_check=True)
                else:
                    last = e.matmul(out, x, y, start=start, stop=stop, skip_group_check=True)
            return last

        return self.op("tensor", fn, *w)

    def act(self, fn, *w):
        return self.op("scalar", fn, *w)

    def dve(self, fn, *w):
        return self.op("vector", fn, *w)

    def pool(self, fn, *w):
        return self.op("gpsimd", fn, *w)

    def load(self, out, in_, *w, engine="sync", name="ld"):
        c = self.count(f"d_{name}_{len(self.counts)}")
        return self.op(engine, lambda e: e.dma_start(out, in_), *w, count=c, inc=16)

    def now(self):
        return [Tok(c, c.off, self.loop) for c in self.main.values()]

    def barrier(self):
        w = self.now()
        for e in self.ENGINES[:4]:
            self.at[e].append(("wait", w))

    @contextmanager
    def repeat(self, n):
        loop = Loop(n, self.loop)
        saved = dict(self.at)
        for e in self.ENGINES:
            body = []
            self.at[e].append(("loop", loop, body))
            self.at[e] = body
        for c in self.counts:
            loop.entry[c], c.off = c.off, 0
        self.loop = loop
        yield loop
        for h in self.hands:
            h.close(loop)
        for c in self.counts:
            if c not in loop.entry:
                loop.entry[c] = 0
            loop.stride[c] = c.off
            c.off = loop.entry[c] + n * c.off
        self.loop = loop.parent
        self.at = saved

    def emit(self):
        block = self.ctx.enter_context(self.nc.Block())
        for name in self.ENGINES:
            enter = {"tensor": block.tensor, "scalar": block.scalar, "vector": block.vector,
                        "gpsimd": block.gpsimd, "sync": block.sync}[name]

            def body(eng, name=name):
                if name in self.main:
                    eng.sem_inc(self.main[name].sem, CREDIT)
                if name == "vector":
                    eng.sem_inc(self.low.sem, CREDIT)
                self.walk(eng, self.queues[name], [])

            enter(body)

    def walk(self, eng, nodes, inside):
        seen = {}

        def wait(t):
            if t.count.off == 0 and t.off == 0:
                return
            key = (t.count, t.loop, t.back)
            if seen.get(key, -1) >= t.off:
                return
            seen[key] = t.off
            eng.wait_ge(t.count.sem, t.value(inside))

        for node in nodes:
            if node[0] == "wait":
                for t in latest(node[1]):
                    wait(t)
            elif node[0] == "raw":
                node[1](eng)
            elif node[0] == "op":
                _, fn, waits, c, inc = node
                for t in latest(waits):
                    wait(t)
                fn(eng).then_inc(c.sem, inc)
            else:
                _, loop, body = node
                if has_ops(body):
                    with eng.Fori(0, loop.n) as i:
                        loop.cur = i
                        self.walk(eng, body, inside + [loop])
                    loop.cur = None


class Pair:

    def __init__(self, hi, lo):
        self.hi, self.lo = hi, lo

    def __getitem__(self, i):
        return Pair(self.hi[i], self.lo[i])

    def rearrange(self, *a, **k):
        return Pair(self.hi.rearrange(*a, **k), self.lo.rearrange(*a, **k))


def has_ops(nodes):
    return any(n[0] in ("op", "wait") or has_ops(n[2]) for n in nodes)


def flat(ws):
    out = []
    for w in ws:
        if isinstance(w, (list, tuple)):
            out += flat(w)
        elif isinstance(w, Hand):
            out += w.take()
        elif w is not None:
            out.append(w)
    return out


def latest(waits):
    best = {}
    for t in waits:
        if isinstance(t, Later):
            for u in t.toks:
                k = (u.count, u.loop, u.back)
                if k not in best or best[k].off < u.off:
                    best[k] = u
            continue
        k = (t.count, t.loop, t.back)
        if k not in best or best[k].off < t.off:
            best[k] = t
    return list(best.values())


class Later:

    def __init__(self):
        self.toks = []


class Hand:

    def __init__(self, prog):
        self.prog, self.toks, self.open = prog, [], []
        prog.hands.append(self)

    def take(self):
        loop, out = self.prog.loop, list(self.toks)
        if loop is not None and not any(t.loop is loop for t in self.toks):
            later = Later()
            self.open.append((loop, later))
            out.append(later)
        return out

    def give(self, *toks):
        self.toks = flat(toks)
        return self.toks

    def close(self, loop):
        for l, later in self.open:
            if l is loop:
                later.toks = [Tok(t.count, t.off, t.loop, 1) for t in self.toks if t.loop is loop]
        self.open = [(l, x) for l, x in self.open if l is not loop]


def shape_constants():
    r = np.arange(P)
    row, colm = r[:, None], r[None, :]
    one = np.ones((P, P))
    chunk = row // 16 == colm // 16
    mats = {
        "identity": row == colm,
        "mean": one / D,
        "mean_half": one / (2 * D),
        "after": row > colm,
        "ones": one,
        "mean_256": one / 256,
        "upto": row <= colm,
        "before": row < colm,
        "not_before": np.where(row < colm, -1e30, 0),
        "head_sum": row // 64 == colm // 64,
        "head_mean": (row // 64 == colm // 64) / 64,
        "chunk_of": row // 16 == colm,
        "chunk_upto": chunk & (row <= colm),
        "chunk_before": chunk & (row < colm),
        "chunk_after": chunk & (row > colm),
        "chunk_all": chunk,
        "identity_pair": row % 64 == colm,
        "flip": row + colm == P - 1,
    }
    return mats


MATS = shape_constants()
CONS = list(MATS)

EPS = [1e-6, 1e-5, 4e-5, 64e-5, 1.0]

def vectors():
    out = []
    for l in range(2):
        out += [("ffn1_pre_g", l), ("ffn1_post_g", l), ("mix_pre_g", l), ("mix_post_g", l), ("b_gate", l),
                ("ffn2_pre_g", l), ("ffn2_post_g", l)]
    out += [("mem_norm_g", ())]
    out += [(f"ln_{x}_2", (i, j)) for i in range(2) for j in range(3) for x in "gb"]
    out += [(n, 0) for n in ("sgu_b_in_2", "sgu_ln_g_2", "sgu_ln_b_2")]
    out += [("rwkv_mu_2", (0, j)) for j in range(6)]
    out += [(f"rwkv_{n}_2", 0) for n in ("w0", "a0", "k_k", "k_a", "r_k", "gn_g", "gn_b")]
    out += [("conv_dw_w_3", (0, j)) for j in range(31)]
    out += [(n, 0) for n in ("conv_dw_b_3", "conv_ln_g_3", "conv_ln_b_3", "hgrn_norm_g_3", "ln1_g_3", "ln1_b_3",
                             "ln2_g_3", "ln2_b_3")]
    out += [("nsa_cmp_b1_3", (0, j)) for j in range(2)]
    out += [("nsa_cmp_pe_3", (0, j)) for j in range(2)]
    return out


SIZES = {"b_gate": 3072, "sgu_b_in_2": 4096, "sgu_ln_g_2": 2048, "sgu_ln_b_2": 2048, "conv_dw_w_3": 256,
         "conv_dw_b_3": 256, "conv_ln_g_3": 256, "conv_ln_b_3": 256, "hgrn_norm_g_3": 256, "nsa_cmp_b1_3": 256,
         "nsa_cmp_pe_3": 2048}
VECTORS = vectors()
COLS, N_COLS = {}, 0
for _name, _index in VECTORS:
    COLS[_name, _index] = N_COLS
    N_COLS += SIZES.get(_name, D) // P
COLS["mem_norm_g"] = COLS["mem_norm_g", ()]


class Core(Prog):

    def __init__(self, nc, ctx, aps):
        super().__init__(nc, ctx)
        self.aps = aps
        self.plan, self.n_units = [], 0
        self.slot = [self.count(f"s_weight_slot{k}") for k in range(RING)]
        self.ring = self.sb("weight_ring", [P, RING, UNIT])
        self.w = Pair(*(self.sb(f"weights_{x}", [P, 2, UNIT], F32R) for x in ("hi", "lo")))
        self.w_ready = [Hand(self) for _ in range(2)]
        self.w_read = [Hand(self) for _ in range(2)]
        self.n_split, self.held = 0, False
        self.bank = [self.ps(f"bank{i}", [P, 512]) for i in range(4)]
        self.acc = self.ps("acc", [P, KT, S])
        self.hb = [Hand(self) for _ in range(4)]
        self.h = self.sb("h", [P, KT, S])
        self.xn = self.sb("xn", [P, KT, S])
        self.tmp = self.sb("tmp", [P, KT, S])
        self.rstd = self.sb("rstd", [P, S])
        self.act_gate = self.sb("act_gate", [P, 2, S])
        self.hidden = self.sb("hidden", [P, 2, S])
        self.h_gate = [Hand(self) for _ in range(2)]
        self.h_tmp = [Hand(self) for _ in range(KT)]
        self.cons = self.sb("cons", [P, len(CONS) * P])
        self.pv = self.sb("pv", [P, N_COLS])
        self.epsc = self.sb("epsc", [P, len(EPS)])
        start = [self.load(self.cons[:, :], aps["shape_constants"], name="cons"),
                 self.load(self.pv[:, :], aps["columns"], engine="scalar", name="pv")]
        start += [self.pool(lambda e, i=i, v=v: e.memset(self.epsc[:, i:i + 1], v)) for i, v in enumerate(EPS)]
        self.everyone_waits(start)

    def everyone_waits(self, toks):
        for e in self.ENGINES[:4]:
            self.at[e].append(("wait", toks))

    def sb(self, name, shape, dt=F32):
        return self.ctx.enter_context(self.nc.sbuf_tensor(name, shape, dt))

    def ps(self, name, shape):
        return self.ctx.enter_context(self.nc.psum_tensor(name, shape, F32))

    def con(self, name):
        i = CONS.index(name)
        return self.cons[:, i * P:(i + 1) * P]

    def col(self, name, k=0, n=1):
        c = COLS[name] + k
        return self.pv[:, c:c + n]

    def eps(self, v):
        i = EPS.index(v)
        return self.epsc[:, i:i + 1]

    def unit(self, what, a=KT, last=False):
        assert not self.held
        self.held = True
        while self.n_split < self.n_units + (1 if last else 2):
            self.split_unit()
        j = self.n_units % 2
        self.n_units += 1
        self.plan.append(what)
        return self.w[:, j, :].rearrange("p (a b) -> p a b", a=a), self.w_ready[j].take()

    def split_unit(self):
        k, j = self.n_split % RING, self.n_split % 2
        self.n_split += 1
        self.slot[k].off += 16
        arrived = Tok(self.slot[k], self.slot[k].off, self.loop)
        w, raw = self.w[:, j, :], self.ring[:, k, :]
        hi = self.act(lambda e: e.activation(w.hi, raw, ACT.Copy), arrived, self.w_read[j])
        lo = self.op("vector", lambda e: e.tensor_tensor(w.lo, raw, w.hi, ALU.subtract), hi, count=self.low)
        self.w_ready[j].give(lo)

    def mms(self, calls, *w, release=False):
        t = super().mms(calls, *w)
        if release:
            self.w_read[(self.n_units - 1) % 2].give(t)
            self.held = False
        return t

    @contextmanager
    def repeat(self, n):
        while self.n_split <= self.n_units:
            self.split_unit()
        plan, self.plan = self.plan, []
        first, ahead = self.n_units, self.n_split - self.n_units
        with super().repeat(n) as loop:
            yield loop
        body = self.plan
        assert len(body) % TURN == 0 and self.n_split - self.n_units == ahead, (len(body), ahead)
        self.n_units = first + n * len(body)
        self.n_split = self.n_units + ahead
        self.plan = plan + [(lambda *o, i=i, w=w: w(*o, i)) for i in range(n) for w in body]

    def pad_units(self, start=0, end=False):
        while (self.n_units - start) % TURN or end:
            last = end and (self.n_units - start) % TURN == TURN - 1
            ap, tok = self.unit(lambda *_: None, last=last)
            t = self.mms([(self.bank[0][:, 0:8], ap[:, 0, 0:P], ap[:, 0, 0:8], True, True)],
                         tok, self.hb[0], release=True)
            self.hb[0].give(t)
            if last:
                break

    def stream(self):
        w, slots = self.aps["weights"], [(self.ring[:, k, :], self.slot[k].sem) for k in range(RING)]

        def run(e):
            for k in range(RING):
                e.dma_start(slots[k][0], w[k]).then_inc(slots[k][1], 16)
            with e.Fori(1, self.n_units // RING) as turn:
                for k in range(RING):
                    e.wait_ge(self.low.sem, (turn - 1) * RING + (CREDIT + k + 1))
                    e.dma_start(slots[k][0], w[turn * RING + k]).then_inc(slots[k][1], 16)
        return run

    def operands(self, of, hidden=2):
        self.x = Pair(*(self.sb(f"{of}_x_{n}", [P, KT, S], F32R) for n in ("hi", "lo")))
        self.hid = Pair(*(self.sb(f"{of}_hidden_{n}", [P, hidden, 2, S], F32R) for n in ("hi", "lo")))
        self.h_hid = [[Hand(self) for _ in range(2)] for _ in range(hidden)]

    @contextmanager
    def scope(self):
        with ExitStack() as own:
            outer, self.ctx = self.ctx, own
            yield
            self.ctx = outer

    def split(self, src, dst, ready, n=KT, step=2, free=None):
        out = []
        for i, k in enumerate(range(0, n, step)):
            s, d = src[:, k:k + step, :], dst[:, k:k + step, :]
            r = ready[k:k + step] if isinstance(ready, list) and len(ready) == n else ready
            hi = self.act(lambda e, s=s, d=d: e.activation(d.hi, s, ACT.Copy), r, free)
            out += [(self.pool if i % 3 == 2 else self.dve)(
                lambda e, s=s, d=d: e.tensor_tensor(d.lo, s, d.hi, ALU.subtract), hi)] * step
        return out

    def tile_T(self, ap, c, tok, src, ready, out, w, kt=KT, release=False):
        if isinstance(ready, list) and len(ready) == kt:
            for k in range(kt):
                t = self.mms([(out, ap[:, k, c * P:(c + 1) * P], src[:, k, :], k == 0, k == kt - 1)],
                             tok, ready[k], w if k == 0 else None, release=release and k == kt - 1)
            return t
        return self.mms([(out, ap[:, k, c * P:(c + 1) * P], src[:, k, :], k == 0, k == kt - 1)
                         for k in range(kt)], tok, ready, w, release=release)

    def tile_tok(self, ap, b, tok, src, ready, out, w, width=256, release=False):
        return self.mms([(out, src[:, k, b * P:(b + 1) * P], ap[:, k, 0:width], k == 0, k == KT - 1)
                         for k in range(KT)], tok, ready, w, release=release)

    def ffn(self, gate, up, down, ready):
        depth, p = 0, self.loop
        while p is not None:
            depth, p = depth + 1, p.parent

        def make(j, par):
            g, tg = self.unit(lambda *i: gate(i[:depth], j(*i[depth:])))
            for c in range(2):
                t = self.tile_T(g, c, tg, self.x, ready, self.bank[c][:, 0:S], self.hb[c], release=c == 1)
                s = self.act(lambda e, c=c: e.activation(self.act_gate[:, c, :], self.bank[c][:, 0:S], ACT.Silu),
                             t, self.h_gate[c])
                self.hb[c].give(s), self.h_gate[c].give(s)
            u, tu = self.unit(lambda *i: up(i[:depth], j(*i[depth:])))
            for c in range(2):
                t = self.tile_T(u, c, tu, self.x, ready, self.bank[2 + c][:, 0:S], self.hb[2 + c], release=c == 1)
                m = self.dve(lambda e, c=c: e.tensor_tensor(self.act_gate[:, c, :], self.bank[2 + c][:, 0:S],
                                                            self.act_gate[:, c, :], ALU.mult), t, self.h_gate[c])
                self.hb[2 + c].give(m)
                self.hidden_parts(self.act_gate, par, c, m)

        def use(j, par, first=False):
            d, td = self.unit(lambda *i: down(i[:depth], j(*i[depth:])), a=2)
            return self.add_down(d, td, par, first)

        make(lambda: 0, 0)
        make(lambda: 1, 1)
        use(lambda: 0, 0, first=True)
        make(lambda: 2, 0)
        use(lambda: 1, 1)
        with self.repeat(4):
            make(lambda i: 3 + 2 * i, 1)
            use(lambda i: 2 + 2 * i, 0)
            make(lambda i: 4 + 2 * i, 0)
            use(lambda i: 3 + 2 * i, 1)
        return use(lambda: 10, 0)

    def hidden_parts(self, src, par, c, ready):
        d = self.hid[:, par, c, :]
        hi = self.act(lambda e: e.activation(d.hi, src[:, c, :], ACT.Copy), ready, self.h_hid[par][c])
        lo = self.dve(lambda e: e.tensor_tensor(d.lo, src[:, c, :], d.hi, ALU.subtract), hi)
        self.h_gate[c].give(lo), self.h_hid[par][c].give(lo)

    def add_down(self, d, td, par, first):
        for c in range(2):
            t = self.mms([(self.acc[:, m, :], d[:, c, m * P:(m + 1) * P], self.hid[:, par, c, :],
                           first and c == 0 and m % 2 == 0, False) for m in range(KT)],
                         td, self.h_hid[par][c], release=c == 1)
            self.h_hid[par][c].give(t)
        return t

    def inv_sqrt(self, ps, eps, ready, scale=1.0):
        s = self.act(lambda e: e.activation(self.rstd[:, :], ps, ACT.Sqrt, bias=self.eps(eps)), ready)
        self.hb[0].give(s)
        r = self.dve(lambda e: e.reciprocal(self.rstd[:, :], self.rstd[:, :]), s)
        if scale != 1.0:
            r = self.dve(lambda e: e.tensor_scalar(self.rstd[:, :], self.rstd[:, :], scale, None, ALU.mult), r)
        return r

    def mean_sq(self, src, kt, ready, sq, mat="mean"):
        hands = self.h_tmp if sq is self.tmp else None
        for k in range(0, kt, 2):
            s = self.act(lambda e, k=k: e.activation(sq[:, k:k + 2, :], src[:, k:k + 2, :], ACT.Square),
                         ready[k:k + 2], hands[k:k + 2] if hands else None)
            t = self.mms([(self.bank[0][:, 0:S], self.con(mat), sq[:, j, :], j == 0, j == kt - 1)
                          for j in (k, k + 1)], s, self.hb[0] if k == 0 else None)
            if hands:
                hands[k].give(t), hands[k + 1].give(t)
        return t

    def rms_norm(self, src, gain, dst, ready):
        t = self.mean_sq(src, KT, ready, self.tmp)
        r = self.inv_sqrt(self.bank[0][:, 0:S], 1e-6, t)
        return [self.dve(lambda e, k=k: e.scalar_tensor_tensor(
            out=dst[:, k, :], in0=src[:, k, :], scalar=gain(k), in1=self.rstd[:, :],
            op0=ALU.mult, op1=ALU.mult), r) for k in range(KT)]

    def add_rms(self, gain, ready, scale):
        t = self.mean_sq(self.acc, KT, [ready] * KT, self.tmp)
        r = self.inv_sqrt(self.bank[0][:, 0:S], 1e-6, t, scale)
        out = []
        for k in range(KT):
            t = self.dve(lambda e, k=k: e.scalar_tensor_tensor(
                out=self.tmp[:, k, :], in0=self.acc[:, k, :], scalar=gain(k), in1=self.rstd[:, :],
                op0=ALU.mult, op1=ALU.mult), r, self.h_tmp[k])
            out.append((self.pool if k % 3 == 1 else self.dve)(
                lambda e, k=k: e.tensor_tensor(self.h[:, k, :], self.h[:, k, :], self.tmp[:, k, :], ALU.add), t))
            self.h_tmp[k].give(out[-1])
        return out

    def layer_norm(self, src, kt, gain, bias, dst, ready, sq, mat="mean", eps=1e-5):
        for j in range(kt):
            t = self.mms([(self.bank[1][:, 0:S], self.con(mat), src[:, j, :], j == 0, j == kt - 1)],
                         ready[j], self.hb[1] if j == 0 else None)
        centred = [self.dve(lambda e, k=k: e.tensor_tensor(src[:, k, :], src[:, k, :], self.bank[1][:, 0:S],
                                                           ALU.subtract), t) for k in range(kt)]
        self.hb[1].give(centred[-1])
        t = self.mean_sq(src, kt, centred, sq, mat)
        r, out = self.inv_sqrt(self.bank[0][:, 0:S], eps, t), []
        for k in range(kt):
            t = self.dve(lambda e, k=k: e.scalar_tensor_tensor(
                out=src[:, k, :], in0=src[:, k, :], scalar=gain(k), in1=self.rstd[:, :],
                op0=ALU.mult, op1=ALU.mult), r)
            out.append(self.act(lambda e, k=k: e.activation(dst[:, k, :], src[:, k, :], ACT.Identity, bias=bias(k)), t))
        return out

    def evac_heads(self, ps, q, t, scale, ready, free):
        a = self.act(lambda e: e.activation(q[:, 2 * t, :], ps[0:64, 0:S], ACT.Copy, scale=scale), ready)
        b = self.dve(lambda e: e.tensor_scalar(q[:, 2 * t + 1, :], ps[64:128, 0:S], scale, None, ALU.mult), ready)
        free.give(a, b)
        return [a, b]

    def project(self, what, n_units, ready, take, src=None):
        src = src or self.x
        out = []
        for n in range(n_units):
            ap, tok = self.unit(lambda *i, n=n: what(i, n))
            for c in range(2):
                b = (2 * n + c) % 4
                t = self.tile_T(ap, c, tok, src, ready, self.bank[b][:, 0:S], self.hb[b], release=c == 1)
                out.append(take(2 * n + c, self.bank[b], t, self.hb[b]))
        return out

    def project_tok(self, what, n_units, ready, dst):
        src = self.x
        out = []
        for n in range(n_units):
            ap, tok = self.unit(lambda *i, n=n: what(i, n))
            for c in range(NB):
                b = (2 * n + c) % 4
                t = self.tile_tok(ap, c, tok, src, ready, self.bank[b][:, 0:S], self.hb[b], release=c == 1)
                d = dst[:, c, n * 256:(n + 1) * 256]
                t = (self.act(lambda e, b=b, d=d: e.activation(d, self.bank[b][:, 0:S], ACT.Copy), t) if c else
                     self.dve(lambda e, b=b, d=d: e.tensor_copy(d, self.bank[b][:, 0:S]), t))
                self.hb[b].give(t)
                out.append(t)
        return out

    def attention_buffers(self, of):
        self.wq = self.sb(f"{of}_att_w_by_query", [P, 2, 2, 512])
        self.wk = self.sb(f"{of}_att_w_by_key", [P, 2, 2, 512])
        self.stat = self.sb(f"{of}_att_stats", [P, 2, 3, 2, NB])
        self.h_wq = [Hand(self) for _ in range(2)]
        self.h_wk = [Hand(self) for _ in range(2)]
        self.h_pt2 = [Hand(self) for _ in range(2)]
        self.h_o = [Hand(self) for _ in range(2)]
        self.turn = 0
        self.h_z = [Hand(self) for _ in range(2)]

    def softmax_pair(self, scores, causal, norm=None, ready=()):
        side = self.turn % 2
        self.turn += 1
        z, wq, wk, st = self.bank[2 * side:2 * side + 2], self.wq[:, side], self.wk[:, side], self.stat[:, side]
        span = [(0, 128), (128, 256)] if causal else [(0, 256), (256, 256)]
        hands = self.hb[2 * side:2 * side + 2]
        normed, done = [], []
        for hd in range(2):
            for qb, (at, n) in enumerate(span):
                last = self.mms(scores(hd, qb, z[hd][:, at:at + n]), hands[hd] if qb == 0 else None, ready)
            mx = [self.dve(lambda e, hd=hd, qb=qb, at=at, n=n: e.tensor_reduce(
                st[:, 0, hd, qb:qb + 1], z[hd][:, at:at + n], AX, ALU.max, negate=True), last,
                self.h_wq[side] if hd + qb == 0 else None) for qb, (at, n) in enumerate(span)]
            ex = [self.act(lambda e, hd=hd, qb=qb, at=at, n=n: e.activation(
                wq[:, hd, at:at + n], z[hd][:, at:at + n], ACT.Exp, bias=st[:, 0, hd, qb:qb + 1],
                accum_out=st[:, 1, hd, qb:qb + 1]), mx) for qb, (at, n) in enumerate(span)]
            hands[hd].give(ex)
            r = self.dve(lambda e, hd=hd: e.reciprocal(st[:, 2, hd, :], st[:, 1, hd, :]), ex)
            if norm is not None:
                for qb in range(NB):
                    r = self.dve(lambda e, hd=hd, qb=qb: e.tensor_tensor(
                        st[:, 2, hd, qb:qb + 1], st[:, 2, hd, qb:qb + 1], norm(hd, qb), ALU.mult), r)
            nrm = [self.dve(lambda e, hd=hd, qb=qb, at=at, n=n: e.tensor_scalar(
                wq[:, hd, at:at + n], wq[:, hd, at:at + n], st[:, 2, hd, qb:qb + 1], None, ALU.mult), r)
                for qb, (at, n) in enumerate(span)]
            normed.append(nrm)
        yield
        for hd in range(2):
            blocks = [(0, 0), (1, 0), (1, 1)] if causal else [(0, 0), (1, 0), (0, 1), (1, 1)]
            pt = self.acc[:, 2 * hd:2 * hd + 2, :].rearrange("p a b -> p (a b)")

            def turn(e, hd=hd, pt=pt):
                for qb, kb in blocks:
                    i = e.transpose(pt[:, self.kcol(qb, kb, causal):][:, 0:P],
                                    wq[:, hd, span[qb][0] + kb * P:][:, 0:P], self.con("identity"))
                return i
            tr = self.pe(turn, normed[hd], self.h_pt2[hd])
            w = 128 * len(blocks)
            if hd:
                cp = self.act(lambda e, hd=hd, pt=pt: e.activation(wk[:, hd, 0:w], pt[:, 0:w], ACT.Copy), tr,
                              self.h_wk[side])
            else:
                cp = self.dve(lambda e, hd=hd, pt=pt: e.tensor_copy(wk[:, hd, 0:w], pt[:, 0:w]), tr, self.h_wk[side])
            self.h_pt2[hd].give(cp)
            done.append(cp)
            trl = tr
        self.h_wq[side].give(trl)
        return side, done

    @staticmethod
    def kcol(qb, kb, causal):
        return (kb * 256 + qb * 128) if not (causal and kb == 1) else 256

    def values_pair(self, side, ready, parts, causal, width, take, first=True, last=True):
        ob = self.acc[:, 4:6, :]
        for hd in range(2):
            calls = []
            for kb in range(NB):
                q0 = 128 if causal and kb == 1 else 0
                w = self.wk[:, side, hd, kb * 256:kb * 256 + 256 - q0]
                calls.append((ob[0:width, hd, q0:256], parts(hd, kb), w, first and kb == 0, last and kb == 1))
            t = self.mms(calls, ready, self.h_o[0] if first and hd == 0 else None)
        self.h_wk[side].give(t)
        if last:
            t = take(ob, t)
            self.h_o[0].give(t)
        return t


def finish(stages):
    while True:
        try:
            next(stages)
        except StopIteration as e:
            return e.value


def stagger(steps, others=()):
    n, done, others = len(steps), [], list(others)
    per = -(-len(others) // n)
    for i in range(n + 2):
        now = others[per * i:per * (i + 1)]
        if i < n:
            next(steps[i])
        for x in now[:-1]:
            finish(x)
        if now:
            next(now[-1])
        if 0 <= i - 1 < n:
            next(steps[i - 1])
        if now:
            finish(now[-1])
        if 0 <= i - 2 < n:
            done.append(finish(steps[i - 2]))
    return done


L1 = 2
HEADS, HD = 8, 64
Q_SB, K_SB, V_SB, Q_FX, K_FX, V_FX, F_FX, Q_MEM = 0, 512, 1024, 1536, 2048, 2560, 3072, 3080
LAYER_COLS = {"ffn1_pre_g": 0, "ffn1_post_g": 8, "mix_pre_g": 16, "mix_post_g": 24, "b_gate": 32,
              "ffn2_pre_g": 56, "ffn2_post_g": 64}
N_LAYER_COLS = 72


def block1(c):
    with ExitStack() as own:
        outer, c.ctx = c.ctx, own
        lp = c.sb("layer_params", [P, N_LAYER_COLS])
        wf, bf = c.sb("w_forget", [P, L1 * KT * HEADS]), c.sb("b_forget", [P, L1 * HEADS])
        wfl, bfl = c.sb("w_forget_layer", [P, KT * HEADS]), c.sb("b_forget_layer", [P, HEADS])
        memn = c.sb("mem_norm", [P, KT, S])
        qa, ka = c.sb("q", [P, HEADS, S]), c.sb("k", [P, HEADS, S])
        qh, kh = qa[0:64], ka[0:64]
        qmem, kmem = qa[:, 0:4], ka[:, 0:4]
        vh = c.sb("v_tokens", [P, NB, 512])
        oT = c.sb("branch_out", [P, 4, S])
        ox = Pair(*(c.sb(f"branch_out_{n}", [P, 4, S], F32R) for n in ("hi", "lo")))
        merged = c.xn
        lf, lf2 = c.sb("log_forget", [P, NB, HEADS]), c.sb("log_forget_t", [P, NB, HEADS])
        cT, ncT = c.sb("cum_forget", [HEADS, S]), c.sb("neg_cum_forget", [HEADS, S])
        zt = [c.sb(f"sb_{n}", [P, 2, 2, 384]) for n in ("abs", "softplus", "log_not")]
        c.attention_buffers("b1")
        c.operands("b1")
        t = [c.load(wf[:, :], c.aps["w_forget"], engine="scalar", name="wf"),
             c.load(bf[:, :], c.aps["b_forget_rows"], engine="scalar", name="bf"),
             c.load(memn[:, :, :], c.aps["memory"], engine="scalar", name="mem")]
        ident = c.con("identity")

        c.rms_norm(memn, lambda k: c.col("mem_norm_g", k), memn, [t] * KT)

        with c.repeat(L1) as layer:
            body_start = c.n_units
            g = lambda name: (lambda k: lp[:, LAYER_COLS[name] + k:LAYER_COLS[name] + k + 1])
            tl = [c.dve(lambda e, to=to, of=of, n=n: e.tensor_copy(to[:, :], of[:, bass.ts(layer.cur, n)]))
                  for to, of, n in ((lp, c.pv, N_LAYER_COLS), (wfl, wf, KT * HEADS), (bfl, bf, HEADS))]

            def ffn(n, ready, before_add=None):
                t = c.rms_norm(c.h, g(f"ffn{n}_pre_g"), c.xn, ready)
                t = c.split(c.xn, c.x, t)
                t = c.ffn(lambda i, j: ("cols", f"ffn{n}_w_gate", i, j * 256),
                          lambda i, j: ("cols", f"ffn{n}_w_up", i, j * 256),
                          lambda i, j: ("rows", f"ffn{n}_w_down", i, j * 256), t)
                other = before_add(t) if before_add else None
                return c.add_rms(g(f"ffn{n}_post_g"), t, 0.5), other

            t_h, t_mem = ffn(1, [tl] * KT, lambda t: c.split(memn, c.x, t))
            w = lambda name, start: (lambda i, n: ("cols", name, i, start + n * 256))

            def take128(dst, sc):
                def take(t, ps, ready, free):
                    x = c.act(lambda e: e.activation(dst[:, t, :], ps[:, 0:S], ACT.Copy, scale=sc), ready)
                    free.give(x)
                    return x
                return take
            r = [c.project(w("w_mem_kv", 0), 2, t_mem, take128(kmem, 1.0)),
                 c.project_tok(w("w_mem_kv", 512), 2, t_mem, vh)]
            t = c.rms_norm(c.h, g("mix_pre_g"), c.xn, t_h)
            x_read = Hand(c)
            x_read.give(r)
            u = c.split(c.xn, c.x, t, free=x_read)

            for b in range(NB):
                t = c.mms([(c.bank[b][:, 0:HEADS], c.xn[:, k, b * P:(b + 1) * P], wfl[:, k * HEADS:(k + 1) * HEADS],
                            k == 0, k == KT - 1) for k in range(KT)], u, tl, c.hb[b])
                x, y = lf[:, b, :], lf2[:, b, :]
                t = c.dve(lambda e, b=b, x=x: e.tensor_tensor(x, c.bank[b][:, 0:HEADS], bfl[:, :], ALU.add), t)
                c.hb[b].give(t)
                a = c.act(lambda e, x=x, y=y: e.activation(y, x, ACT.Abs), t)
                a = c.act(lambda e, y=y: e.activation(y, y, ACT.Exp, scale=-1.0), a)
                a = c.act(lambda e, y=y: e.activation(y, y, ACT.Ln, bias=c.eps(1.0)), a)
                tlf = c.dve(lambda e, x=x, y=y: e.scalar_tensor_tensor(out=x, in0=x, scalar=0.0, in1=y, op0=ALU.min,
                                                                       op1=ALU.subtract), a)
            t = c.mms([(c.bank[0][0:HEADS, 0:128], lf[:, 0, :], c.con("upto"), True, True),
                       (c.bank[0][0:HEADS, 128:256], lf[:, 0, :], c.con("ones"), False, False),
                       (c.bank[0][0:HEADS, 128:256], lf[:, 1, :], c.con("upto"), False, True)], tlf, c.hb[0])
            a = c.dve(lambda e: e.tensor_copy(cT[:, :], c.bank[0][0:HEADS, 0:S]), t)
            t_cum = c.dve(lambda e: e.tensor_scalar(ncT[:, :], c.bank[0][0:HEADS, 0:S], -1.0, None, ALU.mult), a)
            c.hb[0].give(t_cum)

            def heads(q_at, k_at, v_at):
                sc = HD ** -0.5
                tq = c.project(w("w_in", q_at), 2, u, lambda t, ps, r, f: c.evac_heads(ps, qh, t, sc, r, f))
                tk = c.project(w("w_in", k_at), 2, u, lambda t, ps, r, f: c.evac_heads(ps, kh, t, 1.0, r, f))
                tv = c.project_tok(w("w_in", v_at), 2, u, vh)
                return [tq, tk, tv]

            def take_heads(pair):
                def take(ob, t):
                    a = c.act(lambda e: e.activation(oT[0:64, pair, :], ob[0:64, 0, :], ACT.Copy), t, h_oT)
                    b = c.dve(lambda e: e.tensor_copy(oT[64:128, pair, :], ob[0:64, 1, :]), a, h_oT)
                    return [a, b]
                return take

            vpart = lambda pair: (lambda hd, kb: vh[:, kb, (2 * pair + hd) * 64:(2 * pair + hd + 1) * 64])

            h_oT, h_bank7 = Hand(c), Hand(c)
            summed = [None] * KT

            def gates(br, n):
                wg, tg = c.unit(lambda *i: ("cols", "w_gate", i, br * D + n * 256))
                for q in range(2):
                    m = 2 * n + q
                    t = c.tile_T(wg, q, tg, c.x, u, c.acc[:, 6, :], h_bank7, release=q == 1)
                    t = c.act(lambda e, m=m: e.activation(c.tmp[:, m, :], c.acc[:, 6, :], ACT.Sigmoid,
                              bias=lp[:, LAYER_COLS["b_gate"] + br * 8 + m:][:, 0:1]), t, c.h_tmp[m])
                    h_bank7.give(t), c.h_tmp[m].give(t)
                    if q == 0:
                        yield

            def merge(name, o_ready, first=False):
                t_o = c.split(oT, ox, o_ready, n=4)
                h_oT.give(t_o)
                for half in range(2):
                    wb, tb = c.unit(lambda *i, half=half: ("cols", name, i, half * 512), a=4)
                    for pair in range(2):
                        bank = [c.h_pt2[0], c.h_pt2[1], c.h_o[0], h_bank7][2 * half + pair]
                        for n in (2 * pair, 2 * pair + 1):
                            m = 4 * half + n
                            t = c.mms([(c.acc[:, m, :], wb[:, k, n * P:(n + 1) * P], ox[:, k, :], k == 0, k == 3)
                                       for k in range(4)], tb, t_o, bank if n % 2 == 0 else None, release=n == 3)
                        for m in (m - 1, m):
                            dst = merged if first else c.tmp
                            v = c.dve(lambda e, m=m, dst=dst: e.tensor_tensor(
                                dst[:, m, :], c.acc[:, m, :], c.tmp[:, m, :], ALU.mult), t, c.h_tmp[m])
                            summed[m] = v
                            if not first:
                                summed[m] = c.pool(lambda e, m=m: e.tensor_tensor(
                                    merged[:, m, :], merged[:, m, :], c.tmp[:, m, :], ALU.add), v)
                            c.h_tmp[m].give(summed[m])
                        bank.give(v)

            r.append(c.project(w("w_in", Q_MEM), 2, u, take128(qmem, 128 ** -0.5)))
            def mem_pair(pair, r):
                scores = lambda hd, qb, z: [(z, qmem[:, 2 * pair + hd, qb * P:(qb + 1) * P], kmem[:, 2 * pair + hd, :],
                                             True, True)]
                side, tw = yield from c.softmax_pair(scores, False, ready=r)
                yield
                take = lambda ob, t: c.act(lambda e: e.activation(oT[:, 2 * pair:2 * pair + 2, :], ob, ACT.Copy), t,
                                           h_oT)
                return c.values_pair(side, [tw, r], lambda hd, kb: vh[:, kb, (2 * pair + hd) * P:(2 * pair + hd + 1) * P],
                                     False, P, take)
            done = stagger([mem_pair(p, r) for p in range(2)], [gates(2, n) for n in range(4)])
            merge("w_br_mem", done, first=True)

            r = heads(Q_SB, K_SB, V_SB)
            h_z = [[Hand(c) for _ in range(2)] for _ in range(2)]

            def scores_sb(pair, hd, r):
                side, wk = pair % 2, c.wk
                ab, sp, ln = (z[:, side] for z in zt)
                hh, zb, bt = 2 * pair + hd, c.bank[2 * side + hd], c.acc[:, 2 * hd:2 * hd + 2, :]
                bt = bt.rearrange("p a b -> p (a b)")
                tz = c.mms([(zb[:, 0:256], kh[:, hh, 0:128], qh[:, hh, :], True, True),
                            (zb[:, 256:384], kh[:, hh, 128:256], qh[:, hh, 128:256], True, True)],
                           r, c.hb[2 * side + hd])
                z = zb[:, 0:384]
                a = c.act(lambda e: e.activation(ab[:, hd, :], z, ACT.Abs), tz, h_z[side][hd])
                a = c.act(lambda e: e.activation(ab[:, hd, :], ab[:, hd, :], ACT.Exp, scale=-1.0), a)
                a = c.act(lambda e: e.activation(ab[:, hd, :], ab[:, hd, :], ACT.Ln, bias=c.eps(1.0)), a)
                s = c.dve(lambda e: e.scalar_tensor_tensor(out=sp[:, hd, :], in0=z, scalar=0.0, in1=ab[:, hd, :],
                                                           op0=ALU.max, op1=ALU.add), a)
                n = None
                for at, m in ((0, "before"), (128, "ones"), (256, "before")):
                    n = c.dve(lambda e, at=at, m=m: e.scalar_tensor_tensor(
                        out=ln[:, hd, at:at + P], in0=sp[:, hd, at:at + P], scalar=-1.0, in1=c.con(m),
                        op0=ALU.mult, op1=ALU.mult), s)
                lb = c.dve(lambda e: e.tensor_tensor(sp[:, hd, :], z, sp[:, hd, :], ALU.subtract), n)
                c.hb[2 * side + hd].give(lb)
                yield
                later, ones = c.con("after"), c.con("ones")
                tb = c.mms([(bt[:, 0:256], later, ln[:, hd, 0:256], True, False),
                            (bt[:, 128:256], ones, ln[:, hd, 256:384], False, True),
                            (bt[:, 256:384], later, ln[:, hd, 256:384], False, True)],
                           n, c.h_pt2[hd])
                x = c.dve(lambda e: e.tensor_tensor(ab[:, hd, :], bt[:, 0:384], sp[:, hd, :], ALU.add), tb, lb)
                c.h_pt2[hd].give(x)
                x = c.act(lambda e: e.activation(ab[:, hd, :], ab[:, hd, :], ACT.Exp), x)
                for at, m in ((0, "before"), (128, "ones"), (256, "before")):
                    x2 = c.pool(lambda e, at=at, m=m: e.tensor_tensor(
                        wk[:, side, hd, at:at + P], ab[:, hd, at:at + P], c.con(m), ALU.mult),
                        x, c.h_wk[side])
                h_z[side][hd].give(x2, tb)
                return x2

            def sb_pair(pair, r):
                heads_ = [scores_sb(pair, hd, r) for hd in range(2)]
                for x in heads_:
                    next(x)
                yield
                x2 = [finish(x) for x in heads_]
                yield
                return c.values_pair(pair % 2, [r, x2], vpart(pair), True, 64, take_heads(pair))
            done = stagger([sb_pair(p, r) for p in range(4)], [gates(0, n) for n in range(4)])
            merge("w_br_sb", done)

            r = heads(Q_FX, K_FX, V_FX)
            r = [r, t_cum]
            def fox_pair(pair, r):
                def scores(hd, qb, z):
                    hh, n = 2 * pair + hd, 128 * (qb + 1)
                    sel = ident[0:HEADS, hh:hh + 1]
                    return [(z, qh[:, hh, qb * P:(qb + 1) * P], kh[:, hh, 0:n], True, False),
                            (z, cT[:, qb * P:(qb + 1) * P], sel.to_broadcast([HEADS, n]), False, False),
                            (z, sel.to_broadcast([HEADS, P]), ncT[:, 0:n], False, False),
                            (z[:, n - P:n], ident, c.con("not_before"), False, True)]
                side, tw = yield from c.softmax_pair(scores, True, ready=r)
                yield
                return c.values_pair(side, tw, vpart(pair), True, 64, take_heads(pair))
            done = stagger([fox_pair(p, r) for p in range(4)], [gates(1, n) for n in range(4)])
            merge("w_br_fox", done)

            t = c.split(merged, c.x, list(summed))
            for n in range(4):
                ap, tok = c.unit(lambda *i, n=n: ("cols", "w_out", i, n * 256))
                for q in range(2):
                    ta = c.tile_T(ap, q, tok, c.x, t, c.acc[:, 2 * n + q, :], None, release=q == 1)
            t_h = c.add_rms(g("mix_post_g"), ta, 1.0)
            ffn(2, t_h)
            c.pad_units(body_start)
            c.barrier()
        c.barrier()
        c.ctx = outer


ALPHA2 = 4 ** 0.25
SGU = 2048
CHUNK = 16
NCH = S // CHUNK


def residual_norm(c, alpha, scale, gain, bias, ready):
    t = [c.dve(lambda e, k=k: e.scalar_tensor_tensor(out=c.h[:, k, :], in0=c.h[:, k, :], scalar=alpha / scale,
                                                     in1=c.acc[:, k, :], op0=ALU.mult, op1=ALU.add), ready)
         for k in range(KT)]
    return c.layer_norm(c.h, KT, gain, bias, c.h, t, c.tmp, eps=1e-5 / scale ** 2)


def block2(c):
    def ln(i, j):
        return [lambda k, x=x: c.col((f"ln_{x}_2", (i, j)), k) for x in "gb"]

    def ffn(i, j, t):
        t = c.split(c.h, c.x, t)
        t = c.ffn(lambda _, n: ("cols", "ffn_w_in_2", (i, 0 if j == 0 else 1), n * 256),
                  lambda _, n: ("cols", "ffn_w_in_2", (i, 0 if j == 0 else 1), DFF + n * 256),
                  lambda _, n: ("rows", "ffn_w_out_2", (i, 0 if j == 0 else 1), n * 256), t)
        return residual_norm(c, ALPHA2, 0.5, *ln(i, j), t)

    with c.scope():
        c.operands("b2a")
        t = ffn(0, 0, None)
        spatial_gating(c, t)
        t = residual_norm(c, ALPHA2, 1.0, *ln(0, 1), None)
        t = ffn(0, 2, t)
        ffn(1, 0, t)
        c.barrier()
    with c.scope():
        rwkv(c)
    with c.scope():
        c.operands("b2b")
        t = residual_norm(c, ALPHA2, 1.0, *ln(1, 1), None)
        ffn(1, 2, t)
        c.barrier()


def spatial_gating(c, ready):
    with ExitStack() as own:
        outer, c.ctx = c.ctx, own
        n_t = SGU // P
        uv = c.sb("sgu_uv", [P, 2 * n_t, S])
        sq = c.sb("sgu_squares", [P, n_t, S])
        rest = Pair(*(c.sb(f"sgu_uv_{n}", [P, KT, S], F32R) for n in ("hi", "lo")))
        uvx = lambda g: c.x[:, g:g + 2, :] if g < KT else rest[:, g - KT:g - KT + 2, :]
        vt = sq[:, :, :].rearrange("p a b -> p (a b)").rearrange("p (b f) -> p b f", b=NB)
        wsp, bsp = c.sb("sgu_w_spatial", [P, n_t, P]), c.sb("sgu_b_spatial", [n_t, P])
        tw = [c.load(wsp[:, :, :], c.aps["sgu_w_spatial"], engine="scalar", name="wsp"),
              c.load(bsp[:, :], c.aps["sgu_b_spatial"], engine="scalar", name="bsp")]
        for g in range(n_t):
            tm = c.pool(lambda e, g=g: e.tensor_tensor(wsp[:, g, :], wsp[:, g, :], c.con("upto"), ALU.mult), tw)

        def take(t, ps, ready, free):
            x = c.act(lambda e: e.activation(uv[:, t, :], ps[:, 0:S], ACT.Gelu, bias=c.col(("sgu_b_in_2", 0), t)), ready)
            free.give(x)
            return x
        t = c.split(c.h, c.x, ready)
        z = c.project(lambda _, n: ("cols", "sgu_w_in_2", 0, n * 256), 16, t, take)
        v = uv[:, n_t:2 * n_t, :]
        t = c.layer_norm(v, n_t, lambda k: c.col(("sgu_ln_g_2", 0), k), lambda k: c.col(("sgu_ln_b_2", 0), k),
                         v, z[n_t:], sq, mat="mean_half")
        c.barrier()
        turned = []
        for b in range(NB):
            for g4 in range(n_t // 4):
                n = (g4 + b * 4) % 4

                def turn(e, b=b, g4=g4, n=n):
                    for q in range(4):
                        i = e.transpose(c.bank[n][:, q * P:(q + 1) * P], v[:, 4 * g4 + q, b * P:(b + 1) * P],
                                        c.con("identity"))
                    return i
                t = c.pe(turn, c.hb[n])
                f = vt[:, b, g4 * 512:(g4 + 1) * 512]
                t = (c.act(lambda e, f=f, n=n: e.activation(f, c.bank[n][:, :], ACT.Copy), t) if n % 2 else
                     c.dve(lambda e, f=f, n=n: e.tensor_copy(f, c.bank[n][:, :]), t))
                c.hb[n].give(t)
                turned.append(t)
        gated = []
        for g in range(n_t):
            n = g % 4
            calls = []
            for b in range(NB):
                o = c.bank[n][:, b * P:(b + 1) * P]
                calls += [(o, vt[:, b, g * P:(g + 1) * P], wsp[:, g, :], b == 0, False),
                          (o, c.con("identity")[0:n_t, g:g + 1].to_broadcast([n_t, P]), bsp[:, :], False, True)]
            t = c.mms(calls, turned, tm, tw, c.hb[n])
            t = c.dve(lambda e, g=g, n=n: e.tensor_tensor(uv[:, g, :], uv[:, g, :], c.bank[n][:, 0:S], ALU.mult), t)
            c.hb[n].give(t)
            gated.append(t)
            if g % 2:
                gated[-2:] = c.split(uv[:, g - 1:g + 1, :], uvx(g - 1), t, n=2) * 2
        for n in range(8):
            ap, tok = c.unit(lambda *_, n=n: ("rows", "sgu_w_out_2", 0, n * 256), a=2)
            for q in range(2):
                t2 = c.mms([(c.acc[:, m, :], ap[:, q, m * P:(m + 1) * P], uvx(2 * n)[:, q, :],
                             n == 0 and q == 0 and m % 2 == 0, False) for m in range(KT)], tok, gated[2 * n + q],
                           release=q == 1)
        c.barrier()
        c.ctx = outer


def rwkv(c):
    flat8 = lambda x: x[:, :, :].rearrange("p a b -> p (a b)")
    r, k, kk, bb, v = (c.sb(f"rwkv_{n}", [P, KT, S]) for n in ("r", "k", "kk", "b", "v"))
    ld = c.sb("rwkv_log_decay", [P, NB, D])

    def shifted(dst):
        a = c.dve(lambda e: e.tensor_tensor(dst[:, :, 1:S], c.h[:, :, 0:S - 1], c.h[:, :, 1:S], ALU.subtract))
        b = c.dve(lambda e: e.tensor_scalar(dst[:, :, 0:1], c.h[:, :, 0:1], -1.0, None, ALU.mult))
        return [a, b]

    def mix(j, xx, dst, ready):
        for q in range(KT):
            t = c.dve(lambda e, q=q: e.scalar_tensor_tensor(
                out=dst[:, q, :], in0=xx[:, q, :], scalar=c.col(("rwkv_mu_2", (0, j)), q), in1=c.h[:, q, :],
                op0=ALU.mult, op1=ALU.add), ready)
        return t

    def copy_out(dst):
        def take(t, ps, ready, free):
            x = (c.act(lambda e: e.activation(dst[:, t, :], ps[:, 0:S], ACT.Copy), ready) if t % 2 else
                 c.dve(lambda e: e.tensor_copy(dst[:, t, :], ps[:, 0:S]), ready))
            free.give(x)
            return x
        return take

    with c.scope():
        lora = Pair(*(c.sb(f"rwkv_lora_{n}", [P, 2, S], F32R) for n in ("hi", "lo")))
        low = c.sb("rwkv_low_rank", [P, 2, S])
        w0row = c.sb("rwkv_w0_row", [1, D])
        tw0 = c.load(w0row[:, :], c.aps["rwkv_w0_row"], engine="scalar", name="w0")
        ones_row = c.con("ones")[0:1, :]
        xs = [Pair(*(c.sb(f"rwkv_x{i}_{n}", [P, KT, S], F32R) for n in ("hi", "lo"))) for i in range(2)]
        x_read, m_read = [Hand(c) for _ in range(2)], [Hand(c) for _ in range(2)]
        sx = shifted(c.tmp)

        def mixed(j, buf):
            t = mix(j, c.tmp, buf, [sx, m_read[j % 2].take()])
            t = c.split(buf, xs[j % 2], t, free=x_read[j % 2])
            m_read[j % 2].give(t)
            return t
        t = mixed(0, c.xn)
        for j, dst in enumerate((r, k, v)):
            t_next = mixed(j + 1, kk if j % 2 == 0 else c.xn)
            out = c.project(lambda _, n, j=j: ("cols", "rwkv_w_rkv_2", (0, j), n * 256), 4, t, copy_out(dst),
                            src=xs[j % 2])
            x_read[j % 2].give(out)
            t = t_next
        xw, xa = t, mixed(4, c.xn)
        ap, tok = c.unit(lambda *_: ("side", ["rwkv_w1_2", "rwkv_a1_2"], 0, 0))
        t1 = c.mms([(c.bank[0][0:64, 0:S], ap[:, q, 0:64], xs[1][:, q, :], q == 0, q == KT - 1) for q in range(KT)],
                   tok, xw, c.hb[0])
        t2 = c.mms([(c.bank[1][0:64, 0:S], ap[:, q, 64:128], xs[0][:, q, :], q == 0, q == KT - 1) for q in range(KT)],
                   tok, xa, c.hb[1], release=True)
        t1 = c.act(lambda e: e.activation(low[0:64, 0, :], c.bank[0][0:64, 0:S], ACT.Tanh), t1)
        t2 = c.dve(lambda e: e.tensor_copy(low[0:64, 1, :], c.bank[1][0:64, 0:S]), t2)
        c.hb[0].give(t1), c.hb[1].give(t2)
        c.split(low[0:64], lora[0:64], [t1, t2], n=2)
        c.barrier()
        ap, tok = c.unit(lambda *_: ("stack", ["rwkv_w2_2", "rwkv_a2_2"], 0, 0), a=2)
        for b in range(NB):
            for q in range(2):
                n = 2 * b + q
                t = c.mms([(c.bank[n][:, :], lora[0:64, 0, b * P:(b + 1) * P], ap[0:64, 0, q * 512:(q + 1) * 512], True, False),
                           (c.bank[n][:, :], ones_row, w0row[:, q * 512:(q + 1) * 512], False, True)], tok, tw0, c.hb[n])
                dst = ld[:, b, q * 512:(q + 1) * 512]
                t = c.act(lambda e, n=n, dst=dst: e.activation(dst, c.bank[n][:, :], ACT.Sigmoid), t)
                c.hb[n].give(t)
                tld = c.dve(lambda e, dst=dst: e.tensor_scalar(dst, dst, -float(np.exp(-0.5)), None, ALU.mult), t)
        for q in range(KT):
            n = q % 4
            t = c.mms([(c.bank[n][:, 0:S], ap[0:64, 1, q * P:(q + 1) * P], lora[0:64, 1, :], True, True)] , tok, c.hb[n],
                      release=q == KT - 1)
            ta = c.act(lambda e, n=n, q=q: e.activation(bb[:, q, :], c.bank[n][:, 0:S], ACT.Sigmoid,
                                                        bias=c.col(("rwkv_a0_2", 0), q)), t)
            c.hb[n].give(ta)
        for q in range(KT):
            t = c.dve(lambda e, q=q: e.tensor_scalar(kk[:, q, :], k[:, q, :], c.col(("rwkv_k_k_2", 0), q), None, ALU.mult))
            t = c.act(lambda e, q=q: e.activation(c.xn[:, q, :], kk[:, q, :], ACT.Square), t)
            n = q % 4
            t = c.mms([(c.bank[n][:, 0:S], c.con("head_sum"), c.xn[:, q, :], True, True)], t, c.hb[n])
            t = c.act(lambda e, q=q, n=n: e.activation(c.tmp[:, q, :], c.bank[n][:, 0:S], ACT.Sqrt), t)
            c.hb[n].give(t)
        t = c.dve(lambda e: e.tensor_scalar(c.tmp[:, :, :], c.tmp[:, :, :], 1e-12, None, ALU.max), t)
        t = c.dve(lambda e: e.reciprocal(c.tmp[:, :, :], c.tmp[:, :, :]), t)
        tkk = c.dve(lambda e: e.tensor_tensor(kk[:, :, :], kk[:, :, :], c.tmp[:, :, :], ALU.mult), t)
        for q in range(KT):
            t = c.dve(lambda e, q=q: e.tensor_scalar(c.xn[:, q, :], bb[:, q, :], 1.0, c.col(("rwkv_k_a_2", 0), q),
                                                     ALU.subtract, ALU.mult), ta, tkk)
        t = c.dve(lambda e: e.scalar_tensor_tensor(out=flat8(k), in0=flat8(c.xn), scalar=1.0, in1=flat8(k),
                                                   op0=ALU.add, op1=ALU.mult), t)
        t = c.dve(lambda e: e.tensor_tensor(bb[:, :, :], bb[:, :, :], kk[:, :, :], ALU.mult), tkk)
        c.barrier()
    with c.scope():
        G, H = c.sb("rwkv_G", [P, 4, NCH, 64]), c.sb("rwkv_H", [P, 4, NCH, 64])
        Rs = c.sb("rwkv_R", [P, 4, S])
        rwkv_scan(c, r, k, kk, bb, v, ld, G, H, Rs)
        c.barrier()

    with c.scope():
        x = Pair(*(c.sb(f"rwkv_out_x_{n}", [P, KT, S], F32R) for n in ("hi", "lo")))
        g_lora = Pair(*(c.sb(f"rwkv_gate_lora_{n}", [P, 2, S], F32R) for n in ("hi", "lo")))
        g_low = c.sb("rwkv_gate_low_rank", [P, 2, S])
        y = kk
        for q in range(KT):
            n = q % 4
            t = c.mms([(c.bank[n][:, 0:S], c.con("head_mean"), y[:, q, :], True, True)], c.hb[n])
            t = c.dve(lambda e, q=q, n=n: e.tensor_tensor(y[:, q, :], y[:, q, :], c.bank[n][:, 0:S], ALU.subtract), t)
            c.hb[n].give(t)
            t = c.act(lambda e, q=q: e.activation(c.tmp[:, q, :], y[:, q, :], ACT.Square), t)
            t = c.mms([(c.bank[n][:, 0:S], c.con("head_mean"), c.tmp[:, q, :], True, True)], t, c.hb[n])
            t = c.act(lambda e, q=q, n=n: e.activation(c.tmp[:, q, :], c.bank[n][:, 0:S], ACT.Sqrt, bias=c.eps(64e-5)), t)
            c.hb[n].give(t)
        t = c.dve(lambda e: e.reciprocal(c.tmp[:, :, :], c.tmp[:, :, :]), t)
        for q in range(KT):
            t2 = c.dve(lambda e, q=q: e.scalar_tensor_tensor(
                out=y[:, q, :], in0=y[:, q, :], scalar=c.col(("rwkv_gn_g_2", 0), q), in1=c.tmp[:, q, :],
                op0=ALU.mult, op1=ALU.mult), t)
            tr = c.dve(lambda e, q=q: e.scalar_tensor_tensor(
                out=c.xn[:, q, :], in0=r[:, q, :], scalar=c.col(("rwkv_r_k_2", 0), q), in1=k[:, q, :],
                op0=ALU.mult, op1=ALU.mult))
            n = q % 4
            tb = c.mms([(c.bank[n][:, 0:S], c.con("head_sum"), c.xn[:, q, :], True, True)], tr, c.hb[n])
            tb = c.dve(lambda e, q=q, n=n: e.tensor_tensor(v[:, q, :], v[:, q, :], c.bank[n][:, 0:S], ALU.mult), tb)
            c.hb[n].give(tb)
            t3 = c.dve(lambda e, q=q: e.scalar_tensor_tensor(
                out=y[:, q, :], in0=y[:, q, :], scalar=c.col(("rwkv_gn_b_2", 0), q), in1=v[:, q, :],
                op0=ALU.add, op1=ALU.add), t2, tb)
        c.barrier()
        sx = shifted(c.tmp)
        t = mix(5, c.tmp, c.xn, sx)
        t = c.split(c.xn, x, [t])
        ap, tok = c.unit(lambda *_: ("side", ["rwkv_g1_2"], 0, 0))
        both = []
        for q, n in enumerate((P, 32)):
            tq = c.mms([(c.bank[q][0:n, 0:S], ap[:, m, q * P:q * P + n], x[:, m, :], m == 0, m == KT - 1)
                        for m in range(KT)], tok, t, c.hb[q], release=q == 1)
            tg = c.act(lambda e, q=q, n=n: e.activation(g_low[0:n, q, :], c.bank[q][0:n, 0:S], ACT.Sigmoid), tq)
            c.hb[q].give(tg)
            tl = c.split(g_low[0:n, q:q + 1], g_lora[0:n, q:q + 1], tg, n=1, step=1)
            tg = [tl, tg]
            both.append(tg)
        yt = []
        ap, tok = c.unit(lambda *_: ("rows", "rwkv_g2_2", 0, 0), a=2)
        for q in range(KT):
            n = q % 4
            t = c.mms([(c.bank[n][:, 0:S], ap[:, 0, q * P:(q + 1) * P], g_lora[:, 0, :], True, False),
                       (c.bank[n][:, 0:S], ap[0:32, 1, q * P:(q + 1) * P], g_lora[0:32, 1, :], False, True)],
                      tok, both, c.hb[n], release=q == KT - 1)
            t = c.dve(lambda e, q=q, n=n: e.tensor_tensor(y[:, q, :], y[:, q, :], c.bank[n][:, 0:S], ALU.mult), t)
            c.hb[n].give(t)
            yt.append(t)
        t = c.split(y, x, yt)
        for n in range(4):
            ap, tok = c.unit(lambda *_, n=n: ("cols", "rwkv_w_o_2", 0, n * 256))
            for q in range(2):
                c.tile_T(ap, q, tok, x, t, c.acc[:, 2 * n + q, :], None, release=q == 1)
        c.barrier()


def rwkv_scan(c, r, k, kk, bb, v, ld, G, H, Rs):
    flat8 = lambda x: x[:, :, :].rearrange("p a b -> p (a b)")
    pair8 = {n: flat8(x) for n, x in (("r", r), ("k", k), ("kk", kk), ("b", bb), ("v", v))}
    part = lambda n, i: pair8[n][:, bass.ts(i, S)]
    two = lambda x: x.rearrange("p (b t) -> p b t", b=NB)
    with ExitStack() as own:
        outer, c.ctx = c.ctx, own
        sb2 = lambda n: c.sb(f"rwkv_{n}", [P, S])
        ldp = c.rstd[:, :].rearrange("p (b f) -> p b f", b=NB)
        eL, emL, eX, eA = (sb2(n) for n in ("e_cum", "e_neg_cum", "e_cum_before", "e_to_end"))
        bt, rt, bh, vs = (sb2(n) for n in ("bt", "rt", "bh", "vs"))
        at, kt, kh = eX, emL, eA
        sq2 = c.sb("rwkv_squares", [P, 2, 4, P])
        wt, zt = (c.sb(f"rwkv_{n}", [P, NB, P]) for n in ("W", "U"))
        ut = zt
        bx, ux, vx = (c.sb(f"rwkv_{n}", [P, 8, 64]) for n in ("b_by_chunk", "u_by_chunk", "v_by_chunk"))
        st = c.sb("rwkv_state", [P, 2, 4, 64])
        tf, xf = flat8(c.tmp), flat8(c.xn)
        tok = tf[:, 0:1024].rearrange("p (a b f) -> p a b f", a=4, b=NB)
        diag = tf[:, 1024:2048].rearrange("p (n j) -> p n j", n=NCH)
        pm = xf[:, 0:1024].rearrange("p (h a t) -> p h a t", h=2, a=4)
        arb = xf[:, 1024:2048].rearrange("p (h a t) -> p h a t", h=2, a=4)
        rk = c.act_gate[:, :, :].rearrange("p h (b t) -> p h b t", b=NB)
        X = c.hidden[:, :, :].rearrange("p h (b t) -> p h b t", b=NB)
        B = [b[:, :] for b in c.bank] + [c.acc[:, 2 * i:2 * i + 2, :].rearrange("p a b -> p (a b)") for i in range(4)]
        hB = c.hb + [Hand(c) for _ in range(4)]
        ident = c.con("identity")
        mask2 = lambda name: c.con(name).unsqueeze(1).to_broadcast([P, 2, P])
        ld_v = ld[:, :, :]

        def copy(dst, src, ready, who):
            if who == "act":
                return c.act(lambda e: e.activation(dst, src, ACT.Copy), ready)
            return c.dve(lambda e: e.tensor_copy(dst, src), ready)

        def tt(dst, a, b, op, *ready, who=c.dve):
            return who(lambda e: e.tensor_tensor(dst, a, b, op), *ready)

        for half in range(2):
            with c.repeat(4) as q:
                px = lambda half=half, q=q: half * 4 + q.cur
                c.barrier()
                t0 = c.dve(lambda e, px=px: e.tensor_copy(ldp[:, :, :], ld_v[:, :, bass.ts(px(), P)]))
                tv = c.pool(lambda e, px=px: e.tensor_copy(vs[:, :], part("v", px())))
                tl = []
                for i, m in enumerate(("chunk_upto", "chunk_before", "chunk_after")):
                    for b in range(NB):
                        o = B[i // 2][:, (i % 2) * S + b * P:][:, 0:P]
                        tl.append(c.mms([(o, ldp[:, b, :], c.con(m), b == 0, True)], t0,
                                        hB[i // 2] if b == 0 and i % 2 == 0 else None))
                ex = []
                for dst, src, sc in ((eL, B[0][:, 0:S], 1.0), (emL, B[0][:, 0:S], -1.0), (eX, B[0][:, S:2 * S], 1.0),
                                     (eA, B[1][:, 0:S], 1.0)):
                    ex.append(c.act(lambda e, dst=dst, src=src, sc=sc: e.activation(dst[:, :], src, ACT.Exp, scale=sc), tl))
                hB[0].give(ex[:3]), hB[1].give(ex[3])
                ta = c.dve(lambda e, px=px: e.scalar_tensor_tensor(out=at[:, :], in0=part("kk", px()), scalar=-1.0,
                                                            in1=eX[:, :], op0=ALU.mult, op1=ALU.mult), ex)
                tb = c.dve(lambda e, px=px: e.tensor_tensor(bt[:, :], part("b", px()), emL[:, :], ALU.mult), ex)
                tr = c.dve(lambda e, px=px: e.tensor_tensor(rt[:, :], part("r", px()), eL[:, :], ALU.mult), ex)
                tk = c.dve(lambda e, px=px: e.tensor_tensor(kt[:, :], part("k", px()), emL[:, :], ALU.mult), ex, tb)
                tbh = c.dve(lambda e, px=px: e.tensor_tensor(bh[:, :], part("b", px()), eA[:, :], ALU.mult), ex)
                tkh = c.dve(lambda e, px=px: e.tensor_tensor(kh[:, :], part("k", px()), eA[:, :], ALU.mult), ex, tbh)
                tt_done = []
                for n, (x, y, w) in enumerate(((at, bh, [ta, tbh]), (kh, vs, [tkh, tv]))):
                    def turn(e, n=n, x=x, y=y):
                        for i, z in enumerate((x, y)):
                            for b in range(NB):
                                ins = e.transpose(B[2 + n][:, (2 * i + b) * P:][:, 0:P], z[:, b * P:(b + 1) * P], ident)
                        return ins
                    t = c.pe(turn, w, hB[2 + n])
                    t = copy(tok[:, 2 * n:2 * n + 2, :, :], B[2 + n].rearrange("p (a b f) -> p a b f", a=2, b=NB), t, "act")
                    hB[2 + n].give(t)
                    tt_done.append(t)
                dc = two(eL[:, :]).rearrange("p b (n t) -> p (b n) t", t=CHUNK)[:, :, CHUNK - 1:CHUNK]
                tdg = tt(diag, c.con("identity_pair")[:, 0:64].unsqueeze(1).to_broadcast([P, NCH, 64]),
                         dc.to_broadcast([P, NCH, 64]), ALU.mult, ex, who=c.pool)
                tri = []
                for hd in range(2):
                    R = slice(64 * hd, 64 * hd + 64)
                    bA, bB, bC = 4 + 2 * hd, 5 + 2 * hd, hd
                    T = [slice(b * P, (b + 1) * P) for b in range(NB)]
                    prod = lambda bank, at_, x, y: [(B[bank][:, at_ + b * P:][:, 0:P], x[R, T[b]], y[R, T[b]],
                                                     at_ == 0 and b == 0, True) for b in range(NB)]
                    t = c.mms(prod(bA, 0, bt, at) + prod(bA, S, at, bt), ta, tb, hB[bA])
                    m1 = tt(pm[:, hd, 0:2, :], two(B[bA][:, 0:S]), mask2("chunk_before"), ALU.mult, t)
                    m2 = tt(pm[:, hd, 2:4, :], two(B[bA][:, S:2 * S]), mask2("chunk_after"), ALU.mult, t)
                    hB[bA].give(m2)
                    t = c.mms(prod(bB, 0, kt, at) + prod(bB, S, bt, rt), ta, tb, tr, tk, hB[bB])
                    m3 = tt(arb[:, hd, 0:2, :], two(B[bB][:, 0:S]), mask2("chunk_before"), ALU.mult, t)
                    m4 = tt(arb[:, hd, 2:4, :], two(B[bB][:, S:2 * S]), mask2("chunk_upto"), ALU.mult, t)
                    hB[bB].give(m4)
                    t = c.mms(prod(bC, 0, kt, rt), tr, tk, hB[bC])
                    m5 = tt(rk[:, hd], two(B[bC][:, 0:S]), mask2("chunk_upto"), ALU.mult, t)
                    hB[bC].give(m5)
                    x0 = tt(X[:, hd], pm[:, hd, 0:2, :], mask2("identity"), ALU.add, m1)
                    tri.append((m1, m2, m3, m4, m5, x0))
                mats = [dict(P=pm[:, hd, 0:2, :], M=pm[:, hd, 2:4, :], t=list(tri[hd])) for hd in range(2)]
                for step in range(3):
                    for hd in range(2):
                        m = mats[hd]
                        bA, bB = 4 + 2 * hd, 5 + 2 * hd
                        dst = sq2[:, hd] if step % 2 == 0 else pm[:, hd]
                        calls = [(B[bA][:, S + b * P:][:, 0:P], m["P"][:, b, :], m["M"][:, b, :], b == 0, True) for b in range(NB)]
                        if step < 2:
                            calls += [(B[bA][:, b * P:][:, 0:P], m["M"][:, b, :], m["P"][:, b, :], False, True) for b in range(NB)]
                        t = c.mms(calls, m["t"], hB[bA])
                        if step < 2:
                            cp = copy(dst, B[bA].rearrange("p (a t) -> p a t", a=4), t, "act")
                        else:
                            cp = copy(dst[:, 2:4, :], two(B[bA][:, S:2 * S]), t, "act")
                        hB[bA].give(cp)
                        m["P"], m["M"] = dst[:, 0:2, :], dst[:, 2:4, :]
                        t = c.mms([(B[bB][:, b * P:][:, 0:P], m["M"][:, b, :], X[:, hd, b, :], b == 0, True)
                                   for b in range(NB)], cp, m["t"], hB[bB])
                        ad = tt(X[:, hd], X[:, hd], two(B[bB][:, 0:S]), ALU.add, t)
                        hB[bB].give(ad)
                        m["t"] = [cp, ad]
                done = [m["t"] for m in mats]
                F = [slice(64 * hd, 64 * hd + 64) for hd in range(2)]
                hdb = [(hd, b) for hd in range(2) for b in range(NB)]
                t = c.mms([(B[2][:, b * P + 64 * hd:][:, 0:64], X[:, hd, b, :], tok[:, 0, b, F[hd]], i == 0, True)
                           for i, (hd, b) in enumerate(hdb)], done, tt_done, hB[2])
                tw_ = copy(wt[:, :, :], two(B[2][:, 0:S]), t, "act")
                hB[2].give(tw_)
                t = c.mms([(B[3][:, b * P + 64 * hd:][:, 0:64], arb[:, hd, b, :], tok[:, 3, b, F[hd]], i == 0, True)
                           for i, (hd, b) in enumerate(hdb)], done, tt_done, hB[3])
                tz = copy(zt[:, :, :], two(B[3][:, 0:S]), t, "dve")
                hB[3].give(tz)
                t = c.mms([(B[3][:, b * P + 64 * hd:][:, 0:64], X[:, hd, b, :], zt[:, b, F[hd]], i == 0, True)
                           for i, (hd, b) in enumerate(hdb)], tz, hB[3])
                tu = copy(ut[:, :, :], two(B[3][:, 0:S]), t, "dve")
                hB[3].give(tu)
                for hd in range(2):
                    R, bk, bk2 = slice(64 * hd, 64 * hd + 64), 4 + hd, 6 + hd
                    t = c.mms([(B[bk][:, b * P:][:, 0:P], wt[:, b, :], arb[:, hd, 2 + b, :], b == 0, True)
                               for b in range(NB)], tw_, tri[hd], hB[bk])
                    t = c.dve(lambda e, R=R, bk=bk, q=q: e.tensor_tensor(
                        Rs[R].rearrange("p a b -> p (a b)")[:, bass.ts(q.cur, S)], B[bk][R, 0:S], rt[R, :], ALU.add), t)
                    hB[bk].give(t)
                    calls = []
                    for b in range(NB):
                        calls += [(B[bk2][:, b * P:][:, 0:P], ut[:, b, :], arb[:, hd, 2 + b, :], b == 0, False),
                                  (B[bk2][:, b * P:][:, 0:P], tok[:, 3, b, :], rk[:, hd, b, :], False, True)]
                    t = c.mms(calls, tu, tri[hd], tt_done, hB[bk2])
                    t = c.act(lambda e, R=R, bk2=bk2, px=px: e.activation(pair8["kk"][R, bass.ts(px(), S)], B[bk2][R, 0:S],
                                                                   ACT.Copy), t, ta)
                    hB[bk2].give(t)
                h_x = None
                for i, (hd, b) in enumerate(hdb):
                    R = slice(64 * hd, 64 * hd + 64)
                    spread = lambda src: src.unsqueeze(1).to_broadcast([P, 8, 64])
                    chunks = c.con("chunk_of")[:, 0:8].unsqueeze(2).to_broadcast([P, 8, 64])
                    s1 = tt(bx[:, :, :], spread(tok[:, 1, b, F[hd]]), chunks, ALU.mult, tt_done, h_x)
                    s2 = tt(ux[:, :, :], spread(ut[:, b, F[hd]]), chunks, ALU.mult, tu, h_x)
                    s3 = tt(vx[:, :, :], spread(tok[:, 3, b, F[hd]]), chunks, ALU.mult, tt_done, h_x, who=c.pool)
                    bg, bq = i % 2, 2 + i % 2
                    fl = lambda x: x[:, :, :].rearrange("p n j -> p (n j)")
                    tg = c.mms([(B[bg], wt[:, b, :], fl(bx), True, True)], tw_, s1, hB[bg])
                    th = c.mms([(B[bq], tok[:, 1, b, :], fl(ux), True, False), (B[bq], tok[:, 2, b, :], fl(vx), False, True)],
                               s2, s3, hB[bq])
                    h_x = [tg, th]
                    n8 = slice(8 * b, 8 * b + 8)
                    gdst = lambda x, R=R, n8=n8, q=q: x[R].rearrange("p q n j -> p q (n j)")[:, bass.ds(q.cur, 1), 512 * (n8.start // 8):][:, :, 0:512]
                    tg = c.dve(lambda e, R=R, n8=n8, bg=bg, gdst=gdst: e.tensor_tensor(
                        gdst(G), B[bg][R, :].unsqueeze(1), diag[R, n8, :].rearrange("p n j -> p (n j)").unsqueeze(1), ALU.add), tg, tdg)
                    hB[bg].give(tg)
                    th = c.act(lambda e, R=R, n8=n8, bq=bq, gdst=gdst: e.activation(
                        gdst(H), B[bq][R, :].unsqueeze(1), ACT.Copy), th)
                    hB[bq].give(th)
            c.barrier()
            t = c.dve(lambda e: e.memset(st[:, 0, :, :], 0.0))
            yb = c.acc[:, 0:4, :]
            for n in range(NCH):
                cur, nxt = n % 2, (n + 1) % 2
                sb_, hs_ = B[nxt], hB[nxt]
                if n < NCH - 1:
                    tg = c.mms([(sb_[64 * hd:64 * hd + 64, p_ * 64:(p_ + 1) * 64], G[64 * hd:64 * hd + 64, p_, n, :],
                                 st[64 * hd:64 * hd + 64, cur, p_, :], p_ == 0, True)
                                for p_ in range(4) for hd in range(2)], t, hs_)
                ty = c.mms([(yb[64 * hd:64 * hd + 64, p_, n * CHUNK:(n + 1) * CHUNK], st[64 * hd:64 * hd + 64, cur, p_, :],
                             Rs[64 * hd:64 * hd + 64, p_, n * CHUNK:(n + 1) * CHUNK], True, True)
                            for p_ in range(4) for hd in range(2)], t)
                if n < NCH - 1:
                    t2 = tt(st[:, nxt], sb_[:, 0:S].rearrange("p (a j) -> p a j", a=4), H[:, :, n, :], ALU.add,
                            tg, last_y if n else None)
                    hs_.give(t2)
                    t = t2
                last_y = ty
            y4 = kk[:, 4 * half:4 * half + 4, :]
            tt(y4, y4, yb, ALU.add, ty)
            c.barrier()
        c.ctx = outer


ALPHA3 = 2 ** 0.25
Q_N, KV_C, KV_S, KV_W, Q_M, K_M, V_M, CONV_A, CONV_G = 0, 256, 384, 512, 652, 908, 1164, 1420, 1676
Q_H, F_H, I_H, G_H = 1932, 2188, 2444, 2700
N_CMP, CMP_STEP = 15, 16
BIAS_W = 512
HANKEL_W = 384
TAPS = 31


def bucket_constants():
    d = 255 - np.arange(BIAS_W)
    n = np.maximum(d, 0)
    large = 16 + (np.log(np.maximum(n, 1).astype(np.float32) / 16) / np.log(128 / 16) * 16).astype(np.int32)
    bucket = np.where(n < 16, n, np.minimum(large, 31))
    hot = (np.arange(32)[:, None] == bucket[None, :]) & (d[None, :] >= 0)
    return hot.astype(np.float32), np.where(d < 0, -1e30, 0.0)[None, :].astype(np.float32)


def block3(c):
    c.barrier()
    w3 = lambda start: (lambda *_: ("cols", "w_in_3", 0, start))
    with ExitStack() as own:
        outer, c.ctx = c.ctx, own
        mix = c.sb("mix_out", [P, KT, S])
        c.operands("b3", hidden=3)
        c.split(c.h, c.x, None)
        c.barrier()
        attention3(c, w3, mix)
        conv3(c, w3, mix)
        hgrn3(c, w3, mix)
        t = c.split(mix, c.x, None)
        for n in range(4):
            ap, tok = c.unit(lambda *_, n=n: ("cols", "w_out_3", 0, n * 256))
            for q in range(2):
                c.tile_T(ap, q, tok, c.x, t, c.acc[:, 2 * n + q, :], None, release=q == 1)
        c.barrier()
        t = residual_norm(c, ALPHA3, 1.0, lambda k: c.col(("ln1_g_3", 0), k), lambda k: c.col(("ln1_b_3", 0), k), None)
        x = c.split(c.h, c.x, t)

        def make(j, n):
            a, ta = c.unit(lambda *i: ("cols", "w_ff1_3", 0, j(*i) * 256))
            for q in range(2):
                b = (2 * n + q) % 4
                t = c.tile_T(a, q, ta, c.x, x, c.bank[b][:, 0:S], c.hb[b], release=q == 1)
                r = c.act(lambda e, q=q, b=b: e.activation(c.act_gate[:, q, :], c.bank[b][:, 0:S], ACT.Relu), t, c.h_gate[q])
                c.hb[b].give(r)
                m = c.dve(lambda e, q=q: e.tensor_tensor(c.act_gate[:, q, :], c.act_gate[:, q, :], c.act_gate[:, q, :],
                                                         ALU.mult), r)
                c.hidden_parts(c.act_gate, n, q, m)

        def use(j, n, first=False):
            d, td = c.unit(lambda *i: ("rows", "w_ff2_3", 0, j(*i) * 256), a=2)
            c.add_down(d, td, n, first)

        make(lambda: 0, 0)
        make(lambda: 1, 1)
        use(lambda: 0, 0, first=True)
        with c.repeat(4):
            for n in range(3):
                make(lambda i, n=n: 2 + 3 * i + n, (2 + n) % 3)
                use(lambda i, n=n: 1 + 3 * i + n, (1 + n) % 3)
        make(lambda: 14, 2)
        use(lambda: 13, 1)
        make(lambda: 15, 0)
        use(lambda: 14, 2)
        use(lambda: 15, 0)
        c.barrier()
        residual_norm(c, ALPHA3, 1.0, lambda k: c.col(("ln2_g_3", 0), k), lambda k: c.col(("ln2_b_3", 0), k), None)
        c.barrier()
        c.ctx = outer


def attention3(c, w3, mix):
    with ExitStack() as own:
        outer, c.ctx = c.ctx, own
        c.attention_buffers("b3")
        hot, mrow = c.sb("bias_one_hot", [32, BIAS_W]), c.sb("bias_mask", [1, BIAS_W])
        tabT, brow = c.sb("bias_table", [32, 8]), c.sb("bias_rows", [8, BIAS_W])
        hk = c.sb("bias_hankel", [P, 8, HANKEL_W])
        w2 = c.sb("cmp_w2", [P, 2, 2, 64])
        qn, qm, kmo = (c.sb(n, [64, 4, S]) for n in ("q_nsa", "q_moba", "k_moba"))
        kw_ = c.sb("k_sel_win", [64, 2, S])
        vw_ = c.sb("v_sel_win", [P, NB, 2, 64])
        vmo = c.sb("v_moba", [P, NB, 256])
        gates = c.sb("nsa_gates", [P, NB, 12])
        dup = c.sb("cmp_tokens", [P, 2, S])
        win = c.sb("cmp_windows", [P, 2, 16, 16])
        wx = Pair(*(c.sb(f"cmp_windows_{n}", [P, 2, 16, 16], F32R) for n in ("hi", "lo")))
        t_zero = c.pool(lambda e: e.memset(win[:, :, :, N_CMP:16], 0.0))
        hc = c.sb("cmp_hidden", [P, 2, 2, N_CMP])
        kc, vc = c.sb("cmp_k", [64, N_CMP]), c.sb("cmp_v", [N_CMP, 64])
        pc, pct = c.sb("cmp_w", [P, 2, NB, 16]), c.sb("cmp_w_by_key", [N_CMP, 2, S])
        cst = c.sb("cmp_stats", [P, 3, 2, NB])
        ident, flip = c.con("identity"), c.con("flip")

        tl = [c.load(x[:, :], c.aps[n], engine="scalar", name=n) for x, n in
              ((hot, "bias_one_hot"), (mrow, "bias_mask"), (tabT, "bias_table"))]
        tw2 = c.load(w2[:, :, :, :], c.aps["cmp_w2"], engine="scalar", name="cmp_w2")
        t = c.mms([(c.bank[0][0:8, :], tabT[:, :], hot[:, :], True, False),
                   (c.bank[0][0:8, :], c.con("ones")[0:1, 0:8], mrow[:, :], False, True)], tl, c.hb[0])
        t = c.dve(lambda e: e.tensor_copy(brow[:, :], c.bank[0][0:8, :]), t)
        c.hb[0].give(t)
        scratch = c.nc.dram_tensor("bias_scratch", (8, BIAS_W), F32, kind="Internal").ap()
        t = c.load(scratch, brow[:, :], t, engine="scalar", name="bias_store")
        hankel = bass.AP(tensor=scratch.tensor, offset=0, ap=[[1, P], [BIAS_W, 8], [1, HANKEL_W]])
        thk = c.load(hk[:, :, :], hankel, t, engine="scalar", name="hankel")

        sc = HD ** -0.5
        take_heads = lambda dst, s: (lambda t, ps, r, f: c.evac_heads(ps, dst, t, s, r, f))
        r_q = c.project(lambda _, n: w3(Q_N)(), 1, None, take_heads(qn, sc))
        ap, tok = c.unit(w3(KV_C))
        t = c.tile_T(ap, 0, tok, c.x, None, c.bank[2][:, 0:S], c.hb[2])
        td = []
        for e_ in range(2):
            for half in range(2):
                td.append(c.act(lambda e, e_=e_, half=half: e.activation(
                    dup[64 * half:64 * half + 64, e_, :], c.bank[2][64 * e_:64 * e_ + 64, 0:S], ACT.Copy), t))
        c.hb[2].give(td)
        t = c.mms([(c.bank[3][0:64, 0:S], ap[:, k, 128:192], c.x[:, k, :], k == 0, k == KT - 1) for k in range(KT)],
                  tok, c.hb[3])
        rk = [c.dve(lambda e: e.tensor_copy(kw_[:, 0, :], c.bank[3][0:64, 0:S]), t)]
        c.hb[3].give(rk)
        rv = []

        def tokens(ap, tok, at, width, b, bank, dst, func=ACT.Copy, release=False):
            t = c.mms([(c.bank[bank][:, 0:width], c.x[:, k, b * P:(b + 1) * P], ap[:, k, at:at + width], k == 0,
                        k == KT - 1) for k in range(KT)], tok, c.hb[bank], release=release)
            t = c.act(lambda e: e.activation(dst, c.bank[bank][:, 0:width], func), t)
            c.hb[bank].give(t)
            return t
        for b in range(NB):
            rv.append(tokens(ap, tok, 192, 64, b, b, vw_[:, b, 0, :], release=b == 1))
        ap, tok = c.unit(w3(KV_W))
        t = c.mms([(c.bank[2][0:64, 0:S], ap[:, k, 0:64], c.x[:, k, :], k == 0, k == KT - 1) for k in range(KT)],
                  tok, c.hb[2])
        rk.append(c.dve(lambda e: e.tensor_copy(kw_[:, 1, :], c.bank[2][0:64, 0:S]), t))
        c.hb[2].give(rk[-1])
        for b in range(NB):
            rv.append(tokens(ap, tok, 64, 64, b, b, vw_[:, b, 1, :]))
        for b in range(NB):
            rv.append(tokens(ap, tok, 128, 12, b, 2 + b, gates[:, b, :], func=ACT.Sigmoid, release=b == 1))
        r_m = [c.project(lambda _, n: w3(Q_M)(), 1, None, take_heads(qm, sc)),
               c.project(lambda _, n: w3(K_M)(), 1, None, take_heads(kmo, 1.0)),
               c.project_tok(lambda _, n: w3(V_M)(), 1, None, vmo)]

        for e_ in range(2):
            tw = []
            for half in range(2):
                R = slice(64 * half, 64 * half + 64)
                v = dup[R, e_, :].rearrange("p (n l m) -> p l m n", n=16, l=8, m=2)
                for hi in range(2):
                    pe_ = c.col(("nsa_cmp_pe_3", (0, e_)), 8 * hi, 8)[R].unsqueeze(2).to_broadcast([64, 8, N_CMP])
                    tw.append(c.dve(lambda e, v=v, hi=hi, half=half, R=R, e_=e_, pe_=pe_: e.tensor_tensor(
                        win[R, e_, 8 * hi:8 * hi + 8, 0:N_CMP], v[:, :, half, hi:hi + N_CMP], pe_, ALU.add), td))
            tw = c.split(win[:, e_], wx[:, e_], [tw, t_zero], n=16, step=8)
            t = []
            for n in range(2):
                ap, tok = c.unit(lambda *_, n=n, e_=e_: ("cols", "nsa_cmp_w1_3", (0, e_, slice(n * D, n * D + D)), 0))
                for m in range(2):
                    t.append(c.mms([(c.bank[2 * e_ + m][:, 0:16], ap[:, k, m * P:(m + 1) * P], wx[:, e_, 8 * n + k, :],
                                     n == 0 and k == 0, n == 1 and k == KT - 1) for k in range(KT)],
                                   tok, tw, c.hb[2 * e_ + m] if n == 0 else None, release=m == 1))
            tg = []
            for m in range(2):
                tg.append(c.act(lambda e, m=m, e_=e_: e.activation(hc[:, e_, m, :], c.bank[2 * e_ + m][:, 0:N_CMP],
                          ACT.Gelu_apprx_tanh, bias=c.col(("nsa_cmp_b1_3", (0, e_)), m)), t))
                c.hb[2 * e_ + m].give(tg[-1])
            if e_ == 0:
                t = c.mms([(c.bank[0][0:64, 0:N_CMP], w2[:, 0, m, :], hc[:, 0, m, :], m == 0, m == 1) for m in range(2)],
                          tg, tw2, c.hb[0])
                tkc = c.dve(lambda e: e.tensor_copy(kc[:, :], c.bank[0][0:64, 0:N_CMP]), t)
                c.hb[0].give(tkc)
            else:
                t = c.mms([(c.bank[1][0:N_CMP, 0:64], hc[:, 1, m, :], w2[:, 1, m, :], m == 0, m == 1) for m in range(2)],
                          tg, tw2, c.hb[1])
                tvc = c.dve(lambda e: e.tensor_copy(vc[:, :], c.bank[1][0:N_CMP, 0:64]), t)
                c.hb[1].give(tvc)

        def bias(z, head, qb):
            w = hk[:, head, P:2 * P] if qb == 0 else hk[:, head, 0:2 * P]
            return (z, flip, w, False, True)

        def take(pair):
            def f(ob, t):
                a = c.act(lambda e: e.activation(mix[0:64, pair, :], ob[0:64, 0, :], ACT.Copy), t)
                return c.act(lambda e: e.activation(mix[64:128, pair, :], ob[0:64, 1, :], ACT.Copy), a)
            return f

        def compressed(pair, ready):
            z = c.bank[0][:, 0:64].rearrange("p (h b n) -> p h b n", h=2, b=NB)
            calls = []
            for hd in range(2):
                for qb in range(NB):
                    h = 2 * pair + hd
                    off = 159 if qb == 0 else 31
                    calls += [(z[:, hd, qb, 0:N_CMP], qn[:, h, qb * P:(qb + 1) * P], kc[:, :], hd + qb == 0, False),
                              (z[:, hd, qb, 0:N_CMP], flip, hk[:, h, off:off + CMP_STEP * (N_CMP - 1) + 1:CMP_STEP], False, True)]
            t = c.mms(calls, ready, c.hb[0])
            t = c.dve(lambda e: e.tensor_reduce(cst[:, 0, :, :], z[:, :, :, 0:N_CMP], AX, ALU.max, negate=True), t)
            t = c.dve(lambda e: e.tensor_scalar(cst[:, 0, :, :], cst[:, 0, :, :], 1e20, None, ALU.min), t)
            ex = [c.act(lambda e, hd=hd, qb=qb: e.activation(
                pc[:, hd, qb, 0:N_CMP], z[:, hd, qb, 0:N_CMP], ACT.Exp, bias=cst[:, 0, hd, qb:qb + 1],
                accum_out=cst[:, 1, hd, qb:qb + 1]), t) for hd in range(2) for qb in range(NB)]
            c.hb[0].give(ex)
            t = c.dve(lambda e: e.tensor_scalar(cst[:, 1, :, :], cst[:, 1, :, :], 1e-30, None, ALU.max), ex)
            t = c.dve(lambda e: e.reciprocal(cst[:, 2, :, :], cst[:, 1, :, :]), t)
            tn = []
            for hd in range(2):
                for qb in range(NB):
                    g = gates[:, qb, 3 * (2 * pair + hd):][:, 0:1]
                    tn.append(c.dve(lambda e, hd=hd, qb=qb, g=g: e.tensor_scalar(
                        pc[:, hd, qb, 0:N_CMP], pc[:, hd, qb, 0:N_CMP], cst[:, 2, hd, qb:qb + 1], g, ALU.mult, ALU.mult), t, rv))
            pt = c.acc[:, 0:2, :].rearrange("p a b -> p (a b)")

            def turn(e):
                for hd in range(2):
                    for qb in range(NB):
                        i = e.transpose(pt[0:N_CMP, (2 * hd + qb) * P:][:, 0:P], pc[:, hd, qb, 0:N_CMP], ident)
                return i
            t = c.pe(turn, tn, c.h_pt2[0])
            t = c.act(lambda e: e.activation(pct[:, :, :], pt[0:N_CMP, :].rearrange("p (h q) -> p h q", h=2), ACT.Copy),
                      t, h_pct)
            c.h_pt2[0].give(t)
            return t

        h_pct = Hand(c)
        for pair in range(2):
            ready = [r_q, rk, thk]
            ws = []
            for kind in range(2):
                def scores(hd, qb, z, kind=kind, pair=pair):
                    h = 2 * pair + hd
                    return [(z, qn[:, h, qb * P:(qb + 1) * P], kw_[:, kind, 0:(qb + 1) * P], True, False), bias(z, h, qb)]
                gate = lambda hd, qb, kind=kind, pair=pair: gates[:, qb, 3 * (2 * pair + hd) + 1 + kind:][:, 0:1]
                ws.append(finish(c.softmax_pair(scores, True, norm=gate, ready=[ready, rv])))
            tc_ = compressed(pair, [ready, tkc])
            ob = c.acc[:, 4 + 2 * pair:6 + 2 * pair, :]
            for hd in range(2):
                calls = [(ob[0:64, hd, :], vc[:, :], pct[:, hd, :], True, False)]
                for kind in range(2):
                    for kb in range(NB):
                        q0 = 128 * kb
                        calls.append((ob[0:64, hd, q0:256], vw_[:, kb, kind, :],
                                      c.wk[:, kind, hd, kb * 256:kb * 256 + 256 - q0], False, kind + kb == 2))
                t = c.mms(calls, [w[1] for w in ws], tc_, tvc, rv, c.h_o[pair] if hd == 0 else None)
            c.h_wk[0].give(t), c.h_wk[1].give(t), h_pct.give(t)
            c.h_o[pair].give(take(pair)(ob, t))
        for pair in range(2):
            def scores(hd, qb, z, pair=pair):
                h = 2 * pair + hd
                return [(z, qm[:, h, qb * P:(qb + 1) * P], kmo[:, h, 0:(qb + 1) * P], True, False), bias(z, 4 + h, qb)]
            side, tw = finish(c.softmax_pair(scores, True, ready=[r_m, thk]))
            c.values_pair(side, [tw, r_m], lambda hd, kb, pair=pair: vmo[:, kb, (2 * pair + hd) * 64:][:, 0:64],
                          True, 64, take(2 + pair))
        c.barrier()
        c.ctx = outer


def conv3(c, w3, mix):
    with ExitStack() as own:
        outer, c.ctx = c.ctx, own
        hp = c.sb("conv_in", [P, 2, S + TAPS - 1])
        sg, cv, sq = (c.sb(f"conv_{n}", [P, 2, S]) for n in ("gate", "out", "sq"))
        pw = c.sb("conv_pw", [P, 2, 256])
        tp = c.load(pw[:, :, :], c.aps["conv_pw"], engine="scalar", name="conv_pw")
        tz = c.pool(lambda e: e.memset(hp[:, :, 0:TAPS - 1], 0.0))

        def copy_in(t, ps, r, f):
            x = c.dve(lambda e: e.tensor_copy(hp[:, t, TAPS - 1:], ps[:, 0:S]), r)
            f.give(x)
            return x

        def gate(t, ps, r, f):
            x = c.act(lambda e: e.activation(sg[:, t, :], ps[:, 0:S], ACT.Sigmoid), r)
            f.give(x)
            return x
        a = c.project(lambda _, n: w3(CONV_A)(), 1, None, copy_in)
        g = c.project(lambda _, n: w3(CONV_G)(), 1, None, gate)
        t = c.dve(lambda e: e.tensor_tensor(hp[:, :, TAPS - 1:], hp[:, :, TAPS - 1:], sg[:, :, :], ALU.mult), a, g)
        t = [c.dve(lambda e, q=q: e.tensor_scalar(cv[:, q, :], hp[:, q, 0:S], c.col(("conv_dw_w_3", (0, 0)), q),
                                                  c.col(("conv_dw_b_3", 0), q), ALU.mult, ALU.add), t, tz) for q in range(2)]
        for j in range(1, TAPS):
            t = [c.dve(lambda e, q=q, j=j: e.scalar_tensor_tensor(
                out=cv[:, q, :], in0=hp[:, q, j:j + S], scalar=c.col(("conv_dw_w_3", (0, j)), q), in1=cv[:, q, :],
                op0=ALU.mult, op1=ALU.add), t[q]) for q in range(2)]
        t = c.layer_norm(cv, 2, lambda k: c.col(("conv_ln_g_3", 0), k), lambda k: c.col(("conv_ln_b_3", 0), k), cv, t, sq,
                         mat="mean_256")
        t = c.act(lambda e: e.activation(cv[:, :, :], cv[:, :, :], ACT.Silu), t)
        for q in range(2):
            t2 = c.mms([(c.bank[q][:, 0:S], pw[:, k, q * P:(q + 1) * P], cv[:, k, :], k == 0, k == 1) for k in range(2)],
                       t, tp, c.hb[q])
            t2 = c.dve(lambda e, q=q: e.tensor_copy(mix[:, 4 + q, :], c.bank[q][:, 0:S]), t2)
            c.hb[q].give(t2)
        c.barrier()
        c.ctx = outer


def hgrn3(c, w3, mix):
    with ExitStack() as own:
        outer, c.ctx = c.ctx, own
        PAD = CHUNK
        t3 = lambda n: c.sb(f"hgrn_{n}", [P, 2, S])
        qT, kT_, eU, eA, F, pr, qp, gT, o, kh = (t3(n) for n in ("q", "k", "e_from_start", "e_to_end", "decay", "pairs",
                                                                "pairs_q", "gate", "o", "k_to_end"))
        kp, fp, vp = (c.sb(f"hgrn_{n}_padded", [P, 2, PAD + S]) for n in ("k", "f", "v"))
        lf, lf2 = c.sb("hgrn_log_f", [P, NB, 256]), c.sb("hgrn_log_f_t", [P, NB, 256])
        vt, kt = c.sb("hgrn_v_tok", [P, NB, 256]), c.sb("hgrn_k_tok", [P, NB, 256])
        vx = c.sb("hgrn_v_by_chunk", [P, 2, 8, 64])
        Hc, St = c.sb("hgrn_H", [P, 2, NCH, 64]), c.sb("hgrn_S", [P, 2, NCH, 64])
        pv_ = c.sb("hgrn_part", [P, 2, S])
        tz = [c.pool(lambda e, x=x: e.memset(x[:, :, 0:PAD], 0.0)) for x in (kp, fp, vp)]

        def to(dst, func=ACT.Copy):
            def take(t, ps, r, f):
                x = c.act(lambda e: e.activation(dst[:, t, :], ps[:, 0:S], func), r)
                f.give(x)
                return x
            return take
        rq = c.project(lambda _, n: w3(Q_H)(), 1, None, to(qT))

        def both(start, take, tok_dst):
            ap, tok = c.unit(w3(start))
            out = []
            for q in range(2):
                t = c.tile_T(ap, q, tok, c.x, None, c.bank[q][:, 0:S], c.hb[q])
                out.append(take(q, c.bank[q], t, c.hb[q]))
            for b in range(NB):
                t = c.tile_tok(ap, b, tok, c.x, None, c.bank[2 + b][:, 0:S], c.hb[2 + b], release=b == 1)
                t = c.dve(lambda e, b=b: e.tensor_copy(tok_dst[:, b, :], c.bank[2 + b][:, 0:S]), t)
                c.hb[2 + b].give(t)
                out.append(t)
            return out
        rf = both(F_H, to(fp[:, :, PAD:], ACT.Sigmoid), lf)
        ri = both(I_H, to(vp[:, :, PAD:]), vt)
        rg = c.project(lambda _, n: w3(G_H)(), 1, None, to(gT, ACT.Sigmoid))
        tk = c.dve(lambda e: e.tensor_scalar(kp[:, :, PAD:], fp[:, :, PAD:], -1.0, 1.0, ALU.mult, ALU.add), rf)
        tf = c.dve(lambda e: e.memset(fp[:, :, :].rearrange("p a (n t) -> p a n t", t=CHUNK)[:, :, :, 0:1], 0.0), tk, tz)
        a = c.act(lambda e: e.activation(lf2[:, :, :], lf[:, :, :], ACT.Abs), rf)
        a = c.act(lambda e: e.activation(lf2[:, :, :], lf2[:, :, :], ACT.Exp, scale=-1.0), a)
        a = c.act(lambda e: e.activation(lf2[:, :, :], lf2[:, :, :], ACT.Ln, bias=c.eps(1.0)), a)
        tl = c.dve(lambda e: e.scalar_tensor_tensor(out=lf[:, :, :].rearrange("p a b -> p (a b)"),
                                                    in0=lf[:, :, :].rearrange("p a b -> p (a b)"), scalar=0.0,
                                                    in1=lf2[:, :, :].rearrange("p a b -> p (a b)"),
                                                    op0=ALU.min, op1=ALU.subtract), a)
        ex = []
        for i, (m, dst) in enumerate((("chunk_upto", eU), ("chunk_after", eA))):
            t = c.mms([(c.bank[i][:, q * S + b * P:][:, 0:P], lf[:, b, q * P:(q + 1) * P], c.con(m), q + b == 0, True)
                       for q in range(2) for b in range(NB)], tl, c.hb[i])
            t = c.act(lambda e, i=i, dst=dst: e.activation(dst[:, :, :].rearrange("p a b -> p (a b)"), c.bank[i][:, :],
                                                           ACT.Exp), t)
            c.hb[i].give(t)
            ex.append(t)
        tkh = c.dve(lambda e: e.tensor_tensor(kh[:, :, :], kp[:, :, PAD:], eA[:, :, :], ALU.mult), ex, tk)
        tqs = c.dve(lambda e: e.tensor_tensor(eA[:, :, :], qT[:, :, :], eU[:, :, :], ALU.mult), tkh, rq, ex)

        def turn(e):
            for q in range(2):
                for b in range(NB):
                    i = e.transpose(c.bank[2][:, b * S + q * P:][:, 0:P], kh[:, q, b * P:(b + 1) * P], c.con("identity"))
            return i
        t = c.pe(turn, tkh, c.hb[2])
        tkt = c.act(lambda e: e.activation(kt[:, :, :].rearrange("p a b -> p (a b)"), c.bank[2][:, :], ACT.Copy), t)
        c.hb[2].give(tkt)
        th = []
        h_vx = [Hand(c) for _ in range(2)]
        for hd in range(4):
            for b in range(NB):
                i, R, q = b, slice(64 * (hd % 2), 64 * (hd % 2) + 64), hd // 2
                s = c.pool(lambda e, hd=hd, b=b, i=i: e.tensor_tensor(
                    vx[:, i, :, :], vt[:, b, hd * 64:(hd + 1) * 64].unsqueeze(1).to_broadcast([P, 8, 64]),
                    c.con("chunk_of")[:, 0:8].unsqueeze(2).to_broadcast([P, 8, 64]), ALU.mult), ri, h_vx[i])
                n = 2 + i
                t = c.mms([(c.bank[n][:, :], kt[:, b, q * P:(q + 1) * P], vx[:, i, :, :].rearrange("p n j -> p (n j)"),
                            True, True)], s, tkt, c.hb[n])
                h_vx[i].give(t)
                t = c.act(lambda e, R=R, q=q, b=b, n=n: e.activation(
                    Hc[R, q, 8 * b:8 * b + 8, :].rearrange("p n j -> p (n j)"), c.bank[n][R, :], ACT.Copy), t)
                c.hb[n].give(t)
                th.append(t)
        t = c.dve(lambda e: e.memset(St[:, :, 0, :], 0.0))
        ts = [t, t]
        for n in range(NCH - 1):
            ts = [c.dve(lambda e, q=q, n=n: e.scalar_tensor_tensor(
                out=St[:, q, n + 1, :], in0=St[:, q, n, :], scalar=eU[:, q, (n + 1) * CHUNK - 1:(n + 1) * CHUNK],
                in1=Hc[:, q, n, :], op0=ALU.mult, op1=ALU.add), ts[q], th, ex) for q in range(2)]
        ob = c.acc[:, 0:2, :]
        ty = c.mms([(ob[64 * hd:64 * hd + 64, q, n * CHUNK:(n + 1) * CHUNK], St[64 * hd:64 * hd + 64, q, n, :],
                     eA[64 * hd:64 * hd + 64, q, n * CHUNK:(n + 1) * CHUNK], True, True)
                    for q in range(2) for n in range(NCH) for hd in range(2)], ts, tqs)
        ab = c.acc[:, 2:4, :]
        h_ab, h_qp, h_pv = Hand(c), Hand(c), Hand(c)

        def distance(q_ready, vsh, first):
            t = c.mms([(ab[:, q, :], c.con("head_sum"), qp[:, q, :], q == 0, True) for q in range(2)], q_ready, h_ab)
            h_qp.give(t)
            if first:
                m = c.dve(lambda e: e.tensor_tensor(o[:, :, :], ab, vsh(), ALU.mult), t, ri)
                h_ab.give(m)
                return m
            m = c.dve(lambda e: e.tensor_tensor(pv_[:, :, :], ab, vsh(), ALU.mult), t, h_pv)
            h_ab.give(m)
            a = c.pool(lambda e: e.tensor_tensor(o[:, :, :], o[:, :, :], pv_[:, :, :], ALU.add), m, h_o)
            h_pv.give(a)
            return a
        h_o = Hand(c)
        t = c.pool(lambda e: e.tensor_tensor(qp[:, :, :], kp[:, :, PAD:], qT[:, :, :], ALU.mult), tk, rq)
        h_o.give(distance(t, lambda: vp[:, :, PAD:], True))
        tF = c.dve(lambda e: e.memset(F[:, :, :], 1.0), tf)
        h_F, h_pr = Hand(c), Hand(c)
        h_F.give(tF)
        with c.repeat(CHUNK - 1) as dist:
            tF = c.dve(lambda e: e.tensor_tensor(F[:, :, :], F[:, :, :], fp[:, :, bass.ds(dist.cur * -1 + PAD, S)], ALU.mult), h_F)
            h_F.give(tF)
            t = c.dve(lambda e: e.tensor_tensor(pr[:, :, :], F[:, :, :], kp[:, :, bass.ds(dist.cur * -1 + (PAD - 1), S)], ALU.mult),
                      tF, h_pr)
            t = c.pool(lambda e: e.tensor_tensor(qp[:, :, :], pr[:, :, :], qT[:, :, :], ALU.mult), t, h_qp)
            h_pr.give(t)
            h_o.give(distance(t, lambda: vp[:, :, bass.ds(dist.cur * -1 + (PAD - 1), S)], False))
        c.barrier()
        t = c.dve(lambda e: e.tensor_tensor(o[:, :, :], o[:, :, :], ob, ALU.add), ty)
        t = c.act(lambda e: e.activation(pr[:, :, :], o[:, :, :], ACT.Square), t)
        t = c.mms([(ab[:, q, :], c.con("head_mean"), pr[:, q, :], q == 0, True) for q in range(2)], t)
        t = c.act(lambda e: e.activation(pr[:, :, :], ab, ACT.Sqrt, bias=c.eps(1e-6)), t)
        t = c.dve(lambda e: e.reciprocal(pr[:, :, :], pr[:, :, :]), t)
        t = c.dve(lambda e: e.tensor_tensor(pr[:, :, :], pr[:, :, :], gT[:, :, :], ALU.mult), t)
        for q in range(2):
            c.dve(lambda e, q=q: e.scalar_tensor_tensor(out=mix[:, 6 + q, :], in0=o[:, q, :],
                                                        scalar=c.col(("hgrn_norm_g_3", 0), q), in1=pr[:, q, :],
                                                        op0=ALU.mult, op1=ALU.mult), t)
        c.barrier()
        c.ctx = outer


def lay_unit(inputs, what):
    out = np.zeros((P, UNIT), np.float32)
    if what is None:
        return out
    kind, name, index, start = what
    if kind in ("side", "stack"):
        for n, x in enumerate(name):
            x = inputs[x][index]
            if kind == "stack":
                out.reshape(P, 2, D)[:x.shape[0], n] = x
            else:
                w = x.shape[1]
                out.reshape(P, KT, 256)[:, :, n * w:(n + 1) * w] = x.reshape(KT, P, w).transpose(1, 0, 2)
        return out
    w = inputs[name][index]
    if kind == "rows":
        part = w[start:start + 256]
        part = np.concatenate([part, np.zeros((256 - len(part), part.shape[1]), np.float32)])
    else:
        part = w[:, start:start + UNIT * P // w.shape[0]]
    k = part.shape[0] // P
    out.reshape(P, k, UNIT // k)[:, :, :part.shape[1]] = part.reshape(k, P, -1).transpose(1, 0, 2)
    return out


def feature_major(a):
    return np.ascontiguousarray(a.reshape(a.shape[0], -1, P).transpose(2, 1, 0))


def small_inputs(inputs):
    columns = np.concatenate([np.asarray(inputs[n][i]).reshape(-1, P) for n, i in VECTORS]).T
    wf = inputs["w_in"][:, :, F_FX:F_FX + HEADS].reshape(L1, KT, P, HEADS).transpose(2, 0, 1, 3)
    hot, mask = bucket_constants()
    w2 = inputs["nsa_cmp_w2_3"][0].reshape(2, 2, P, 64).transpose(2, 0, 1, 3)
    return {
        "bias_one_hot": hot,
        "bias_mask": mask,
        "bias_table": np.ascontiguousarray(inputs["rel_bias_3"].T),
        "cmp_w2": np.ascontiguousarray(w2),
        "conv_pw": np.ascontiguousarray(inputs["conv_pw_w_3"][0].reshape(2, P, 256).transpose(1, 0, 2)),
        "columns": np.ascontiguousarray(columns),
        "shape_constants": np.concatenate([np.asarray(MATS[n], np.float32) for n in CONS], axis=1),
        "w_forget": np.ascontiguousarray(wf.reshape(P, -1)),
        "b_forget_rows": np.ascontiguousarray(np.broadcast_to(inputs["b_forget"].reshape(1, -1), (P, L1 * HEADS))),
        "sgu_w_spatial": np.ascontiguousarray(inputs["sgu_w_sp_2"][0].transpose(2, 0, 1)),
        "sgu_b_spatial": inputs["sgu_b_sp_2"][0],
        "rwkv_w0_row": inputs["rwkv_w0_2"],
        "memory": feature_major(inputs["mem"][0]),
        "x": feature_major(inputs["x"][0]),
    }


def build(nc, small, blocks):
    aps = {n: nc.dram_tensor(f"in_{n}", a.shape, F32, kind="ExternalInput").ap() for n, a in small.items()}
    out = nc.dram_tensor("out", (P, KT, S), F32, kind="ExternalOutput").ap()
    with ExitStack() as ctx:
        c = Core(nc, ctx, aps)
        c.everyone_waits([c.load(c.h[:, :, :], aps["x"], name="x")])
        c.at["sync"].append(("raw", lambda e: c.stream()(e)))
        for b in blocks:
            b(c)
        c.pad_units(end=True)
        aps["weights"] = nc.dram_tensor("in_weights", (c.n_units, P, UNIT), F32, kind="ExternalInput").ap()
        t = c.load(out, c.h[:, :, :], c.now(), name="out")
        c.at["sync"].append(("wait", [t]))
        c.emit()
    return [w() for w in c.plan]


BLOCKS = [block1, block2, block3]


def kernel(**inputs):
    import concourse.bacc as bacc
    from concourse.bass_utils import run_bass_kernel_spmd

    nc = bacc.Bacc("TRN2", target_bir_lowering=False, num_devices=1)
    inputs = {k: np.asarray(v) for k, v in inputs.items()}
    small = small_inputs(inputs)
    plan = build(nc, small, BLOCKS)
    weights = np.stack([lay_unit(inputs, w) for w in plan])
    got = run_bass_kernel_spmd(nc, [{f"in_{n}": a for n, a in {**small, "weights": weights}.items()}], core_ids=[0]).results[0]["out"]
    return np.ascontiguousarray(got.transpose(2, 1, 0)).reshape(1, S, D)
```

```python
from contextlib import ExitStack, contextmanager

import numpy as np
import concourse.bass as bass
from concourse import mybir

F32 = mybir.dt.float32
F32R = mybir.dt.float32r
ALU = mybir.AluOpType
ACT = mybir.ActivationFunctionType
AX = mybir.AxisListType.X

P = 128
D = 1024
KT = D // P
S = 256
NB = S // P
DFF = 2816
RING = 3
TURN = 6
UNIT = 2048
CREDIT = 512


class Loop:

    def __init__(self, n, parent):
        self.n, self.parent, self.entry, self.stride, self.cur = n, parent, {}, {}, None


class Count:

    def __init__(self, sem, start=0):
        self.sem, self.off = sem, start


class Tok:

    def __init__(self, count, off, loop, back=0):
        self.count, self.off, self.loop, self.back = count, off, loop, back

    def value(self, inside):
        v, s, back = self.off, self.loop, self.back
        while s is not None:
            if s in inside:
                v = v + s.entry[self.count] + (s.cur - back) * s.stride[self.count]
            else:
                v = v + s.entry[self.count] + (s.n - 1) * s.stride[self.count]
            back, s = 0, s.parent
        return v


class Prog:

    ENGINES = ("tensor", "scalar", "vector", "gpsimd", "sync")

    def __init__(self, nc, ctx):
        self.nc, self.ctx = nc, ctx
        self.queues = {e: [] for e in self.ENGINES}
        self.at = {e: self.queues[e] for e in self.ENGINES}
        self.counts, self.hands, self.loop = [], [], None
        self.low = self.count("s_units_split", CREDIT)
        self.main = {e: self.count(f"s_{e}", CREDIT) for e in self.ENGINES[:4]}

    def count(self, name, start=0):
        c = Count(self.ctx.enter_context(self.nc.semaphore(name)), start)
        self.counts.append(c)
        return c

    def op(self, engine, fn, *waits, count=None, inc=1):
        c = count or self.main[engine]
        c.off += inc
        self.at[engine].append(("op", fn, flat(waits), c, inc))
        return Tok(c, c.off, self.loop)

    def pe(self, fn, *w):
        return self.op("tensor", fn, *w)

    def mms(self, calls, *w):
        def fn(e):
            for out, x, y, start, stop in calls:
                if isinstance(x, Pair):
                    e.matmul(out, x.hi, y.hi, start=start, stop=False, skip_group_check=True)
                    e.matmul(out, x.hi, y.lo, start=False, stop=False, skip_group_check=True)
                    last = e.matmul(out, x.lo, y.hi, start=False, stop=stop, skip_group_check=True)
                else:
                    last = e.matmul(out, x, y, start=start, stop=stop, skip_group_check=True)
            return last

        return self.op("tensor", fn, *w)

    def act(self, fn, *w):
        return self.op("scalar", fn, *w)

    def dve(self, fn, *w):
        return self.op("vector", fn, *w)

    def pool(self, fn, *w):
        return self.op("gpsimd", fn, *w)

    def load(self, out, in_, *w, engine="sync", name="ld"):
        c = self.count(f"d_{name}_{len(self.counts)}")
        return self.op(engine, lambda e: e.dma_start(out, in_), *w, count=c, inc=16)

    def now(self):
        return [Tok(c, c.off, self.loop) for c in self.main.values()]

    def barrier(self):
        w = self.now()
        for e in self.ENGINES[:4]:
            self.at[e].append(("wait", w))

    @contextmanager
    def repeat(self, n):
        loop = Loop(n, self.loop)
        saved = dict(self.at)
        for e in self.ENGINES:
            body = []
            self.at[e].append(("loop", loop, body))
            self.at[e] = body
        for c in self.counts:
            loop.entry[c], c.off = c.off, 0
        self.loop = loop
        yield loop
        for h in self.hands:
            h.close(loop)
        for c in self.counts:
            if c not in loop.entry:
                loop.entry[c] = 0
            loop.stride[c] = c.off
            c.off = loop.entry[c] + n * c.off
        self.loop = loop.parent
        self.at = saved

    def emit(self):
        block = self.ctx.enter_context(self.nc.Block())
        for name in self.ENGINES:
            enter = {"tensor": block.tensor, "scalar": block.scalar, "vector": block.vector,
                        "gpsimd": block.gpsimd, "sync": block.sync}[name]

            def body(eng, name=name):
                if name in self.main:
                    eng.sem_inc(self.main[name].sem, CREDIT)
                if name == "vector":
                    eng.sem_inc(self.low.sem, CREDIT)
                self.walk(eng, self.queues[name], [])

            enter(body)

    def walk(self, eng, nodes, inside):
        seen = {}

        def wait(t):
            if t.count.off == 0 and t.off == 0:
                return
            key = (t.count, t.loop, t.back)
            if seen.get(key, -1) >= t.off:
                return
            seen[key] = t.off
            eng.wait_ge(t.count.sem, t.value(inside))

        for node in nodes:
            if node[0] == "wait":
                for t in latest(node[1]):
                    wait(t)
            elif node[0] == "raw":
                node[1](eng)
            elif node[0] == "op":
                _, fn, waits, c, inc = node
                for t in latest(waits):
                    wait(t)
                fn(eng).then_inc(c.sem, inc)
            else:
                _, loop, body = node
                if has_ops(body):
                    with eng.Fori(0, loop.n) as i:
                        loop.cur = i
                        self.walk(eng, body, inside + [loop])
                    loop.cur = None


class Pair:

    def __init__(self, hi, lo):
        self.hi, self.lo = hi, lo

    def __getitem__(self, i):
        return Pair(self.hi[i], self.lo[i])

    def rearrange(self, *a, **k):
        return Pair(self.hi.rearrange(*a, **k), self.lo.rearrange(*a, **k))


def has_ops(nodes):
    return any(n[0] in ("op", "wait") or has_ops(n[2]) for n in nodes)


def flat(ws):
    out = []
    for w in ws:
        if isinstance(w, (list, tuple)):
            out += flat(w)
        elif isinstance(w, Hand):
            out += w.take()
        elif w is not None:
            out.append(w)
    return out


def latest(waits):
    best = {}
    for t in waits:
        if isinstance(t, Later):
            for u in t.toks:
                k = (u.count, u.loop, u.back)
                if k not in best or best[k].off < u.off:
                    best[k] = u
            continue
        k = (t.count, t.loop, t.back)
        if k not in best or best[k].off < t.off:
            best[k] = t
    return list(best.values())


class Later:

    def __init__(self):
        self.toks = []


class Hand:

    def __init__(self, prog):
        self.prog, self.toks, self.open = prog, [], []
        prog.hands.append(self)

    def take(self):
        loop, out = self.prog.loop, list(self.toks)
        if loop is not None and not any(t.loop is loop for t in self.toks):
            later = Later()
            self.open.append((loop, later))
            out.append(later)
        return out

    def give(self, *toks):
        self.toks = flat(toks)
        return self.toks

    def close(self, loop):
        for l, later in self.open:
            if l is loop:
                later.toks = [Tok(t.count, t.off, t.loop, 1) for t in self.toks if t.loop is loop]
        self.open = [(l, x) for l, x in self.open if l is not loop]


def shape_constants():
    r = np.arange(P)
    row, colm = r[:, None], r[None, :]
    one = np.ones((P, P))
    chunk = row // 16 == colm // 16
    mats = {
        "identity": row == colm,
        "mean": one / D,
        "mean_half": one / (2 * D),
        "after": row > colm,
        "ones": one,
        "mean_256": one / 256,
        "upto": row <= colm,
        "before": row < colm,
        "not_before": np.where(row < colm, -1e30, 0),
        "head_sum": row // 64 == colm // 64,
        "head_mean": (row // 64 == colm // 64) / 64,
        "chunk_of": row // 16 == colm,
        "chunk_upto": chunk & (row <= colm),
        "chunk_before": chunk & (row < colm),
        "chunk_after": chunk & (row > colm),
        "chunk_all": chunk,
        "identity_pair": row % 64 == colm,
        "flip": row + colm == P - 1,
        "head_of": colm % 16 == 2 * (colm // 16) + row // 64,
    }
    return mats


MATS = shape_constants()
CONS = list(MATS)

EPS = [1e-6, 1e-5, 4e-5, 64e-5, 1.0]

def vectors():
    out = []
    for l in range(2):
        out += [("ffn1_pre_g", l), ("ffn1_post_g", l), ("mix_pre_g", l), ("mix_post_g", l), ("b_gate", l),
                ("ffn2_pre_g", l), ("ffn2_post_g", l)]
    out += [("mem_norm_g", ())]
    out += [(f"ln_{x}_2", (i, j)) for i in range(2) for j in range(3) for x in "gb"]
    out += [(n, 0) for n in ("sgu_b_in_2", "sgu_ln_g_2", "sgu_ln_b_2")]
    out += [("rwkv_mu_2", (0, j)) for j in range(6)]
    out += [(f"rwkv_{n}_2", 0) for n in ("w0", "a0", "k_k", "k_a", "r_k", "gn_g", "gn_b")]
    out += [("conv_dw_w_3", (0, j)) for j in range(31)]
    out += [(n, 0) for n in ("conv_dw_b_3", "conv_ln_g_3", "conv_ln_b_3", "hgrn_norm_g_3", "ln1_g_3", "ln1_b_3",
                             "ln2_g_3", "ln2_b_3")]
    out += [("nsa_cmp_b1_3", (0, j)) for j in range(2)]
    out += [("nsa_cmp_pe_3", (0, j)) for j in range(2)]
    return out


SIZES = {"b_gate": 3072, "sgu_b_in_2": 4096, "sgu_ln_g_2": 2048, "sgu_ln_b_2": 2048, "conv_dw_w_3": 256,
         "conv_dw_b_3": 256, "conv_ln_g_3": 256, "conv_ln_b_3": 256, "hgrn_norm_g_3": 256, "nsa_cmp_b1_3": 256,
         "nsa_cmp_pe_3": 2048}
VECTORS = vectors()
COLS, N_COLS = {}, 0
for _name, _index in VECTORS:
    COLS[_name, _index] = N_COLS
    N_COLS += SIZES.get(_name, D) // P
COLS["mem_norm_g"] = COLS["mem_norm_g", ()]


class Core(Prog):

    def __init__(self, nc, ctx, aps):
        super().__init__(nc, ctx)
        self.aps = aps
        self.plan, self.n_units = [], 0
        self.slot = [self.count(f"s_weight_slot{k}") for k in range(RING)]
        self.ring = self.sb("weight_ring", [P, RING, UNIT])
        self.w = Pair(*(self.sb(f"weights_{x}", [P, 2, UNIT], F32R) for x in ("hi", "lo")))
        self.w_ready = [Hand(self) for _ in range(2)]
        self.w_read = [Hand(self) for _ in range(2)]
        self.n_split, self.held = 0, False
        self.bank = [self.ps(f"bank{i}", [P, 512]) for i in range(4)]
        self.acc = self.ps("acc", [P, KT, S])
        self.hb = [Hand(self) for _ in range(4)]
        self.h = self.sb("h", [P, KT, S])
        self.xn = self.sb("xn", [P, KT, S])
        self.tmp = self.sb("tmp", [P, KT, S])
        self.rstd = self.sb("rstd", [P, S])
        self.act_gate = self.sb("act_gate", [P, 2, S])
        self.hidden = self.sb("hidden", [P, 2, S])
        self.h_gate = [Hand(self) for _ in range(2)]
        self.h_tmp = [Hand(self) for _ in range(KT)]
        self.cons = self.sb("cons", [P, len(CONS) * P])
        self.pv = self.sb("pv", [P, N_COLS])
        self.epsc = self.sb("epsc", [P, len(EPS)])
        start = [self.load(self.cons[:, :], aps["shape_constants"], name="cons"),
                 self.load(self.pv[:, :], aps["columns"], engine="scalar", name="pv")]
        start += [self.pool(lambda e, i=i, v=v: e.memset(self.epsc[:, i:i + 1], v)) for i, v in enumerate(EPS)]
        self.everyone_waits(start)

    def everyone_waits(self, toks):
        for e in self.ENGINES[:4]:
            self.at[e].append(("wait", toks))

    def sb(self, name, shape, dt=F32):
        return self.ctx.enter_context(self.nc.sbuf_tensor(name, shape, dt))

    def ps(self, name, shape):
        return self.ctx.enter_context(self.nc.psum_tensor(name, shape, F32))

    def con(self, name):
        i = CONS.index(name)
        return self.cons[:, i * P:(i + 1) * P]

    def col(self, name, k=0, n=1):
        c = COLS[name] + k
        return self.pv[:, c:c + n]

    def eps(self, v):
        i = EPS.index(v)
        return self.epsc[:, i:i + 1]

    def unit(self, what, a=KT, last=False):
        assert not self.held
        self.held = True
        while self.n_split < self.n_units + (1 if last else 2):
            self.split_unit()
        j = self.n_units % 2
        self.n_units += 1
        self.plan.append(what)
        return self.w[:, j, :].rearrange("p (a b) -> p a b", a=a), self.w_ready[j].take()

    def split_unit(self):
        k, j = self.n_split % RING, self.n_split % 2
        self.n_split += 1
        self.slot[k].off += 16
        arrived = Tok(self.slot[k], self.slot[k].off, self.loop)
        w, raw = self.w[:, j, :], self.ring[:, k, :]
        hi = self.act(lambda e: e.activation(w.hi, raw, ACT.Copy), arrived, self.w_read[j])
        lo = self.op("vector", lambda e: e.tensor_tensor(w.lo, raw, w.hi, ALU.subtract), hi, count=self.low)
        self.w_ready[j].give(lo)

    def mms(self, calls, *w, release=False):
        t = super().mms(calls, *w)
        if release:
            self.w_read[(self.n_units - 1) % 2].give(t)
            self.held = False
        return t

    @contextmanager
    def repeat(self, n):
        while self.n_split <= self.n_units:
            self.split_unit()
        plan, self.plan = self.plan, []
        first, ahead = self.n_units, self.n_split - self.n_units
        with super().repeat(n) as loop:
            yield loop
        body = self.plan
        assert len(body) % TURN == 0 and self.n_split - self.n_units == ahead, (len(body), ahead)
        self.n_units = first + n * len(body)
        self.n_split = self.n_units + ahead
        self.plan = plan + [(lambda *o, i=i, w=w: w(*o, i)) for i in range(n) for w in body]

    def pad_units(self, start=0, end=False):
        while (self.n_units - start) % TURN or end:
            last = end and (self.n_units - start) % TURN == TURN - 1
            ap, tok = self.unit(lambda *_: None, last=last)
            t = self.mms([(self.bank[0][:, 0:8], ap[:, 0, 0:P], ap[:, 0, 0:8], True, True)],
                         tok, self.hb[0], release=True)
            self.hb[0].give(t)
            if last:
                break

    def stream(self):
        w, slots = self.aps["weights"], [(self.ring[:, k, :], self.slot[k].sem) for k in range(RING)]

        def run(e):
            for k in range(RING):
                e.dma_start(slots[k][0], w[k]).then_inc(slots[k][1], 16)
            with e.Fori(1, self.n_units // RING) as turn:
                for k in range(RING):
                    e.wait_ge(self.low.sem, (turn - 1) * RING + (CREDIT + k + 1))
                    e.dma_start(slots[k][0], w[turn * RING + k]).then_inc(slots[k][1], 16)
        return run

    def operands(self, of, hidden=2):
        self.x = Pair(*(self.sb(f"{of}_x_{n}", [P, KT, S], F32R) for n in ("hi", "lo")))
        if hidden:
            self.hidden_buffers(of, hidden)

    def hidden_buffers(self, of, hidden):
        self.hid = Pair(*(self.sb(f"{of}_hidden_{n}", [P, hidden, 2, S], F32R) for n in ("hi", "lo")))
        self.h_hid = [[Hand(self) for _ in range(2)] for _ in range(hidden)]

    @contextmanager
    def scope(self):
        with ExitStack() as own:
            outer, self.ctx = self.ctx, own
            yield
            self.ctx = outer

    def split(self, src, dst, ready, n=KT, step=2, free=None):
        parts = Parts(self, src, dst, step, free)
        for k in range(0, n, step):
            parts.high(k, ready[k:k + step] if isinstance(ready, list) and len(ready) == n else ready)
            parts.low()
        return parts.out

    def tile_T(self, ap, c, tok, src, ready, out, w, kt=KT, release=False):
        if isinstance(ready, list) and len(ready) == kt:
            for k in range(kt):
                t = self.mms([(out, ap[:, k, c * P:(c + 1) * P], src[:, k, :], k == 0, k == kt - 1)],
                             tok, ready[k], w if k == 0 else None, release=release and k == kt - 1)
            return t
        return self.mms([(out, ap[:, k, c * P:(c + 1) * P], src[:, k, :], k == 0, k == kt - 1)
                         for k in range(kt)], tok, ready, w, release=release)

    def tile_tok(self, ap, b, tok, src, ready, out, w, width=256, release=False):
        return self.mms([(out, src[:, k, b * P:(b + 1) * P], ap[:, k, 0:width], k == 0, k == KT - 1)
                         for k in range(KT)], tok, ready, w, release=release)

    def ffn(self, gate, up, down, ready):
        depth, p = 0, self.loop
        while p is not None:
            depth, p = depth + 1, p.parent

        def make(j, par):
            g, tg = self.unit(lambda *i: gate(i[:depth], j(*i[depth:])))
            for c in range(2):
                t = self.tile_T(g, c, tg, self.x, ready, self.bank[c][:, 0:S], self.hb[c], release=c == 1)
                s = self.act(lambda e, c=c: e.activation(self.act_gate[:, c, :], self.bank[c][:, 0:S], ACT.Silu),
                             t, self.h_gate[c])
                self.hb[c].give(s), self.h_gate[c].give(s)
            u, tu = self.unit(lambda *i: up(i[:depth], j(*i[depth:])))
            for c in range(2):
                t = self.tile_T(u, c, tu, self.x, ready, self.bank[2 + c][:, 0:S], self.hb[2 + c], release=c == 1)
                m = self.dve(lambda e, c=c: e.tensor_tensor(self.act_gate[:, c, :], self.bank[2 + c][:, 0:S],
                                                            self.act_gate[:, c, :], ALU.mult), t, self.h_gate[c])
                self.hb[2 + c].give(m)
                self.hidden_parts(self.act_gate, par, c, m)

        def use(j, par, first=False):
            d, td = self.unit(lambda *i: down(i[:depth], j(*i[depth:])), a=2)
            return self.add_down(d, td, par, first)

        make(lambda: 0, 0)
        make(lambda: 1, 1)
        use(lambda: 0, 0, first=True)
        make(lambda: 2, 0)
        use(lambda: 1, 1)
        with self.repeat(4):
            make(lambda i: 3 + 2 * i, 1)
            use(lambda i: 2 + 2 * i, 0)
            make(lambda i: 4 + 2 * i, 0)
            use(lambda i: 3 + 2 * i, 1)
        return use(lambda: 10, 0)

    def hidden_parts(self, src, par, c, ready):
        d = self.hid[:, par, c, :]
        hi = self.act(lambda e: e.activation(d.hi, src[:, c, :], ACT.Copy), ready, self.h_hid[par][c])
        lo = self.dve(lambda e: e.tensor_tensor(d.lo, src[:, c, :], d.hi, ALU.subtract), hi)
        self.h_gate[c].give(lo), self.h_hid[par][c].give(lo)

    def add_down(self, d, td, par, first):
        for c in range(2):
            t = self.mms([(self.acc[:, m, :], d[:, c, m * P:(m + 1) * P], self.hid[:, par, c, :],
                           first and c == 0 and m % 2 == 0, False) for m in range(KT)],
                         td, self.h_hid[par][c], release=c == 1)
            self.h_hid[par][c].give(t)
        return t

    def inv_sqrt(self, ps, eps, ready, scale=1.0):
        s = self.act(lambda e: e.activation(self.rstd[:, :], ps, ACT.Sqrt, bias=self.eps(eps)), ready)
        self.hb[0].give(s)
        r = self.dve(lambda e: e.reciprocal(self.rstd[:, :], self.rstd[:, :]), s)
        if scale != 1.0:
            r = self.dve(lambda e: e.tensor_scalar(self.rstd[:, :], self.rstd[:, :], scale, None, ALU.mult), r)
        return r

    def mean_sq(self, src, kt, ready, sq, mat="mean"):
        hands = self.h_tmp if sq is self.tmp else None
        for k in range(0, kt, 2):
            s = self.act(lambda e, k=k: e.activation(sq[:, k:k + 2, :], src[:, k:k + 2, :], ACT.Square),
                         ready[k:k + 2], hands[k:k + 2] if hands else None)
            t = self.mms([(self.bank[0][:, 0:S], self.con(mat), sq[:, j, :], j == 0, j == kt - 1)
                          for j in (k, k + 1)], s, self.hb[0] if k == 0 else None)
            if hands:
                hands[k].give(t), hands[k + 1].give(t)
        return t

    def rms_norm(self, src, gain, dst, ready, parts=None, free=None):
        t = self.mean_sq(src, KT, ready, self.tmp)
        r, out = self.inv_sqrt(self.bank[0][:, 0:S], 1e-6, t), []
        p = Parts(self, dst, parts, 2, free)
        for k in range(KT):
            out.append(self.dve(lambda e, k=k: e.scalar_tensor_tensor(
                out=dst[:, k, :], in0=src[:, k, :], scalar=gain(k), in1=self.rstd[:, :],
                op0=ALU.mult, op1=ALU.mult), r))
            p.next(k, out)
        return p.finish() or out

    def add_rms(self, gain, ready, scale):
        t = self.mean_sq(self.acc, KT, [ready] * KT, self.tmp)
        r = self.inv_sqrt(self.bank[0][:, 0:S], 1e-6, t, scale)
        out = []
        for k in range(KT):
            t = self.dve(lambda e, k=k: e.scalar_tensor_tensor(
                out=self.tmp[:, k, :], in0=self.acc[:, k, :], scalar=gain(k), in1=self.rstd[:, :],
                op0=ALU.mult, op1=ALU.mult), r, self.h_tmp[k])
            out.append((self.pool if k % 3 == 1 else self.dve)(
                lambda e, k=k: e.tensor_tensor(self.h[:, k, :], self.h[:, k, :], self.tmp[:, k, :], ALU.add), t))
            self.h_tmp[k].give(out[-1])
        return out

    def layer_norm(self, src, kt, gain, bias, dst, ready, sq, mat="mean", eps=1e-5, parts=None):
        for j in range(kt):
            t = self.mms([(self.bank[1][:, 0:S], self.con(mat), src[:, j, :], j == 0, j == kt - 1)],
                         ready[j], self.hb[1] if j == 0 else None)
        centred = [self.dve(lambda e, k=k: e.tensor_tensor(src[:, k, :], src[:, k, :], self.bank[1][:, 0:S],
                                                           ALU.subtract), t) for k in range(kt)]
        self.hb[1].give(centred[-1])
        t = self.mean_sq(src, kt, centred, sq, mat)
        r, out = self.inv_sqrt(self.bank[0][:, 0:S], eps, t), []
        p = Parts(self, dst, parts, 2, None)
        for k in range(kt):
            t = self.dve(lambda e, k=k: e.scalar_tensor_tensor(
                out=src[:, k, :], in0=src[:, k, :], scalar=gain(k), in1=self.rstd[:, :],
                op0=ALU.mult, op1=ALU.mult), r)
            out.append(self.act(lambda e, k=k: e.activation(dst[:, k, :], src[:, k, :], ACT.Identity, bias=bias(k)), t))
            p.next(k, out)
        return p.finish() or out

    def evac_heads(self, ps, q, t, scale, ready, free):
        a = self.act(lambda e: e.activation(q[:, 2 * t, :], ps[0:64, 0:S], ACT.Copy, scale=scale), ready)
        b = self.dve(lambda e: e.tensor_scalar(q[:, 2 * t + 1, :], ps[64:128, 0:S], scale, None, ALU.mult), ready)
        free.give(a, b)
        return [a, b]

    def project(self, what, n_units, ready, take, src=None):
        src = src or self.x
        out = []
        for n in range(n_units):
            ap, tok = self.unit(lambda *i, n=n: what(i, n))
            for c in range(2):
                b = (2 * n + c) % 4
                t = self.tile_T(ap, c, tok, src, ready, self.bank[b][:, 0:S], self.hb[b], release=c == 1)
                out.append(take(2 * n + c, self.bank[b], t, self.hb[b]))
        return out

    def project_tok(self, what, n_units, ready, dst):
        src = self.x
        out = []
        for n in range(n_units):
            ap, tok = self.unit(lambda *i, n=n: what(i, n))
            for c in range(NB):
                b = (2 * n + c) % 4
                t = self.tile_tok(ap, c, tok, src, ready, self.bank[b][:, 0:S], self.hb[b], release=c == 1)
                d = dst[:, c, n * 256:(n + 1) * 256]
                t = (self.act(lambda e, b=b, d=d: e.activation(d, self.bank[b][:, 0:S], ACT.Copy), t) if c else
                     self.dve(lambda e, b=b, d=d: e.tensor_copy(d, self.bank[b][:, 0:S]), t))
                self.hb[b].give(t)
                out.append(t)
        return out

    def attention_buffers(self, of):
        self.wq = self.sb(f"{of}_att_w_by_query", [P, 2, 2, 512])
        self.wk = self.sb(f"{of}_att_w_by_key", [P, 2, 2, 512])
        self.stat = self.sb(f"{of}_att_stats", [P, 2, 3, 2, NB])
        self.h_wq = [Hand(self) for _ in range(2)]
        self.h_wk = [Hand(self) for _ in range(2)]
        self.h_pt2 = [Hand(self) for _ in range(2)]
        self.h_o = [Hand(self) for _ in range(2)]
        self.turn = 0
        self.bank7, self.h_bank7 = self.acc[:, 6:8, :], Hand(self)
        self.h_z = [Hand(self) for _ in range(2)]

    def softmax_pair(self, scores, causal, norm=None, ready=()):
        side = self.turn % 2
        self.turn += 1
        z, wq, wk, st = self.bank[2 * side:2 * side + 2], self.wq[:, side], self.wk[:, side], self.stat[:, side]
        span = [(0, 128), (128, 256)] if causal else [(0, 256), (256, 256)]
        hands = self.hb[2 * side:2 * side + 2]
        normed, done = [], []
        for hd in range(2):
            for qb, (at, n) in enumerate(span):
                last = self.mms(scores(hd, qb, z[hd][:, at:at + n]), hands[hd] if qb == 0 else None, ready)
            mx = [self.dve(lambda e, hd=hd, qb=qb, at=at, n=n: e.tensor_reduce(
                st[:, 0, hd, qb:qb + 1], z[hd][:, at:at + n], AX, ALU.max, negate=True), last,
                self.h_wq[side] if hd + qb == 0 else None) for qb, (at, n) in enumerate(span)]
            ex = [self.act(lambda e, hd=hd, qb=qb, at=at, n=n: e.activation(
                wq[:, hd, at:at + n], z[hd][:, at:at + n], ACT.Exp, bias=st[:, 0, hd, qb:qb + 1],
                accum_out=st[:, 1, hd, qb:qb + 1]), mx) for qb, (at, n) in enumerate(span)]
            hands[hd].give(ex)
            r = self.dve(lambda e, hd=hd: e.reciprocal(st[:, 2, hd, :], st[:, 1, hd, :]), ex)
            if norm is not None:
                for qb in range(NB):
                    r = self.dve(lambda e, hd=hd, qb=qb: e.tensor_tensor(
                        st[:, 2, hd, qb:qb + 1], st[:, 2, hd, qb:qb + 1], norm(hd, qb), ALU.mult), r)
            nrm = [self.dve(lambda e, hd=hd, qb=qb, at=at, n=n: e.tensor_scalar(
                wq[:, hd, at:at + n], wq[:, hd, at:at + n], st[:, 2, hd, qb:qb + 1], None, ALU.mult), r)
                for qb, (at, n) in enumerate(span)]
            normed.append(nrm)
        yield
        for hd in range(2):
            blocks = [(0, 0), (1, 0), (1, 1)] if causal else [(0, 0), (1, 0), (0, 1), (1, 1)]
            pt = self.acc[:, 2 * hd:2 * hd + 2, :].rearrange("p a b -> p (a b)")

            def turn(e, hd=hd, pt=pt):
                for qb, kb in blocks:
                    i = e.transpose(pt[:, self.kcol(qb, kb, causal):][:, 0:P],
                                    wq[:, hd, span[qb][0] + kb * P:][:, 0:P], self.con("identity"))
                return i
            tr = self.pe(turn, normed[hd], self.h_pt2[hd])
            w = 128 * len(blocks)
            if hd:
                cp = self.act(lambda e, hd=hd, pt=pt: e.activation(wk[:, hd, 0:w], pt[:, 0:w], ACT.Copy), tr,
                              self.h_wk[side])
            else:
                cp = self.dve(lambda e, hd=hd, pt=pt: e.tensor_copy(wk[:, hd, 0:w], pt[:, 0:w]), tr, self.h_wk[side])
            self.h_pt2[hd].give(cp)
            done.append(cp)
            trl = tr
        self.h_wq[side].give(trl)
        return side, done

    @staticmethod
    def kcol(qb, kb, causal):
        return (kb * 256 + qb * 128) if not (causal and kb == 1) else 256

    def values_pair(self, side, ready, parts, causal, width, take, first=True, last=True):
        ob = self.acc[:, 4:6, :]
        for hd in range(2):
            calls = []
            for kb in range(NB):
                q0 = 128 if causal and kb == 1 else 0
                w = self.wk[:, side, hd, kb * 256:kb * 256 + 256 - q0]
                calls.append((ob[0:width, hd, q0:256], parts(hd, kb), w, first and kb == 0, last and kb == 1))
            t = self.mms(calls, ready, self.h_o[0] if first and hd == 0 else None)
        self.h_wk[side].give(t)
        if last:
            t = take(ob, t)
            self.h_o[0].give(t)
        return t


class Parts:

    def __init__(self, c, src, dst, step, free):
        self.c, self.src, self.dst, self.step, self.free = c, src, dst, step, free
        self.out, self.waiting = [], None

    def high(self, k, ready):
        s, d = self.src[:, k:k + self.step, :], self.dst[:, k:k + self.step, :]
        self.waiting = s, d, self.c.act(lambda e: e.activation(d.hi, s, ACT.Copy), ready, self.free)

    def low(self):
        s, d, hi = self.waiting
        who = self.c.pool if len(self.out) // self.step % 3 == 2 else self.c.dve
        self.out += [who(lambda e: e.tensor_tensor(d.lo, s, d.hi, ALU.subtract), hi)] * self.step
        self.waiting = None

    def next(self, k, made):
        if self.dst is not None and (k + 1) % self.step == 0:
            if self.waiting:
                self.low()
            self.high(k + 1 - self.step, made[k + 1 - self.step:])

    def finish(self):
        if self.waiting:
            self.low()
        return self.out


def finish(stages):
    while True:
        try:
            next(stages)
        except StopIteration as e:
            return e.value


def stagger(steps, others=()):
    n, done, others = len(steps), [], list(others)
    per = -(-len(others) // n)
    for i in range(n + 2):
        now = others[per * i:per * (i + 1)]
        if i < n:
            next(steps[i])
        for x in now[:-1]:
            finish(x)
        if now:
            next(now[-1])
        if 0 <= i - 1 < n:
            next(steps[i - 1])
        if now:
            finish(now[-1])
        if 0 <= i - 2 < n:
            done.append(finish(steps[i - 2]))
    return done


def advance(stages):
    next(stages, None)
    yield
    next(stages, None)


L1 = 2
HEADS, HD = 8, 64
Q_SB, K_SB, V_SB, Q_FX, K_FX, V_FX, F_FX, Q_MEM = 0, 512, 1024, 1536, 2048, 2560, 3072, 3080
LAYER_COLS = {"ffn1_pre_g": 0, "ffn1_post_g": 8, "mix_pre_g": 16, "mix_post_g": 24, "b_gate": 32,
              "ffn2_pre_g": 56, "ffn2_post_g": 64}
N_LAYER_COLS = 72


def block1(c):
    with ExitStack() as own:
        outer, c.ctx = c.ctx, own
        lp = c.sb("layer_params", [P, N_LAYER_COLS])
        wf, bf = c.sb("w_forget", [P, L1 * KT * HEADS]), c.sb("b_forget", [P, L1 * HEADS])
        wfl, bfl = c.sb("w_forget_layer", [P, KT * HEADS]), c.sb("b_forget_layer", [P, HEADS])
        memn = c.sb("mem_norm", [P, KT, S])
        qa, ka = c.sb("q", [P, HEADS, S]), c.sb("k", [P, HEADS, S])
        qh, kh = qa[0:64], ka[0:64]
        qmem, kmem = qa[:, 0:4], ka[:, 0:4]
        vh = c.sb("v_tokens", [P, NB, 512])
        oT = c.sb("branch_out", [P, 4, S])
        ox = Pair(*(c.sb(f"branch_out_{n}", [P, 4, S], F32R) for n in ("hi", "lo")))
        merged = c.xn
        lf, lf2 = c.sb("log_forget", [P, NB, HEADS]), c.sb("log_forget_t", [P, NB, HEADS])
        cT, ncT = c.sb("cum_forget", [HEADS, S]), c.sb("neg_cum_forget", [HEADS, S])
        zt = [c.sb(f"sb_{n}", [P, 2, 2, 384]) for n in ("abs", "softplus", "log_not")]
        c.attention_buffers("b1")
        c.operands("b1")
        t = [c.load(wf[:, :], c.aps["w_forget"], engine="scalar", name="wf"),
             c.load(bf[:, :], c.aps["b_forget_rows"], engine="scalar", name="bf"),
             c.load(memn[:, :, :], c.aps["memory"], engine="scalar", name="mem")]
        ident = c.con("identity")

        c.rms_norm(memn, lambda k: c.col("mem_norm_g", k), memn, [t] * KT)

        with c.repeat(L1) as layer:
            body_start = c.n_units
            g = lambda name: (lambda k: lp[:, LAYER_COLS[name] + k:LAYER_COLS[name] + k + 1])
            tl = [c.dve(lambda e, to=to, of=of, n=n: e.tensor_copy(to[:, :], of[:, bass.ts(layer.cur, n)]))
                  for to, of, n in ((lp, c.pv, N_LAYER_COLS), (wfl, wf, KT * HEADS), (bfl, bf, HEADS))]

            def ffn(n, ready, before_add=None):
                t = c.rms_norm(c.h, g(f"ffn{n}_pre_g"), c.xn, ready, parts=c.x)
                t = c.ffn(lambda i, j: ("cols", f"ffn{n}_w_gate", i, j * 256),
                          lambda i, j: ("cols", f"ffn{n}_w_up", i, j * 256),
                          lambda i, j: ("rows", f"ffn{n}_w_down", i, j * 256), t)
                other = before_add(t) if before_add else None
                return c.add_rms(g(f"ffn{n}_post_g"), t, 0.5), other

            t_h, t_mem = ffn(1, [[tl, c.t_x]] * KT, lambda t: c.split(memn, c.x, t))
            w = lambda name, start: (lambda i, n: ("cols", name, i, start + n * 256))

            def take128(dst, sc):
                def take(t, ps, ready, free):
                    x = c.act(lambda e: e.activation(dst[:, t, :], ps[:, 0:S], ACT.Copy, scale=sc), ready)
                    free.give(x)
                    return x
                return take
            r = [c.project(w("w_mem_kv", 0), 2, t_mem, take128(kmem, 1.0)),
                 c.project_tok(w("w_mem_kv", 512), 2, t_mem, vh)]
            x_read = Hand(c)
            x_read.give(r)
            u = c.rms_norm(c.h, g("mix_pre_g"), c.xn, t_h, parts=c.x, free=x_read)

            for b in range(NB):
                t = c.mms([(c.bank[b][:, 0:HEADS], c.xn[:, k, b * P:(b + 1) * P], wfl[:, k * HEADS:(k + 1) * HEADS],
                            k == 0, k == KT - 1) for k in range(KT)], u, tl, c.hb[b])
                x, y = lf[:, b, :], lf2[:, b, :]
                t = c.dve(lambda e, b=b, x=x: e.tensor_tensor(x, c.bank[b][:, 0:HEADS], bfl[:, :], ALU.add), t)
                c.hb[b].give(t)
                a = c.act(lambda e, x=x, y=y: e.activation(y, x, ACT.Abs), t)
                a = c.act(lambda e, y=y: e.activation(y, y, ACT.Exp, scale=-1.0), a)
                a = c.act(lambda e, y=y: e.activation(y, y, ACT.Ln, bias=c.eps(1.0)), a)
                tlf = c.dve(lambda e, x=x, y=y: e.scalar_tensor_tensor(out=x, in0=x, scalar=0.0, in1=y, op0=ALU.min,
                                                                       op1=ALU.subtract), a)
            t = c.mms([(c.bank[0][0:HEADS, 0:128], lf[:, 0, :], c.con("upto"), True, True),
                       (c.bank[0][0:HEADS, 128:256], lf[:, 0, :], c.con("ones"), False, False),
                       (c.bank[0][0:HEADS, 128:256], lf[:, 1, :], c.con("upto"), False, True)], tlf, c.hb[0])
            a = c.dve(lambda e: e.tensor_copy(cT[:, :], c.bank[0][0:HEADS, 0:S]), t)
            t_cum = c.dve(lambda e: e.tensor_scalar(ncT[:, :], c.bank[0][0:HEADS, 0:S], -1.0, None, ALU.mult), a)
            c.hb[0].give(t_cum)

            def heads(q_at, k_at, v_at):
                sc = HD ** -0.5
                tq = c.project(w("w_in", q_at), 2, u, lambda t, ps, r, f: c.evac_heads(ps, qh, t, sc, r, f))
                tk = c.project(w("w_in", k_at), 2, u, lambda t, ps, r, f: c.evac_heads(ps, kh, t, 1.0, r, f))
                tv = c.project_tok(w("w_in", v_at), 2, u, vh)
                return [tq, tk, tv]

            def take_heads(pair):
                def take(ob, t):
                    a = c.act(lambda e: e.activation(oT[0:64, pair, :], ob[0:64, 0, :], ACT.Copy), t, h_oT)
                    b = c.dve(lambda e: e.tensor_copy(oT[64:128, pair, :], ob[0:64, 1, :]), a, h_oT)
                    return [a, b]
                return take

            vpart = lambda pair: (lambda hd, kb: vh[:, kb, (2 * pair + hd) * 64:(2 * pair + hd + 1) * 64])

            h_oT, h_bank7 = Hand(c), c.h_bank7
            summed = [None] * KT

            def gates(br, n):
                wg, tg = c.unit(lambda *i: ("cols", "w_gate", i, br * D + n * 256))
                c.tile_T(wg, 0, tg, c.x, u, c.acc[:, 6, :], h_bank7)
                yield
                t = c.tile_T(wg, 1, tg, c.x, u, c.acc[:, 7, :], None, release=True)
                for q in range(2):
                    m = 2 * n + q
                    a = c.act(lambda e, m=m, q=q: e.activation(c.tmp[:, m, :], c.acc[:, 6 + q, :], ACT.Sigmoid,
                              bias=lp[:, LAYER_COLS["b_gate"] + br * 8 + m:][:, 0:1]), t, c.h_tmp[m])
                    h_bank7.give(a), c.h_tmp[m].give(a)

            def merge(name, o_ready, first=False):
                t_o = c.split(oT, ox, o_ready, n=4)
                h_oT.give(t_o)
                for half in range(2):
                    wb, tb = c.unit(lambda *i, half=half: ("cols", name, i, half * 512), a=4)
                    for pair in range(2):
                        bank = [c.h_pt2[0], c.h_pt2[1], c.h_o[0], h_bank7][2 * half + pair]
                        for n in (2 * pair, 2 * pair + 1):
                            m = 4 * half + n
                            t = c.mms([(c.acc[:, m, :], wb[:, k, n * P:(n + 1) * P], ox[:, k, :], k == 0, k == 3)
                                       for k in range(4)], tb, t_o, bank if n % 2 == 0 else None, release=n == 3)
                        for m in (m - 1, m):
                            dst = merged if first else c.tmp
                            v = c.dve(lambda e, m=m, dst=dst: e.tensor_tensor(
                                dst[:, m, :], c.acc[:, m, :], c.tmp[:, m, :], ALU.mult), t, c.h_tmp[m])
                            summed[m] = v
                            if not first:
                                summed[m] = c.pool(lambda e, m=m: e.tensor_tensor(
                                    merged[:, m, :], merged[:, m, :], c.tmp[:, m, :], ALU.add), v)
                            c.h_tmp[m].give(summed[m])
                        bank.give(v)

            r.append(c.project(w("w_in", Q_MEM), 2, u, take128(qmem, 128 ** -0.5)))
            def mem_pair(pair, r):
                scores = lambda hd, qb, z: [(z, qmem[:, 2 * pair + hd, qb * P:(qb + 1) * P], kmem[:, 2 * pair + hd, :],
                                             True, True)]
                side, tw = yield from c.softmax_pair(scores, False, ready=r)
                yield
                take = lambda ob, t: c.act(lambda e: e.activation(oT[:, 2 * pair:2 * pair + 2, :], ob, ACT.Copy), t,
                                           h_oT)
                return c.values_pair(side, [tw, r], lambda hd, kb: vh[:, kb, (2 * pair + hd) * P:(2 * pair + hd + 1) * P],
                                     False, P, take)
            done = stagger([mem_pair(p, r) for p in range(2)], [gates(2, n) for n in range(4)])
            merge("w_br_mem", done, first=True)

            r = heads(Q_SB, K_SB, V_SB)
            h_z = [[Hand(c) for _ in range(2)] for _ in range(2)]

            def scores_sb(pair, hd, r):
                side, wk = pair % 2, c.wk
                ab, sp, ln = (z[:, side] for z in zt)
                hh, zb, bt = 2 * pair + hd, c.bank[2 * side + hd], c.acc[:, 2 * hd:2 * hd + 2, :]
                bt = bt.rearrange("p a b -> p (a b)")
                tz = c.mms([(zb[:, 0:256], kh[:, hh, 0:128], qh[:, hh, :], True, True),
                            (zb[:, 256:384], kh[:, hh, 128:256], qh[:, hh, 128:256], True, True)],
                           r, c.hb[2 * side + hd])
                z = zb[:, 0:384]
                a = c.act(lambda e: e.activation(ab[:, hd, :], z, ACT.Abs), tz, h_z[side][hd])
                a = c.act(lambda e: e.activation(ab[:, hd, :], ab[:, hd, :], ACT.Exp, scale=-1.0), a)
                a = c.act(lambda e: e.activation(ab[:, hd, :], ab[:, hd, :], ACT.Ln, bias=c.eps(1.0)), a)
                s = c.dve(lambda e: e.scalar_tensor_tensor(out=sp[:, hd, :], in0=z, scalar=0.0, in1=ab[:, hd, :],
                                                           op0=ALU.max, op1=ALU.add), a)
                n = None
                for at, m in ((0, "before"), (128, "ones"), (256, "before")):
                    n = c.dve(lambda e, at=at, m=m: e.scalar_tensor_tensor(
                        out=ln[:, hd, at:at + P], in0=sp[:, hd, at:at + P], scalar=-1.0, in1=c.con(m),
                        op0=ALU.mult, op1=ALU.mult), s)
                lb = c.dve(lambda e: e.tensor_tensor(sp[:, hd, :], z, sp[:, hd, :], ALU.subtract), n)
                c.hb[2 * side + hd].give(lb)
                yield
                later, ones = c.con("after"), c.con("ones")
                tb = c.mms([(bt[:, 0:256], later, ln[:, hd, 0:256], True, False),
                            (bt[:, 128:256], ones, ln[:, hd, 256:384], False, True),
                            (bt[:, 256:384], later, ln[:, hd, 256:384], False, True)],
                           n, c.h_pt2[hd])
                x = c.dve(lambda e: e.tensor_tensor(ab[:, hd, :], bt[:, 0:384], sp[:, hd, :], ALU.add), tb, lb)
                c.h_pt2[hd].give(x)
                x = c.act(lambda e: e.activation(ab[:, hd, :], ab[:, hd, :], ACT.Exp), x)
                for at, m in ((0, "before"), (128, "ones"), (256, "before")):
                    x2 = c.pool(lambda e, at=at, m=m: e.tensor_tensor(
                        wk[:, side, hd, at:at + P], ab[:, hd, at:at + P], c.con(m), ALU.mult),
                        x, c.h_wk[side])
                h_z[side][hd].give(x2, tb)
                return x2

            def sb_pair(pair, r):
                heads_ = [scores_sb(pair, hd, r) for hd in range(2)]
                for x in heads_:
                    next(x)
                yield
                x2 = [finish(x) for x in heads_]
                yield
                return c.values_pair(pair % 2, [r, x2], vpart(pair), True, 64, take_heads(pair))
            done = stagger([sb_pair(p, r) for p in range(4)], [gates(0, n) for n in range(4)])
            merge("w_br_sb", done)

            r = heads(Q_FX, K_FX, V_FX)
            r = [r, t_cum]
            def fox_pair(pair, r):
                def scores(hd, qb, z):
                    hh, n = 2 * pair + hd, 128 * (qb + 1)
                    sel = ident[0:HEADS, hh:hh + 1]
                    return [(z, qh[:, hh, qb * P:(qb + 1) * P], kh[:, hh, 0:n], True, False),
                            (z, cT[:, qb * P:(qb + 1) * P], sel.to_broadcast([HEADS, n]), False, False),
                            (z, sel.to_broadcast([HEADS, P]), ncT[:, 0:n], False, False),
                            (z[:, n - P:n], ident, c.con("not_before"), False, True)]
                side, tw = yield from c.softmax_pair(scores, True, ready=r)
                yield
                return c.values_pair(side, tw, vpart(pair), True, 64, take_heads(pair))
            done = stagger([fox_pair(p, r) for p in range(4)], [gates(1, n) for n in range(4)])
            merge("w_br_fox", done)

            t = c.split(merged, c.x, list(summed))
            for n in range(4):
                ap, tok = c.unit(lambda *i, n=n: ("cols", "w_out", i, n * 256))
                for q in range(2):
                    ta = c.tile_T(ap, q, tok, c.x, t, c.acc[:, 2 * n + q, :], None, release=q == 1)
            t_h = c.add_rms(g("mix_post_g"), ta, 1.0)
            ffn(2, t_h)
            c.pad_units(body_start)
            c.barrier()
        c.barrier()
        c.ctx = outer


ALPHA2 = 4 ** 0.25
SGU = 2048
CHUNK = 16
NCH = S // CHUNK


def residual_norm(c, alpha, scale, gain, bias, ready, parts=None):
    t = [c.dve(lambda e, k=k: e.scalar_tensor_tensor(out=c.h[:, k, :], in0=c.h[:, k, :], scalar=alpha / scale,
                                                     in1=c.acc[:, k, :], op0=ALU.mult, op1=ALU.add), ready)
         for k in range(KT)]
    return c.layer_norm(c.h, KT, gain, bias, c.h, t, c.tmp, eps=1e-5 / scale ** 2, parts=parts)


def block2(c):
    def ln(i, j):
        return [lambda k, x=x: c.col((f"ln_{x}_2", (i, j)), k) for x in "gb"]

    def ffn(i, j, t, parts=None):
        t = c.ffn(lambda _, n: ("cols", "ffn_w_in_2", (i, 0 if j == 0 else 1), n * 256),
                  lambda _, n: ("cols", "ffn_w_in_2", (i, 0 if j == 0 else 1), DFF + n * 256),
                  lambda _, n: ("rows", "ffn_w_out_2", (i, 0 if j == 0 else 1), n * 256), t)
        return residual_norm(c, ALPHA2, 0.5, *ln(i, j), t, parts)

    with c.scope():
        c.operands("b2a")
        t = ffn(0, 0, c.split(c.h, c.x, None), c.x)
        spatial_gating(c, t)
        t = residual_norm(c, ALPHA2, 1.0, *ln(0, 1), None, c.x)
        t = ffn(0, 2, t, c.x)
        ffn(1, 0, t)
        c.barrier()
    with c.scope():
        rwkv(c)
    with c.scope():
        c.operands("b2b")
        t = residual_norm(c, ALPHA2, 1.0, *ln(1, 1), None, c.x)
        ffn(1, 2, t)
        c.barrier()


def spatial_gating(c, ready):
    with ExitStack() as own:
        outer, c.ctx = c.ctx, own
        n_t = SGU // P
        uv = c.sb("sgu_uv", [P, 2 * n_t, S])
        sq = c.sb("sgu_squares", [P, n_t, S])
        rest = Pair(*(c.sb(f"sgu_uv_{n}", [P, KT, S], F32R) for n in ("hi", "lo")))
        uvx = lambda g: c.x[:, g:g + 2, :] if g < KT else rest[:, g - KT:g - KT + 2, :]
        vt = sq[:, :, :].rearrange("p a b -> p (a b)").rearrange("p (b f) -> p b f", b=NB)
        wsp, bsp = c.sb("sgu_w_spatial", [P, n_t, P]), c.sb("sgu_b_spatial", [n_t, P])
        tw = [c.load(wsp[:, :, :], c.aps["sgu_w_spatial"], engine="scalar", name="wsp"),
              c.load(bsp[:, :], c.aps["sgu_b_spatial"], engine="scalar", name="bsp")]
        for g in range(n_t):
            tm = c.pool(lambda e, g=g: e.tensor_tensor(wsp[:, g, :], wsp[:, g, :], c.con("upto"), ALU.mult), tw)

        def take(t, ps, ready, free):
            x = c.act(lambda e: e.activation(uv[:, t, :], ps[:, 0:S], ACT.Gelu, bias=c.col(("sgu_b_in_2", 0), t)), ready)
            free.give(x)
            return x
        z = c.project(lambda _, n: ("cols", "sgu_w_in_2", 0, n * 256), 16, ready, take)
        v = uv[:, n_t:2 * n_t, :]
        t = c.layer_norm(v, n_t, lambda k: c.col(("sgu_ln_g_2", 0), k), lambda k: c.col(("sgu_ln_b_2", 0), k),
                         v, z[n_t:], sq, mat="mean_half")
        c.barrier()
        turned = []
        for b in range(NB):
            for g4 in range(n_t // 4):
                n = (g4 + b * 4) % 4

                def turn(e, b=b, g4=g4, n=n):
                    for q in range(4):
                        i = e.transpose(c.bank[n][:, q * P:(q + 1) * P], v[:, 4 * g4 + q, b * P:(b + 1) * P],
                                        c.con("identity"))
                    return i
                t = c.pe(turn, c.hb[n])
                f = vt[:, b, g4 * 512:(g4 + 1) * 512]
                t = (c.act(lambda e, f=f, n=n: e.activation(f, c.bank[n][:, :], ACT.Copy), t) if n % 2 else
                     c.dve(lambda e, f=f, n=n: e.tensor_copy(f, c.bank[n][:, :]), t))
                c.hb[n].give(t)
                turned.append(t)
        gated = []
        for g in range(n_t):
            n = g % 4
            calls = []
            for b in range(NB):
                o = c.bank[n][:, b * P:(b + 1) * P]
                calls += [(o, vt[:, b, g * P:(g + 1) * P], wsp[:, g, :], b == 0, False),
                          (o, c.con("identity")[0:n_t, g:g + 1].to_broadcast([n_t, P]), bsp[:, :], False, True)]
            t = c.mms(calls, turned, tm, tw, c.hb[n])
            t = c.dve(lambda e, g=g, n=n: e.tensor_tensor(uv[:, g, :], uv[:, g, :], c.bank[n][:, 0:S], ALU.mult), t)
            c.hb[n].give(t)
            gated.append(t)
            if g % 2:
                gated[-2:] = c.split(uv[:, g - 1:g + 1, :], uvx(g - 1), t, n=2) * 2
        for n in range(8):
            ap, tok = c.unit(lambda *_, n=n: ("rows", "sgu_w_out_2", 0, n * 256), a=2)
            for q in range(2):
                t2 = c.mms([(c.acc[:, m, :], ap[:, q, m * P:(m + 1) * P], uvx(2 * n)[:, q, :],
                             n == 0 and q == 0 and m % 2 == 0, False) for m in range(KT)], tok, gated[2 * n + q],
                           release=q == 1)
        c.barrier()
        c.ctx = outer


def rwkv(c):
    flat8 = lambda x: x[:, :, :].rearrange("p a b -> p (a b)")
    r, k, kk, bb, v = (c.sb(f"rwkv_{n}", [P, KT, S]) for n in ("r", "k", "kk", "b", "v"))
    ld = c.sb("rwkv_log_decay", [P, NB, D])

    def shifted(dst):
        a = c.dve(lambda e: e.tensor_tensor(dst[:, :, 1:S], c.h[:, :, 0:S - 1], c.h[:, :, 1:S], ALU.subtract))
        b = c.dve(lambda e: e.tensor_scalar(dst[:, :, 0:1], c.h[:, :, 0:1], -1.0, None, ALU.mult))
        return [a, b]

    def mix(j, xx, dst, ready):
        for q in range(KT):
            t = c.dve(lambda e, q=q: e.scalar_tensor_tensor(
                out=dst[:, q, :], in0=xx[:, q, :], scalar=c.col(("rwkv_mu_2", (0, j)), q), in1=c.h[:, q, :],
                op0=ALU.mult, op1=ALU.add), ready)
        return t

    def head_vectors(of):
        rows = c.sb(f"rwkv_{of}_head_rows", [16, D])
        for half in range(2):
            def turn(e, half=half):
                for j in range(4):
                    i = e.transpose(c.bank[2 + half][0:16, j * P:(j + 1) * P],
                                    c.con("head_of")[:, 16 * (4 * half + j):][:, 0:16], c.con("identity"))
                return i
            t = c.pe(turn, c.hb[2 + half])
            t = c.act(lambda e, half=half: e.activation(rows[:, half * 512:(half + 1) * 512],
                                                        c.bank[2 + half][0:16, :], ACT.Copy), t)
            c.hb[2 + half].give(t)
        return c.sb(f"rwkv_{of}_head_numbers", [16, S]), (rows, t)

    def sum_heads(q, x, ready):
        return c.mms([(c.bank[0][0:16, 0:S], c.con("head_of")[:, 16 * q:16 * q + 16], x, q == 0, q == KT - 1)],
                     ready, c.hb[0] if q == 0 else None)

    def to_features(q, x, h_rows, ready):
        n = 1 + q % 3
        return n, c.mms([(c.bank[n][:, 0:S], h_rows[0][:, q * P:(q + 1) * P], x[:, :], True, True)], ready,
                        h_rows[1], c.hb[n])

    def copy_out(dst):
        def take(t, ps, ready, free):
            x = (c.act(lambda e: e.activation(dst[:, t, :], ps[:, 0:S], ACT.Copy), ready) if t % 2 else
                 c.dve(lambda e: e.tensor_copy(dst[:, t, :], ps[:, 0:S]), ready))
            free.give(x)
            return x
        return take

    with c.scope():
        lora = Pair(*(c.sb(f"rwkv_lora_{n}", [P, 2, S], F32R) for n in ("hi", "lo")))
        low = c.sb("rwkv_low_rank", [P, 2, S])
        w0row = c.sb("rwkv_w0_row", [1, D])
        tw0 = c.load(w0row[:, :], c.aps["rwkv_w0_row"], engine="scalar", name="w0")
        ones_row = c.con("ones")[0:1, :]
        xs = [Pair(*(c.sb(f"rwkv_x{i}_{n}", [P, KT, S], F32R) for n in ("hi", "lo"))) for i in range(2)]
        x_read, m_read = [Hand(c) for _ in range(2)], [Hand(c) for _ in range(2)]
        sx = shifted(c.tmp)

        def mixed(j, buf):
            t = mix(j, c.tmp, buf, [sx, m_read[j % 2].take()])
            t = c.split(buf, xs[j % 2], t, free=x_read[j % 2])
            m_read[j % 2].give(t)
            return t
        t = mixed(0, c.xn)
        for j, dst in enumerate((r, k, v)):
            t_next = mixed(j + 1, kk if j % 2 == 0 else c.xn)
            out = c.project(lambda _, n, j=j: ("cols", "rwkv_w_rkv_2", (0, j), n * 256), 4, t, copy_out(dst),
                            src=xs[j % 2])
            x_read[j % 2].give(out)
            t = t_next
        xw, xa = t, mixed(4, c.xn)
        ap, tok = c.unit(lambda *_: ("side", ["rwkv_w1_2", "rwkv_a1_2"], 0, 0))
        t1 = c.mms([(c.bank[0][0:64, 0:S], ap[:, q, 0:64], xs[1][:, q, :], q == 0, q == KT - 1) for q in range(KT)],
                   tok, xw, c.hb[0])
        t2 = c.mms([(c.bank[1][0:64, 0:S], ap[:, q, 64:128], xs[0][:, q, :], q == 0, q == KT - 1) for q in range(KT)],
                   tok, xa, c.hb[1], release=True)
        t1 = c.act(lambda e: e.activation(low[0:64, 0, :], c.bank[0][0:64, 0:S], ACT.Tanh), t1)
        t2 = c.dve(lambda e: e.tensor_copy(low[0:64, 1, :], c.bank[1][0:64, 0:S]), t2)
        c.hb[0].give(t1), c.hb[1].give(t2)
        c.split(low[0:64], lora[0:64], [t1, t2], n=2)
        c.barrier()
        ap, tok = c.unit(lambda *_: ("stack", ["rwkv_w2_2", "rwkv_a2_2"], 0, 0), a=2)
        for b in range(NB):
            for q in range(2):
                n = 2 * b + q
                t = c.mms([(c.bank[n][:, :], lora[0:64, 0, b * P:(b + 1) * P], ap[0:64, 0, q * 512:(q + 1) * 512], True, False),
                           (c.bank[n][:, :], ones_row, w0row[:, q * 512:(q + 1) * 512], False, True)], tok, tw0, c.hb[n])
                dst = ld[:, b, q * 512:(q + 1) * 512]
                t = c.act(lambda e, n=n, dst=dst: e.activation(dst, c.bank[n][:, :], ACT.Sigmoid), t)
                c.hb[n].give(t)
                tld = c.dve(lambda e, dst=dst: e.tensor_scalar(dst, dst, -float(np.exp(-0.5)), None, ALU.mult), t)
        for q in range(KT):
            n = q % 4
            t = c.mms([(c.bank[n][:, 0:S], ap[0:64, 1, q * P:(q + 1) * P], lora[0:64, 1, :], True, True)] , tok, c.hb[n],
                      release=q == KT - 1)
            ta = c.act(lambda e, n=n, q=q: e.activation(bb[:, q, :], c.bank[n][:, 0:S], ACT.Sigmoid,
                                                        bias=c.col(("rwkv_a0_2", 0), q)), t)
            c.hb[n].give(ta)
        hv, h_rows = head_vectors("kk")
        for q in range(KT):
            t = c.dve(lambda e, q=q: e.tensor_scalar(kk[:, q, :], k[:, q, :], c.col(("rwkv_k_k_2", 0), q), None, ALU.mult))
            t = c.act(lambda e, q=q: e.activation(c.xn[:, q, :], kk[:, q, :], ACT.Square), t)
            t = sum_heads(q, c.xn[:, q, :], t)
        t = c.act(lambda e, hv=hv: e.activation(hv[:, :], c.bank[0][0:16, 0:S], ACT.Sqrt), t)
        c.hb[0].give(t)
        t = c.dve(lambda e, hv=hv: e.tensor_scalar(hv[:, :], hv[:, :], 1e-12, None, ALU.max), t)
        t = c.dve(lambda e, hv=hv: e.reciprocal(hv[:, :], hv[:, :]), t)
        for q in range(KT):
            n, th = to_features(q, hv, h_rows, t)
            tkk = c.dve(lambda e, q=q, n=n: e.tensor_tensor(kk[:, q, :], kk[:, q, :], c.bank[n][:, 0:S], ALU.mult), th)
            c.hb[n].give(tkk)
        for q in range(KT):
            t = c.dve(lambda e, q=q: e.tensor_scalar(c.xn[:, q, :], bb[:, q, :], 1.0, c.col(("rwkv_k_a_2", 0), q),
                                                     ALU.subtract, ALU.mult), ta, tkk)
        t = c.dve(lambda e: e.scalar_tensor_tensor(out=flat8(k), in0=flat8(c.xn), scalar=1.0, in1=flat8(k),
                                                   op0=ALU.add, op1=ALU.mult), t)
        t = c.dve(lambda e: e.tensor_tensor(bb[:, :, :], bb[:, :, :], kk[:, :, :], ALU.mult), tkk)
        c.barrier()
    with c.scope():
        G, H = c.sb("rwkv_G", [P, 4, NCH, 64]), c.sb("rwkv_H", [P, 4, NCH, 64])
        Rs = c.sb("rwkv_R", [P, 4, S])
        rwkv_scan(c, r, k, kk, bb, v, ld, G, H, Rs)
        c.barrier()

    with c.scope():
        x = Pair(*(c.sb(f"rwkv_out_x_{n}", [P, KT, S], F32R) for n in ("hi", "lo")))
        g_lora = Pair(*(c.sb(f"rwkv_gate_lora_{n}", [P, 2, S], F32R) for n in ("hi", "lo")))
        g_low = c.sb("rwkv_gate_low_rank", [P, 2, S])
        y = kk
        hv2, h_rows2 = head_vectors("y")
        squares = []
        for q in range(KT):
            n = 1 + q % 3
            t = c.mms([(c.bank[n][:, 0:S], c.con("head_mean"), y[:, q, :], True, True)], c.hb[n])
            t = c.dve(lambda e, q=q, n=n: e.tensor_tensor(y[:, q, :], y[:, q, :], c.bank[n][:, 0:S], ALU.subtract), t)
            c.hb[n].give(t)
            squares.append(c.act(lambda e, q=q: e.activation(c.tmp[:, q, :], y[:, q, :], ACT.Square), t))
        for q in range(KT):
            t = sum_heads(q, c.tmp[:, q, :], squares[q])
        t = c.act(lambda e: e.activation(hv2[:, :], c.bank[0][0:16, 0:S], ACT.Sqrt, bias=c.eps(64e-5)[0:16],
                                         scale=1 / 64), t)
        c.hb[0].give(t)
        t_std = c.dve(lambda e: e.reciprocal(hv2[:, :], hv2[:, :]), t)
        bonus = []
        for q in range(KT):
            t = c.dve(lambda e, q=q: e.scalar_tensor_tensor(
                out=c.xn[:, q, :], in0=r[:, q, :], scalar=c.col(("rwkv_r_k_2", 0), q), in1=k[:, q, :],
                op0=ALU.mult, op1=ALU.mult))
            n = 1 + q % 3
            t = c.mms([(c.bank[n][:, 0:S], c.con("head_sum"), c.xn[:, q, :], True, True)], t, c.hb[n])
            bonus.append(c.dve(lambda e, q=q, n=n: e.tensor_tensor(v[:, q, :], v[:, q, :], c.bank[n][:, 0:S], ALU.mult), t))
            c.hb[n].give(bonus[-1])
        for q in range(KT):
            n, t = to_features(q, hv2, h_rows2, t_std)
            t = c.dve(lambda e, q=q, n=n: e.scalar_tensor_tensor(
                out=y[:, q, :], in0=y[:, q, :], scalar=c.col(("rwkv_gn_g_2", 0), q), in1=c.bank[n][:, 0:S],
                op0=ALU.mult, op1=ALU.mult), t)
            c.hb[n].give(t)
            c.dve(lambda e, q=q: e.scalar_tensor_tensor(
                out=y[:, q, :], in0=y[:, q, :], scalar=c.col(("rwkv_gn_b_2", 0), q), in1=v[:, q, :],
                op0=ALU.add, op1=ALU.add), t, bonus[q])
        c.barrier()
        sx = shifted(c.tmp)
        t = mix(5, c.tmp, c.xn, sx)
        t = c.split(c.xn, x, [t])
        ap, tok = c.unit(lambda *_: ("side", ["rwkv_g1_2"], 0, 0))
        both = []
        for q, n in enumerate((P, 32)):
            tq = c.mms([(c.bank[q][0:n, 0:S], ap[:, m, q * P:q * P + n], x[:, m, :], m == 0, m == KT - 1)
                        for m in range(KT)], tok, t, c.hb[q], release=q == 1)
            tg = c.act(lambda e, q=q, n=n: e.activation(g_low[0:n, q, :], c.bank[q][0:n, 0:S], ACT.Sigmoid), tq)
            c.hb[q].give(tg)
            tl = c.split(g_low[0:n, q:q + 1], g_lora[0:n, q:q + 1], tg, n=1, step=1)
            tg = [tl, tg]
            both.append(tg)
        yt = []
        ap, tok = c.unit(lambda *_: ("rows", "rwkv_g2_2", 0, 0), a=2)
        for q in range(KT):
            n = q % 4
            t = c.mms([(c.bank[n][:, 0:S], ap[:, 0, q * P:(q + 1) * P], g_lora[:, 0, :], True, False),
                       (c.bank[n][:, 0:S], ap[0:32, 1, q * P:(q + 1) * P], g_lora[0:32, 1, :], False, True)],
                      tok, both, c.hb[n], release=q == KT - 1)
            t = c.dve(lambda e, q=q, n=n: e.tensor_tensor(y[:, q, :], y[:, q, :], c.bank[n][:, 0:S], ALU.mult), t)
            c.hb[n].give(t)
            yt.append(t)
        t = c.split(y, x, yt)
        for n in range(4):
            ap, tok = c.unit(lambda *_, n=n: ("cols", "rwkv_w_o_2", 0, n * 256))
            for q in range(2):
                c.tile_T(ap, q, tok, x, t, c.acc[:, 2 * n + q, :], None, release=q == 1)
        c.barrier()


def rwkv_scan(c, r, k, kk, bb, v, ld, G, H, Rs):
    flat8 = lambda x: x[:, :, :].rearrange("p a b -> p (a b)")
    pair8 = {n: flat8(x) for n, x in (("r", r), ("k", k), ("kk", kk), ("b", bb), ("v", v))}
    part = lambda n, i: pair8[n][:, bass.ts(i, S)]
    two = lambda x: x.rearrange("p (b t) -> p b t", b=NB)
    with ExitStack() as own:
        outer, c.ctx = c.ctx, own
        sb2 = lambda n: c.sb(f"rwkv_{n}", [P, S])
        ldp = c.rstd[:, :].rearrange("p (b f) -> p b f", b=NB)
        eL, emL, eX, eA = (sb2(n) for n in ("e_cum", "e_neg_cum", "e_cum_before", "e_to_end"))
        bt, rt, bh, vs = (sb2(n) for n in ("bt", "rt", "bh", "vs"))
        at, kt, kh = eX, emL, eA
        sq2 = c.sb("rwkv_squares", [P, 2, 4, P])
        wt, zt = (c.sb(f"rwkv_{n}", [P, NB, P]) for n in ("W", "U"))
        ut = zt
        bx = c.sb("rwkv_b_by_chunk", [P, 8, 64])
        ux, vx = (c.sb(f"rwkv_{n}_by_chunk", [P, 2, 8, 64]) for n in "uv")
        st = c.sb("rwkv_state", [P, 2, 4, 64])
        tf, xf = flat8(c.tmp), flat8(c.xn)
        tok = tf[:, 0:1024].rearrange("p (a b f) -> p a b f", a=4, b=NB)
        diag = tf[:, 1024:2048].rearrange("p (n j) -> p n j", n=NCH)
        pm = xf[:, 0:1024].rearrange("p (h a t) -> p h a t", h=2, a=4)
        arb = xf[:, 1024:2048].rearrange("p (h a t) -> p h a t", h=2, a=4)
        rk = c.act_gate[:, :, :].rearrange("p h (b t) -> p h b t", b=NB)
        X = c.hidden[:, :, :].rearrange("p h (b t) -> p h b t", b=NB)
        B = [b[:, :] for b in c.bank] + [c.acc[:, 2 * i:2 * i + 2, :].rearrange("p a b -> p (a b)") for i in range(4)]
        hB = c.hb + [Hand(c) for _ in range(4)]
        ident = c.con("identity")
        mask2 = lambda name: c.con(name).unsqueeze(1).to_broadcast([P, 2, P])
        ld_v = ld[:, :, :]

        def copy(dst, src, ready, who):
            if who == "act":
                return c.act(lambda e: e.activation(dst, src, ACT.Copy), ready)
            return c.dve(lambda e: e.tensor_copy(dst, src), ready)

        def tt(dst, a, b, op, *ready, who=c.dve):
            return who(lambda e: e.tensor_tensor(dst, a, b, op), *ready)

        ready, free, last = {}, Hand(c), Hand(c)
        for n_ in ("ta", "tb", "tr", "tk", "tbh", "tkh", "tv", "ex"):
            ready[n_] = Hand(c)

        def front(px):
            t0 = c.dve(lambda e: e.tensor_copy(ldp[:, :, :], ld_v[:, :, bass.ts(px(), P)]), free)
            tv = c.pool(lambda e: e.tensor_copy(vs[:, :], part("v", px())), free)
            tl = []
            for i, m in enumerate(("chunk_upto", "chunk_before", "chunk_after")):
                for b in range(NB):
                    o = B[i // 2][:, (i % 2) * S + b * P:][:, 0:P]
                    tl.append(c.mms([(o, ldp[:, b, :], c.con(m), b == 0, True)], t0,
                                    hB[i // 2] if b == 0 and i % 2 == 0 else None))
            ex = []
            for dst, src, sc in ((eL, B[0][:, 0:S], 1.0), (emL, B[0][:, 0:S], -1.0), (eX, B[0][:, S:2 * S], 1.0),
                                 (eA, B[1][:, 0:S], 1.0)):
                ex.append(c.act(lambda e, dst=dst, src=src, sc=sc: e.activation(dst[:, :], src, ACT.Exp, scale=sc), tl, free))
            hB[0].give(ex[:3]), hB[1].give(ex[3])
            yield
            ta = c.dve(lambda e: e.scalar_tensor_tensor(out=at[:, :], in0=part("kk", px()), scalar=-1.0,
                                                        in1=eX[:, :], op0=ALU.mult, op1=ALU.mult), ex)
            tb = c.dve(lambda e: e.tensor_tensor(bt[:, :], part("b", px()), emL[:, :], ALU.mult), ex)
            tr = c.dve(lambda e: e.tensor_tensor(rt[:, :], part("r", px()), eL[:, :], ALU.mult), ex)
            tk = c.dve(lambda e: e.tensor_tensor(kt[:, :], part("k", px()), emL[:, :], ALU.mult), ex, tb)
            tbh = c.dve(lambda e: e.tensor_tensor(bh[:, :], part("b", px()), eA[:, :], ALU.mult), ex)
            tkh = c.dve(lambda e: e.tensor_tensor(kh[:, :], part("k", px()), eA[:, :], ALU.mult), ex, tbh)
            for n_, t in (("ta", ta), ("tb", tb), ("tr", tr), ("tk", tk), ("tbh", tbh), ("tkh", tkh), ("tv", tv), ("ex", ex)):
                ready[n_].give(t)

        def pair(px, local, next_px):
            ta, tb, tr, tk, tbh, tkh, tv, ex = (ready[n_].take() for n_ in ("ta", "tb", "tr", "tk", "tbh", "tkh", "tv", "ex"))
            ended = last.take()
            tt_done = []
            for n, (x, y, w) in enumerate(((at, bh, [ta, tbh]), (kh, vs, [tkh, tv]))):
                def turn(e, n=n, x=x, y=y):
                    for i, z in enumerate((x, y)):
                        for b in range(NB):
                            ins = e.transpose(B[2 + n][:, (2 * i + b) * P:][:, 0:P], z[:, b * P:(b + 1) * P], ident)
                    return ins
                t = c.pe(turn, w, hB[2 + n])
                t = copy(tok[:, 2 * n:2 * n + 2, :, :], B[2 + n].rearrange("p (a b f) -> p a b f", a=2, b=NB), [t, ended], "act")
                hB[2 + n].give(t)
                tt_done.append(t)
            dc = two(eL[:, :]).rearrange("p b (n t) -> p (b n) t", t=CHUNK)[:, :, CHUNK - 1:CHUNK]
            tdg = tt(diag, c.con("identity_pair")[:, 0:64].unsqueeze(1).to_broadcast([P, NCH, 64]),
                     dc.to_broadcast([P, NCH, 64]), ALU.mult, ex, ended, who=c.pool)
            tri = []
            for hd in range(2):
                R = slice(64 * hd, 64 * hd + 64)
                bA, bB, bC = 4 + 2 * hd, 5 + 2 * hd, hd
                T = [slice(b * P, (b + 1) * P) for b in range(NB)]
                prod = lambda bank, at_, x, y: [(B[bank][:, at_ + b * P:][:, 0:P], x[R, T[b]], y[R, T[b]],
                                                 at_ == 0 and b == 0, True) for b in range(NB)]
                t = c.mms(prod(bA, 0, bt, at) + prod(bA, S, at, bt), ta, tb, hB[bA])
                m1 = tt(pm[:, hd, 0:2, :], two(B[bA][:, 0:S]), mask2("chunk_before"), ALU.mult, t)
                m2 = tt(pm[:, hd, 2:4, :], two(B[bA][:, S:2 * S]), mask2("chunk_after"), ALU.mult, t)
                hB[bA].give(m2)
                t = c.mms(prod(bB, 0, kt, at) + prod(bB, S, bt, rt), ta, tb, tr, tk, hB[bB])
                m3 = tt(arb[:, hd, 0:2, :], two(B[bB][:, 0:S]), mask2("chunk_before"), ALU.mult, t)
                m4 = tt(arb[:, hd, 2:4, :], two(B[bB][:, S:2 * S]), mask2("chunk_upto"), ALU.mult, t)
                hB[bB].give(m4)
                t = c.mms(prod(bC, 0, kt, rt), tr, tk, hB[bC])
                m5 = tt(rk[:, hd], two(B[bC][:, 0:S]), mask2("chunk_upto"), ALU.mult, t)
                hB[bC].give(m5)
                x0 = tt(X[:, hd], pm[:, hd, 0:2, :], mask2("identity"), ALU.add, m1)
                tri.append((m1, m2, m3, m4, m5, x0))
            F = [slice(64 * hd, 64 * hd + 64) for hd in range(2)]
            hdb = [(hd, b) for hd in range(2) for b in range(NB)]
            t = c.mms([(B[3][:, b * P + 64 * hd:][:, 0:64], arb[:, hd, b, :], tok[:, 3, b, F[hd]], i == 0, True)
                       for i, (hd, b) in enumerate(hdb)], [x[2] for x in tri], tt_done, hB[3])
            tz = copy(zt[:, :, :], two(B[3][:, 0:S]), [t, ended], "dve")
            hB[3].give(tz)
            mats = [dict(P=pm[:, hd, 0:2, :], M=pm[:, hd, 2:4, :], square=tri[hd], X=tri[hd]) for hd in range(2)]
            for step in range(3):
                for hd, m in enumerate(mats):
                    bA = 4 + 2 * hd
                    dst = sq2[:, hd] if step % 2 == 0 else pm[:, hd]
                    calls = [(B[bA][:, S + b * P:][:, 0:P], m["P"][:, b, :], m["M"][:, b, :], b == 0, True) for b in range(NB)]
                    if step < 2:
                        calls += [(B[bA][:, b * P:][:, 0:P], m["M"][:, b, :], m["P"][:, b, :], False, True) for b in range(NB)]
                    t = c.mms(calls, m["square"], hB[bA])
                    if step < 2:
                        cp = copy(dst, B[bA].rearrange("p (a t) -> p a t", a=4), t, "act")
                    else:
                        cp = copy(dst[:, 2:4, :], two(B[bA][:, S:2 * S]), t, "act")
                    hB[bA].give(cp)
                    m["P"], m["M"], m["square"] = dst[:, 0:2, :], dst[:, 2:4, :], cp
                for hd, m in enumerate(mats):
                    bB = 5 + 2 * hd
                    t = c.mms([(B[bB][:, b * P:][:, 0:P], m["M"][:, b, :], X[:, hd, b, :], b == 0, True)
                               for b in range(NB)], m["square"], m["X"], hB[bB])
                    m["X"] = tt(X[:, hd], X[:, hd], two(B[bB][:, 0:S]), ALU.add, t)
                    hB[bB].give(m["X"])
            done = [m["X"] for m in mats]
            t = c.mms([(B[3][:, b * P + 64 * hd:][:, 0:64], X[:, hd, b, :], zt[:, b, F[hd]], i == 0, True)
                       for i, (hd, b) in enumerate(hdb)], done, tz, hB[3])
            tu = copy(ut[:, :, :], two(B[3][:, 0:S]), t, "dve")
            hB[3].give(tu)
            t = c.mms([(B[2][:, b * P + 64 * hd:][:, 0:64], X[:, hd, b, :], tok[:, 0, b, F[hd]], i == 0, True)
                       for i, (hd, b) in enumerate(hdb)], done, tt_done, hB[2])
            tw_ = copy(wt[:, :, :], two(B[2][:, 0:S]), [t, ended], "act")
            hB[2].give(tw_)
            for hd in range(2):
                R, bk, bk2 = slice(64 * hd, 64 * hd + 64), 4 + hd, 6 + hd
                t = c.mms([(B[bk][:, b * P:][:, 0:P], wt[:, b, :], arb[:, hd, 2 + b, :], b == 0, True)
                           for b in range(NB)], tw_, tri[hd], hB[bk])
                t = c.dve(lambda e, R=R, bk=bk: e.tensor_tensor(
                    Rs[R].rearrange("p a b -> p (a b)")[:, bass.ts(local(), S)], B[bk][R, 0:S], rt[R, :], ALU.add), t)
                hB[bk].give(t)
                calls = []
                for b in range(NB):
                    calls += [(B[bk2][:, b * P:][:, 0:P], ut[:, b, :], arb[:, hd, 2 + b, :], b == 0, False),
                              (B[bk2][:, b * P:][:, 0:P], tok[:, 3, b, :], rk[:, hd, b, :], False, True)]
                t = c.mms(calls, tu, tri[hd], tt_done, hB[bk2])
                t = c.act(lambda e, R=R, bk2=bk2: e.activation(pair8["kk"][R, bass.ts(px(), S)], B[bk2][R, 0:S],
                                                               ACT.Copy), t, ta)
                hB[bk2].give(t)
            free.give(c.now())
            next_front = front(next_px) if next_px else iter(())
            next(next_front, None)
            h_b, h_u = [ended], [ended, ended]
            for i, (hd, b) in enumerate(hdb):
                R = slice(64 * hd, 64 * hd + 64)
                spread = lambda src: src.unsqueeze(1).to_broadcast([P, 8, 64])
                chunks = c.con("chunk_of")[:, 0:8].unsqueeze(2).to_broadcast([P, 8, 64])
                s1 = tt(bx[:, :, :], spread(tok[:, 1, b, F[hd]]), chunks, ALU.mult, tt_done, h_b)
                s2 = tt(ux[:, i % 2], spread(ut[:, b, F[hd]]), chunks, ALU.mult, tu, h_u[i % 2])
                s3 = tt(vx[:, i % 2], spread(tok[:, 3, b, F[hd]]), chunks, ALU.mult, tt_done, h_u[i % 2], who=c.pool)
                if i == 0:
                    next(next_front, None)
                bg, bq = i % 2, 2 + i % 2
                fl = lambda x: x.rearrange("p n j -> p (n j)")
                tg = c.mms([(B[bg], wt[:, b, :], fl(bx[:, :, :]), True, True)], tw_, s1, hB[bg])
                th = c.mms([(B[bq], tok[:, 1, b, :], fl(ux[:, i % 2]), True, False), (B[bq], tok[:, 2, b, :], fl(vx[:, i % 2]), False, True)],
                           s2, s3, hB[bq])
                h_b, h_u[i % 2] = tg, th
                n8 = slice(8 * b, 8 * b + 8)
                gdst = lambda x, R=R, n8=n8: x[R].rearrange("p q n j -> p q (n j)")[:, bass.ds(local(), 1), 512 * (n8.start // 8):][:, :, 0:512]
                tg = c.dve(lambda e, R=R, n8=n8, bg=bg, gdst=gdst: e.tensor_tensor(
                    gdst(G), B[bg][R, :].unsqueeze(1), diag[R, n8, :].rearrange("p n j -> p (n j)").unsqueeze(1), ALU.add), tg, tdg)
                hB[bg].give(tg)
                th = c.act(lambda e, R=R, n8=n8, bq=bq, gdst=gdst: e.activation(
                    gdst(H), B[bq][R, :].unsqueeze(1), ACT.Copy), th)
                hB[bq].give(th)
            last.give(c.now())

        finish(front(lambda: 0))
        for half in range(2):
            with c.repeat(3) as q:
                pair(lambda q=q, half=half: q.cur + half * 4, lambda q=q: q.cur,
                     lambda q=q, half=half: q.cur + (half * 4 + 1))
            pair(lambda half=half: half * 4 + 3, lambda: 3, (lambda: 4) if half == 0 else None)
            c.barrier()
            t = c.dve(lambda e: e.memset(st[:, 0, :, :], 0.0))
            yb = c.acc[:, 0:4, :]
            for n in range(NCH):
                cur, nxt = n % 2, (n + 1) % 2
                sb_, hs_ = B[nxt], hB[nxt]
                if n < NCH - 1:
                    tg = c.mms([(sb_[64 * hd:64 * hd + 64, p_ * 64:(p_ + 1) * 64], G[64 * hd:64 * hd + 64, p_, n, :],
                                 st[64 * hd:64 * hd + 64, cur, p_, :], p_ == 0, True)
                                for p_ in range(4) for hd in range(2)], t, hs_)
                ty = c.mms([(yb[64 * hd:64 * hd + 64, p_, n * CHUNK:(n + 1) * CHUNK], st[64 * hd:64 * hd + 64, cur, p_, :],
                             Rs[64 * hd:64 * hd + 64, p_, n * CHUNK:(n + 1) * CHUNK], True, True)
                            for p_ in range(4) for hd in range(2)], t)
                if n < NCH - 1:
                    t2 = tt(st[:, nxt], sb_[:, 0:S].rearrange("p (a j) -> p a j", a=4), H[:, :, n, :], ALU.add,
                            tg, last_y if n else None)
                    hs_.give(t2)
                    t = t2
                last_y = ty
            y4 = kk[:, 4 * half:4 * half + 4, :]
            tt(y4, y4, yb, ALU.add, ty)
            c.barrier()
        c.ctx = outer


ALPHA3 = 2 ** 0.25
Q_N, KV_C, KV_S, KV_W, Q_M, K_M, V_M, CONV_A, CONV_G = 0, 256, 384, 512, 652, 908, 1164, 1420, 1676
Q_H, F_H, I_H, G_H = 1932, 2188, 2444, 2700
N_CMP, CMP_STEP = 15, 16
BIAS_W = 512
HANKEL_W = 384
TAPS = 31


def bucket_constants():
    d = 255 - np.arange(BIAS_W)
    n = np.maximum(d, 0)
    large = 16 + (np.log(np.maximum(n, 1).astype(np.float32) / 16) / np.log(128 / 16) * 16).astype(np.int32)
    bucket = np.where(n < 16, n, np.minimum(large, 31))
    hot = (np.arange(32)[:, None] == bucket[None, :]) & (d[None, :] >= 0)
    return hot.astype(np.float32), np.where(d < 0, -1e30, 0.0)[None, :].astype(np.float32)


def block3(c):
    c.barrier()
    w3 = lambda start: (lambda *_: ("cols", "w_in_3", 0, start))
    with ExitStack() as own:
        outer, c.ctx = c.ctx, own
        mix = c.sb("mix_out", [P, KT, S])
        c.operands("b3", hidden=0)
        c.split(c.h, c.x, None)
        c.barrier()
        attention3(c, w3, mix)
        hgrn3(c, w3, mix)
        t = c.split(mix, c.x, None)
        for n in range(4):
            ap, tok = c.unit(lambda *_, n=n: ("cols", "w_out_3", 0, n * 256))
            for q in range(2):
                c.tile_T(ap, q, tok, c.x, t, c.acc[:, 2 * n + q, :], None, release=q == 1)
        c.barrier()
        x = residual_norm(c, ALPHA3, 1.0, lambda k: c.col(("ln1_g_3", 0), k), lambda k: c.col(("ln1_b_3", 0), k), None, c.x)
        c.hidden_buffers("b3", 3)

        def make(j, n):
            a, ta = c.unit(lambda *i: ("cols", "w_ff1_3", 0, j(*i) * 256))
            for q in range(2):
                b = (2 * n + q) % 4
                t = c.tile_T(a, q, ta, c.x, x, c.bank[b][:, 0:S], c.hb[b], release=q == 1)
                r = c.act(lambda e, q=q, b=b: e.activation(c.act_gate[:, q, :], c.bank[b][:, 0:S], ACT.Relu), t, c.h_gate[q])
                c.hb[b].give(r)
                m = c.dve(lambda e, q=q: e.tensor_tensor(c.act_gate[:, q, :], c.act_gate[:, q, :], c.act_gate[:, q, :],
                                                         ALU.mult), r)
                c.hidden_parts(c.act_gate, n, q, m)

        def use(j, n, first=False):
            d, td = c.unit(lambda *i: ("rows", "w_ff2_3", 0, j(*i) * 256), a=2)
            c.add_down(d, td, n, first)

        make(lambda: 0, 0)
        make(lambda: 1, 1)
        use(lambda: 0, 0, first=True)
        with c.repeat(4):
            for n in range(3):
                make(lambda i, n=n: 2 + 3 * i + n, (2 + n) % 3)
                use(lambda i, n=n: 1 + 3 * i + n, (1 + n) % 3)
        make(lambda: 14, 2)
        use(lambda: 13, 1)
        make(lambda: 15, 0)
        use(lambda: 14, 2)
        use(lambda: 15, 0)
        c.barrier()
        residual_norm(c, ALPHA3, 1.0, lambda k: c.col(("ln2_g_3", 0), k), lambda k: c.col(("ln2_b_3", 0), k), None)
        c.barrier()
        c.ctx = outer


def attention3(c, w3, mix):
    with ExitStack() as own:
        outer, c.ctx = c.ctx, own
        c.attention_buffers("b3")
        hot, mrow = c.sb("bias_one_hot", [32, BIAS_W]), c.sb("bias_mask", [1, BIAS_W])
        tabT, brow = c.sb("bias_table", [32, 8]), c.sb("bias_rows", [8, BIAS_W])
        hk = c.sb("bias_hankel", [P, 8, HANKEL_W])
        w2 = c.sb("cmp_w2", [P, 2, 2, 64])
        qn, qm, kmo = (c.sb(n, [64, 4, S]) for n in ("q_nsa", "q_moba", "k_moba"))
        kw_ = c.sb("k_sel_win", [64, 2, S])
        vw_ = c.sb("v_sel_win", [P, NB, 2, 64])
        vmo = c.sb("v_moba", [P, NB, 256])
        gates = c.sb("nsa_gates", [P, NB, 12])
        dup = c.sb("cmp_tokens", [P, 2, S])
        win = c.sb("cmp_windows", [P, 2, 16, 16])
        wx = Pair(*(c.sb(f"cmp_windows_{n}", [P, 2, 16, 16], F32R) for n in ("hi", "lo")))
        t_zero = c.pool(lambda e: e.memset(win[:, :, :, N_CMP:16], 0.0))
        rows = c.sb("cmp_rows", [16, 2, 256])
        hc = c.sb("cmp_hidden", [P, 2, 2, N_CMP])
        kc, vc = c.sb("cmp_k", [64, N_CMP]), c.sb("cmp_v", [N_CMP, 64])
        pc, pct = c.sb("cmp_w", [P, 2, NB, 16]), c.sb("cmp_w_by_key", [N_CMP, 2, S])
        cst = c.sb("cmp_stats", [P, 3, 2, NB])
        ident, flip = c.con("identity"), c.con("flip")

        tl = [c.load(x[:, :], c.aps[n], engine="scalar", name=n) for x, n in
              ((hot, "bias_one_hot"), (mrow, "bias_mask"), (tabT, "bias_table"))]
        tw2 = c.load(w2[:, :, :, :], c.aps["cmp_w2"], engine="scalar", name="cmp_w2")
        t = c.mms([(c.bank[0][0:8, :], tabT[:, :], hot[:, :], True, False),
                   (c.bank[0][0:8, :], c.con("ones")[0:1, 0:8], mrow[:, :], False, True)], tl, c.hb[0])
        t = c.dve(lambda e: e.tensor_copy(brow[:, :], c.bank[0][0:8, :]), t)
        c.hb[0].give(t)
        scratch = c.nc.dram_tensor("bias_scratch", (8, BIAS_W), F32, kind="Internal").ap()
        t = c.load(scratch, brow[:, :], t, engine="scalar", name="bias_store")
        hankel = bass.AP(tensor=scratch.tensor, offset=0, ap=[[1, P], [BIAS_W, 8], [1, HANKEL_W]])
        thk = c.load(hk[:, :, :], hankel, t, engine="scalar", name="hankel")

        sc = HD ** -0.5
        take_heads = lambda dst, s: (lambda t, ps, r, f: c.evac_heads(ps, dst, t, s, r, f))
        r_q = c.project(lambda _, n: w3(Q_N)(), 1, None, take_heads(qn, sc))
        ap, tok = c.unit(w3(KV_C))
        t = c.tile_T(ap, 0, tok, c.x, None, c.bank[2][:, 0:S], c.hb[2])
        td = []
        for e_ in range(2):
            for half in range(2):
                td.append(c.act(lambda e, e_=e_, half=half: e.activation(
                    dup[64 * half:64 * half + 64, e_, :], c.bank[2][64 * e_:64 * e_ + 64, 0:S], ACT.Copy), t))
        c.hb[2].give(td)
        t = c.mms([(c.bank[3][0:64, 0:S], ap[:, k, 128:192], c.x[:, k, :], k == 0, k == KT - 1) for k in range(KT)],
                  tok, c.hb[3])
        rk = [c.dve(lambda e: e.tensor_copy(kw_[:, 0, :], c.bank[3][0:64, 0:S]), t)]
        c.hb[3].give(rk)
        rv = []

        def tokens(ap, tok, at, width, b, bank, dst, func=ACT.Copy, release=False):
            t = c.mms([(c.bank[bank][:, 0:width], c.x[:, k, b * P:(b + 1) * P], ap[:, k, at:at + width], k == 0,
                        k == KT - 1) for k in range(KT)], tok, c.hb[bank], release=release)
            t = c.act(lambda e: e.activation(dst, c.bank[bank][:, 0:width], func), t)
            c.hb[bank].give(t)
            return t
        for b in range(NB):
            rv.append(tokens(ap, tok, 192, 64, b, b, vw_[:, b, 0, :], release=b == 1))
        ap, tok = c.unit(w3(KV_W))
        t = c.mms([(c.bank[2][0:64, 0:S], ap[:, k, 0:64], c.x[:, k, :], k == 0, k == KT - 1) for k in range(KT)],
                  tok, c.hb[2])
        rk.append(c.dve(lambda e: e.tensor_copy(kw_[:, 1, :], c.bank[2][0:64, 0:S]), t))
        c.hb[2].give(rk[-1])
        for b in range(NB):
            rv.append(tokens(ap, tok, 64, 64, b, b, vw_[:, b, 1, :]))
        for b in range(NB):
            rv.append(tokens(ap, tok, 128, 12, b, 2 + b, gates[:, b, :], func=ACT.Sigmoid, release=b == 1))
        r_m = [c.project(lambda _, n: w3(Q_M)(), 1, None, take_heads(qm, sc)),
               c.project(lambda _, n: w3(K_M)(), 1, None, take_heads(kmo, 1.0)),
               c.project_tok(lambda _, n: w3(V_M)(), 1, None, vmo)]
        taps, conv_out = conv3(c, w3, mix)

        b7 = c.bank7.rearrange("p a b -> p (a b)")
        small = {}

        def compress(e_):
            tw = []
            for half in range(2):
                R = slice(64 * half, 64 * half + 64)
                v = dup[R, e_, :].rearrange("p (n l m) -> p l m n", n=16, l=8, m=2)
                for hi in range(2):
                    pe_ = c.col(("nsa_cmp_pe_3", (0, e_)), 8 * hi, 8)[R].unsqueeze(2).to_broadcast([64, 8, N_CMP])
                    tw.append(c.dve(lambda e, v=v, hi=hi, half=half, R=R, pe_=pe_: e.tensor_tensor(
                        win[R, e_, 8 * hi:8 * hi + 8, 0:N_CMP], v[:, :, half, hi:hi + N_CMP], pe_, ALU.add), td))
            tw = c.split(win[:, e_], wx[:, e_], [tw, t_zero], n=16, step=8)
            for n in range(2):
                ap, tok = c.unit(lambda *_, n=n: ("cols", "nsa_cmp_w1_3", (0, e_, slice(n * D, n * D + D)), 0))
                t = c.mms([(b7[0:16, 0:256], wx[:, e_, 8 * n + k, :], ap[:, k, :], n + k == 0, n == 1 and k == KT - 1)
                           for k in range(KT)], tok, tw, c.h_bank7 if n == 0 else None, release=True)
                if n == 0:
                    yield
            t = c.dve(lambda e: e.tensor_copy(rows[:, e_, :], b7[0:16, 0:256]), t)
            t = c.mms([(b7[:, 16 * m:16 * m + 16], rows[:, e_, m * P:(m + 1) * P], ident[0:16, 0:16], m == 0, True)
                       for m in range(2)], t)
            tg = [c.act(lambda e, m=m: e.activation(hc[:, e_, m, :], b7[:, 16 * m:16 * m + N_CMP],
                        ACT.Gelu_apprx_tanh, bias=c.col(("nsa_cmp_b1_3", (0, e_)), m)), t) for m in range(2)]
            if e_ == 0:
                t = c.mms([(b7[0:64, 0:N_CMP], w2[:, 0, m, :], hc[:, 0, m, :], m == 0, m == 1) for m in range(2)],
                          tg, tw2)
                t = small["k"] = c.dve(lambda e: e.tensor_copy(kc[:, :], b7[0:64, 0:N_CMP]), t)
            else:
                t = c.mms([(b7[0:N_CMP, 0:64], hc[:, 1, m, :], w2[:, 1, m, :], m == 0, m == 1) for m in range(2)],
                          tg, tw2)
                t = small["v"] = c.dve(lambda e: e.tensor_copy(vc[:, :], b7[0:N_CMP, 0:64]), t)
            c.h_bank7.give(t)

        def bias(z, head, qb):
            w = hk[:, head, P:2 * P] if qb == 0 else hk[:, head, 0:2 * P]
            return (z, flip, w, False, True)

        def take(pair):
            def f(ob, t):
                a = c.act(lambda e: e.activation(mix[0:64, pair, :], ob[0:64, 0, :], ACT.Copy), t)
                return c.act(lambda e: e.activation(mix[64:128, pair, :], ob[0:64, 1, :], ACT.Copy), a)
            return f

        def compressed(pair, ready):
            z = b7[:, 0:64].rearrange("p (h b n) -> p h b n", h=2, b=NB)
            calls = []
            for hd in range(2):
                for qb in range(NB):
                    h = 2 * pair + hd
                    off = 159 if qb == 0 else 31
                    calls += [(z[:, hd, qb, 0:N_CMP], qn[:, h, qb * P:(qb + 1) * P], kc[:, :], hd + qb == 0, False),
                              (z[:, hd, qb, 0:N_CMP], flip, hk[:, h, off:off + CMP_STEP * (N_CMP - 1) + 1:CMP_STEP], False, True)]
            t = c.mms(calls, ready, c.h_bank7)
            t = c.dve(lambda e: e.tensor_reduce(cst[:, 0, :, :], z[:, :, :, 0:N_CMP], AX, ALU.max, negate=True), t)
            t = c.dve(lambda e: e.tensor_scalar(cst[:, 0, :, :], cst[:, 0, :, :], 1e20, None, ALU.min), t)
            ex = [c.act(lambda e, hd=hd, qb=qb: e.activation(
                pc[:, hd, qb, 0:N_CMP], z[:, hd, qb, 0:N_CMP], ACT.Exp, bias=cst[:, 0, hd, qb:qb + 1],
                accum_out=cst[:, 1, hd, qb:qb + 1]), t) for hd in range(2) for qb in range(NB)]
            c.h_bank7.give(ex)
            t = c.dve(lambda e: e.tensor_scalar(cst[:, 1, :, :], cst[:, 1, :, :], 1e-30, None, ALU.max), ex)
            t = c.dve(lambda e: e.reciprocal(cst[:, 2, :, :], cst[:, 1, :, :]), t)
            tn = []
            for hd in range(2):
                for qb in range(NB):
                    g = gates[:, qb, 3 * (2 * pair + hd):][:, 0:1]
                    tn.append(c.dve(lambda e, hd=hd, qb=qb, g=g: e.tensor_scalar(
                        pc[:, hd, qb, 0:N_CMP], pc[:, hd, qb, 0:N_CMP], cst[:, 2, hd, qb:qb + 1], g, ALU.mult, ALU.mult), t, rv))
            yield
            pt = c.acc[:, 0:2, :].rearrange("p a b -> p (a b)")

            def turn(e):
                for hd in range(2):
                    for qb in range(NB):
                        i = e.transpose(pt[0:N_CMP, (2 * hd + qb) * P:][:, 0:P], pc[:, hd, qb, 0:N_CMP], ident)
                return i
            t = c.pe(turn, tn, c.h_pt2[0])
            t = c.act(lambda e: e.activation(pct[:, :, :], pt[0:N_CMP, :].rearrange("p (h q) -> p h q", h=2), ACT.Copy),
                      t, h_pct)
            c.h_pt2[0].give(t)
            return t

        def moba(pair):
            def scores(hd, qb, z):
                h = 2 * pair + hd
                return [(z, qm[:, h, qb * P:(qb + 1) * P], kmo[:, h, 0:(qb + 1) * P], True, False), bias(z, 4 + h, qb)]
            side, tw = yield from c.softmax_pair(scores, True, ready=[r_m, thk])
            yield
            c.values_pair(side, [tw, r_m], lambda hd, kb: vmo[:, kb, (2 * pair + hd) * 64:][:, 0:64], True, 64,
                          take(2 + pair))

        def nsa(pair, kind):
            ready = [r_q, rk, rv, thk]

            def scores(hd, qb, z):
                h = 2 * pair + hd
                return [(z, qn[:, h, qb * P:(qb + 1) * P], kw_[:, kind, 0:(qb + 1) * P], True, False), bias(z, h, qb)]
            gate = lambda hd, qb: gates[:, qb, 3 * (2 * pair + hd) + 1 + kind:][:, 0:1]
            own = c.softmax_pair(scores, True, norm=gate, ready=ready)
            cmp_ = compressed(pair, [ready, small["k"]]) if kind == 0 else None
            next(own)
            if cmp_:
                next(cmp_)
            yield
            side, tw = finish(own)
            tc_ = finish(cmp_) if cmp_ else None
            yield
            ob = c.acc[:, 4:6, :]
            for hd in range(2):
                calls = [(ob[0:64, hd, :], vc[:, :], pct[:, hd, :], hd == 0, False)] if cmp_ else []
                for kb in range(NB):
                    q0 = 128 * kb
                    calls.append((ob[0:64, hd, q0:256], vw_[:, kb, kind, :],
                                  c.wk[:, side, hd, kb * 256:kb * 256 + 256 - q0], False, kind + kb == 2))
                t = c.mms(calls, tw, tc_, small["v"], c.h_o[0] if cmp_ and hd == 0 else None)
            c.h_wk[side].give(t)
            if cmp_:
                h_pct.give(t)
            else:
                c.h_o[0].give(take(pair)(ob, t))

        h_pct = Hand(c)
        stagger([moba(p) for p in range(2)], [compress(e_) for e_ in range(2)])
        stagger([nsa(p, kind) for p in range(2) for kind in range(2)], [advance(taps) for _ in range(4)])
        conv_out()
        c.barrier()
        c.ctx = outer


def conv3(c, w3, mix):
    hp = c.sb("conv_in", [P, 2, S + TAPS - 1])
    sg, cv = (c.sb(f"conv_{n}", [P, 2, S]) for n in ("gate", "out"))
    pw = c.sb("conv_pw", [P, 2, 256])
    tp = c.load(pw[:, :, :], c.aps["conv_pw"], engine="scalar", name="conv_pw")
    tz = c.pool(lambda e: e.memset(hp[:, :, 0:TAPS - 1], 0.0))

    def copy_in(t, ps, r, f):
        x = c.dve(lambda e: e.tensor_copy(hp[:, t, TAPS - 1:], ps[:, 0:S]), r)
        f.give(x)
        return x

    def gate(t, ps, r, f):
        x = c.act(lambda e: e.activation(sg[:, t, :], ps[:, 0:S], ACT.Sigmoid), r)
        f.give(x)
        return x
    a = c.project(lambda _, n: w3(CONV_A)(), 1, None, copy_in)
    g = c.project(lambda _, n: w3(CONV_G)(), 1, None, gate)
    t = c.dve(lambda e: e.tensor_tensor(hp[:, :, TAPS - 1:], hp[:, :, TAPS - 1:], sg[:, :, :], ALU.mult), a, g)
    t = [c.dve(lambda e, q=q: e.tensor_scalar(cv[:, q, :], hp[:, q, 0:S], c.col(("conv_dw_w_3", (0, 0)), q),
                                              c.col(("conv_dw_b_3", 0), q), ALU.mult, ALU.add), t, tz) for q in range(2)]
    done = {}

    def dve_taps():
        u = t[0]
        for j in range(1, TAPS):
            u = c.dve(lambda e, j=j: e.scalar_tensor_tensor(
                out=cv[:, 0, :], in0=hp[:, 0, j:j + S], scalar=c.col(("conv_dw_w_3", (0, j)), 0), in1=cv[:, 0, :],
                op0=ALU.mult, op1=ALU.add), u)
            if j % 4 == 0:
                yield
        done[0] = u
    u = t[1]
    for j in range(1, TAPS):
        u = c.pool(lambda e, j=j: e.tensor_scalar(sg[:, 1, :], hp[:, 1, j:j + S], c.col(("conv_dw_w_3", (0, j)), 1),
                                                  None, ALU.mult), u)
        u = c.pool(lambda e: e.tensor_tensor(cv[:, 1, :], cv[:, 1, :], sg[:, 1, :], ALU.add), u)
    done[1] = u

    def rest():
        out = c.layer_norm(cv, 2, lambda k: c.col(("conv_ln_g_3", 0), k), lambda k: c.col(("conv_ln_b_3", 0), k), cv,
                           [done[0], done[1]], sg, mat="mean_256")
        t1 = c.act(lambda e: e.activation(cv[:, :, :], cv[:, :, :], ACT.Silu), out)
        for q in range(2):
            t2 = c.mms([(c.bank[q][:, 0:S], pw[:, k, q * P:(q + 1) * P], cv[:, k, :], k == 0, k == 1) for k in range(2)],
                       t1, tp, c.hb[q])
            t2 = c.dve(lambda e, q=q: e.tensor_copy(mix[:, 4 + q, :], c.bank[q][:, 0:S]), t2)
            c.hb[q].give(t2)
    return dve_taps(), rest


def hgrn3(c, w3, mix):
    with ExitStack() as own:
        outer, c.ctx = c.ctx, own
        PAD = CHUNK
        t3 = lambda n: c.sb(f"hgrn_{n}", [P, 2, S])
        qT, kT_, eU, eA, F, pr, qp, gT, o, kh = (t3(n) for n in ("q", "k", "e_from_start", "e_to_end", "decay", "pairs",
                                                                "pairs_q", "gate", "o", "k_to_end"))
        kp, fp, vp = (c.sb(f"hgrn_{n}_padded", [P, 2, PAD + S]) for n in ("k", "f", "v"))
        lf, lf2 = c.sb("hgrn_log_f", [P, NB, 256]), c.sb("hgrn_log_f_t", [P, NB, 256])
        vt, kt = c.sb("hgrn_v_tok", [P, NB, 256]), c.sb("hgrn_k_tok", [P, NB, 256])
        vx = c.sb("hgrn_v_by_chunk", [P, 2, 8, 64])
        Hc, St = c.sb("hgrn_H", [P, 2, NCH, 64]), c.sb("hgrn_S", [P, 2, NCH, 64])
        pv_ = c.sb("hgrn_part", [P, 2, S])
        tz = [c.pool(lambda e, x=x: e.memset(x[:, :, 0:PAD], 0.0)) for x in (kp, fp, vp)]

        def to(dst, func=ACT.Copy):
            def take(t, ps, r, f):
                x = c.act(lambda e: e.activation(dst[:, t, :], ps[:, 0:S], func), r)
                f.give(x)
                return x
            return take
        rq = c.project(lambda _, n: w3(Q_H)(), 1, None, to(qT))

        def both(start, take, tok_dst):
            ap, tok = c.unit(w3(start))
            out = []
            for q in range(2):
                t = c.tile_T(ap, q, tok, c.x, None, c.bank[q][:, 0:S], c.hb[q])
                out.append(take(q, c.bank[q], t, c.hb[q]))
            for b in range(NB):
                t = c.tile_tok(ap, b, tok, c.x, None, c.bank[2 + b][:, 0:S], c.hb[2 + b], release=b == 1)
                t = c.dve(lambda e, b=b: e.tensor_copy(tok_dst[:, b, :], c.bank[2 + b][:, 0:S]), t)
                c.hb[2 + b].give(t)
                out.append(t)
            return out
        rf = both(F_H, to(fp[:, :, PAD:], ACT.Sigmoid), lf)
        ri = both(I_H, to(vp[:, :, PAD:]), vt)
        rg = c.project(lambda _, n: w3(G_H)(), 1, None, to(gT, ACT.Sigmoid))
        tk = c.dve(lambda e: e.tensor_scalar(kp[:, :, PAD:], fp[:, :, PAD:], -1.0, 1.0, ALU.mult, ALU.add), rf)
        tf = c.dve(lambda e: e.memset(fp[:, :, :].rearrange("p a (n t) -> p a n t", t=CHUNK)[:, :, :, 0:1], 0.0), tk, tz)
        a = c.act(lambda e: e.activation(lf2[:, :, :], lf[:, :, :], ACT.Abs), rf)
        a = c.act(lambda e: e.activation(lf2[:, :, :], lf2[:, :, :], ACT.Exp, scale=-1.0), a)
        a = c.act(lambda e: e.activation(lf2[:, :, :], lf2[:, :, :], ACT.Ln, bias=c.eps(1.0)), a)
        tl = c.dve(lambda e: e.scalar_tensor_tensor(out=lf[:, :, :].rearrange("p a b -> p (a b)"),
                                                    in0=lf[:, :, :].rearrange("p a b -> p (a b)"), scalar=0.0,
                                                    in1=lf2[:, :, :].rearrange("p a b -> p (a b)"),
                                                    op0=ALU.min, op1=ALU.subtract), a)
        ex = []
        for i, (m, dst) in enumerate((("chunk_upto", eU), ("chunk_after", eA))):
            t = c.mms([(c.bank[i][:, q * S + b * P:][:, 0:P], lf[:, b, q * P:(q + 1) * P], c.con(m), q + b == 0, True)
                       for q in range(2) for b in range(NB)], tl, c.hb[i])
            t = c.act(lambda e, i=i, dst=dst: e.activation(dst[:, :, :].rearrange("p a b -> p (a b)"), c.bank[i][:, :],
                                                           ACT.Exp), t)
            c.hb[i].give(t)
            ex.append(t)
        tkh = c.dve(lambda e: e.tensor_tensor(kh[:, :, :], kp[:, :, PAD:], eA[:, :, :], ALU.mult), ex, tk)
        tqs = c.dve(lambda e: e.tensor_tensor(eA[:, :, :], qT[:, :, :], eU[:, :, :], ALU.mult), tkh, rq, ex)

        def turn(e):
            for q in range(2):
                for b in range(NB):
                    i = e.transpose(c.bank[2][:, b * S + q * P:][:, 0:P], kh[:, q, b * P:(b + 1) * P], c.con("identity"))
            return i
        t = c.pe(turn, tkh, c.hb[2])
        tkt = c.act(lambda e: e.activation(kt[:, :, :].rearrange("p a b -> p (a b)"), c.bank[2][:, :], ACT.Copy), t)
        c.hb[2].give(tkt)
        th = []
        h_vx = [Hand(c) for _ in range(2)]
        for hd in range(4):
            for b in range(NB):
                i, R, q = b, slice(64 * (hd % 2), 64 * (hd % 2) + 64), hd // 2
                s = c.pool(lambda e, hd=hd, b=b, i=i: e.tensor_tensor(
                    vx[:, i, :, :], vt[:, b, hd * 64:(hd + 1) * 64].unsqueeze(1).to_broadcast([P, 8, 64]),
                    c.con("chunk_of")[:, 0:8].unsqueeze(2).to_broadcast([P, 8, 64]), ALU.mult), ri, h_vx[i])
                n = 2 + i
                t = c.mms([(c.bank[n][:, :], kt[:, b, q * P:(q + 1) * P], vx[:, i, :, :].rearrange("p n j -> p (n j)"),
                            True, True)], s, tkt, c.hb[n])
                h_vx[i].give(t)
                t = c.act(lambda e, R=R, q=q, b=b, n=n: e.activation(
                    Hc[R, q, 8 * b:8 * b + 8, :].rearrange("p n j -> p (n j)"), c.bank[n][R, :], ACT.Copy), t)
                c.hb[n].give(t)
                th.append(t)
        t = c.dve(lambda e: e.memset(St[:, :, 0, :], 0.0))
        ts = [t, t]
        for n in range(NCH - 1):
            ts = [c.dve(lambda e, q=q, n=n: e.scalar_tensor_tensor(
                out=St[:, q, n + 1, :], in0=St[:, q, n, :], scalar=eU[:, q, (n + 1) * CHUNK - 1:(n + 1) * CHUNK],
                in1=Hc[:, q, n, :], op0=ALU.mult, op1=ALU.add), ts[q], th, ex) for q in range(2)]
        ob = c.acc[:, 0:2, :]
        ty = c.mms([(ob[64 * hd:64 * hd + 64, q, n * CHUNK:(n + 1) * CHUNK], St[64 * hd:64 * hd + 64, q, n, :],
                     eA[64 * hd:64 * hd + 64, q, n * CHUNK:(n + 1) * CHUNK], True, True)
                    for q in range(2) for n in range(NCH) for hd in range(2)], ts, tqs)
        ab = [c.acc[:, 2:4, :], c.acc[:, 4:6, :]]
        qps = [qp, c.sb("hgrn_pairs_q_2", [P, 2, S])]
        h_ab, h_qp, h_pv = [Hand(c) for _ in range(2)], [Hand(c) for _ in range(2)], Hand(c)

        h_o, h_F, h_pr = Hand(c), Hand(c), Hand(c)

        def head_sums(j, ready):
            t = c.mms([(ab[j][:, q, :], c.con("head_sum"), qps[j][:, q, :], q == 0, True) for q in range(2)], ready,
                      h_ab[j])
            h_qp[j].give(t), h_ab[j].give(t)

        def weights(at, j):
            t = c.dve(lambda e: e.tensor_tensor(F[:, :, :], F[:, :, :], fp[:, :, bass.ds(at() + 1, S)], ALU.mult), h_F)
            h_F.give(t)
            t = c.dve(lambda e: e.tensor_tensor(pr[:, :, :], F[:, :, :], kp[:, :, bass.ds(at(), S)], ALU.mult), t, h_pr)
            t = c.pool(lambda e: e.tensor_tensor(qps[j][:, :, :], pr[:, :, :], qT[:, :, :], ALU.mult), t, h_qp[j])
            h_pr.give(t)
            head_sums(j, t)

        def values(at, j):
            t = c.dve(lambda e: e.tensor_tensor(pv_[:, :, :], ab[j], vp[:, :, bass.ds(at(), S)], ALU.mult), h_ab[j], h_pv)
            h_ab[j].give(t)
            t = (c.pool if j else c.dve)(lambda e: e.tensor_tensor(o[:, :, :], o[:, :, :], pv_[:, :, :], ALU.add), t, h_o)
            h_pv.give(t), h_o.give(t)

        t = c.pool(lambda e: e.tensor_tensor(qps[0][:, :, :], kp[:, :, PAD:], qT[:, :, :], ALU.mult), tk, rq)
        head_sums(0, t)
        t = c.dve(lambda e: e.tensor_tensor(o[:, :, :], ab[0], vp[:, :, PAD:], ALU.mult), h_ab[0], ri)
        h_ab[0].give(t), h_o.give(t)
        h_F.give(c.dve(lambda e: e.memset(F[:, :, :], 1.0), tf))
        weights(lambda: PAD - 1, 0)
        with c.repeat((CHUNK - 2) // 2) as i:
            weights(lambda: i.cur * -2 + (PAD - 2), 1)
            values(lambda: i.cur * -2 + (PAD - 1), 0)
            weights(lambda: i.cur * -2 + (PAD - 3), 0)
            values(lambda: i.cur * -2 + (PAD - 2), 1)
        values(lambda: PAD - CHUNK + 1, 0)
        c.barrier()
        t = c.dve(lambda e: e.tensor_tensor(o[:, :, :], o[:, :, :], ob, ALU.add), ty)
        t = c.act(lambda e: e.activation(pr[:, :, :], o[:, :, :], ACT.Square), t)
        t = c.mms([(ab[0][:, q, :], c.con("head_mean"), pr[:, q, :], q == 0, True) for q in range(2)], t)
        t = c.act(lambda e: e.activation(pr[:, :, :], ab[0], ACT.Sqrt, bias=c.eps(1e-6)), t)
        t = c.dve(lambda e: e.reciprocal(pr[:, :, :], pr[:, :, :]), t)
        t = c.dve(lambda e: e.tensor_tensor(pr[:, :, :], pr[:, :, :], gT[:, :, :], ALU.mult), t)
        for q in range(2):
            c.dve(lambda e, q=q: e.scalar_tensor_tensor(out=mix[:, 6 + q, :], in0=o[:, q, :],
                                                        scalar=c.col(("hgrn_norm_g_3", 0), q), in1=pr[:, q, :],
                                                        op0=ALU.mult, op1=ALU.mult), t)
        c.barrier()
        c.ctx = outer


def lay_unit(inputs, what):
    out = np.zeros((P, UNIT), np.float32)
    if what is None:
        return out
    kind, name, index, start = what
    if kind in ("side", "stack"):
        for n, x in enumerate(name):
            x = inputs[x][index]
            if kind == "stack":
                out.reshape(P, 2, D)[:x.shape[0], n] = x
            else:
                w = x.shape[1]
                out.reshape(P, KT, 256)[:, :, n * w:(n + 1) * w] = x.reshape(KT, P, w).transpose(1, 0, 2)
        return out
    w = inputs[name][index]
    if kind == "rows":
        part = w[start:start + 256]
        part = np.concatenate([part, np.zeros((256 - len(part), part.shape[1]), np.float32)])
    else:
        part = w[:, start:start + UNIT * P // w.shape[0]]
    k = part.shape[0] // P
    out.reshape(P, k, UNIT // k)[:, :, :part.shape[1]] = part.reshape(k, P, -1).transpose(1, 0, 2)
    return out


def feature_major(a):
    return np.ascontiguousarray(a.reshape(a.shape[0], -1, P).transpose(2, 1, 0))


def small_inputs(inputs):
    columns = np.concatenate([np.asarray(inputs[n][i]).reshape(-1, P) for n, i in VECTORS]).T
    wf = inputs["w_in"][:, :, F_FX:F_FX + HEADS].reshape(L1, KT, P, HEADS).transpose(2, 0, 1, 3)
    hot, mask = bucket_constants()
    w2 = inputs["nsa_cmp_w2_3"][0].reshape(2, 2, P, 64).transpose(2, 0, 1, 3)
    return {
        "bias_one_hot": hot,
        "bias_mask": mask,
        "bias_table": np.ascontiguousarray(inputs["rel_bias_3"].T),
        "cmp_w2": np.ascontiguousarray(w2),
        "conv_pw": np.ascontiguousarray(inputs["conv_pw_w_3"][0].reshape(2, P, 256).transpose(1, 0, 2)),
        "columns": np.ascontiguousarray(columns),
        "shape_constants": np.concatenate([np.asarray(MATS[n], np.float32) for n in CONS], axis=1),
        "w_forget": np.ascontiguousarray(wf.reshape(P, -1)),
        "b_forget_rows": np.ascontiguousarray(np.broadcast_to(inputs["b_forget"].reshape(1, -1), (P, L1 * HEADS))),
        "sgu_w_spatial": np.ascontiguousarray(inputs["sgu_w_sp_2"][0].transpose(2, 0, 1)),
        "sgu_b_spatial": inputs["sgu_b_sp_2"][0],
        "rwkv_w0_row": inputs["rwkv_w0_2"],
        "memory": feature_major(inputs["mem"][0]),
        "x": feature_major(inputs["x"][0]),
    }


def build(nc, small, blocks):
    aps = {n: nc.dram_tensor(f"in_{n}", a.shape, F32, kind="ExternalInput").ap() for n, a in small.items()}
    out = nc.dram_tensor("out", (P, KT, S), F32, kind="ExternalOutput").ap()
    with ExitStack() as ctx:
        c = Core(nc, ctx, aps)
        c.t_x = c.load(c.h[:, :, :], aps["x"], name="x")
        c.at["sync"].append(("wait", [c.t_x]))
        c.at["sync"].append(("raw", lambda e: c.stream()(e)))
        for b in blocks:
            b(c)
        c.pad_units(end=True)
        aps["weights"] = nc.dram_tensor("in_weights", (c.n_units, P, UNIT), F32, kind="ExternalInput").ap()
        t = c.load(out, c.h[:, :, :], c.now(), name="out")
        c.at["sync"].append(("wait", [t]))
        c.emit()
    return [w() for w in c.plan]


BLOCKS = [block1, block2, block3]


def kernel(**inputs):
    import concourse.bacc as bacc
    from concourse.bass_utils import run_bass_kernel_spmd

    nc = bacc.Bacc("TRN2", target_bir_lowering=False, num_devices=1)
    inputs = {k: np.asarray(v) for k, v in inputs.items()}
    small = small_inputs(inputs)
    plan = build(nc, small, BLOCKS)
    weights = np.stack([lay_unit(inputs, w) for w in plan])
    got = run_bass_kernel_spmd(nc, [{f"in_{n}": a for n, a in {**small, "weights": weights}.items()}], core_ids=[0]).results[0]["out"]
    return np.ascontiguousarray(got.transpose(2, 1, 0)).reshape(1, S, D)
```
